# Optimizing a Trainium2 kernel written in Bass

```python
import jax, jax.numpy as jnp
from jax import lax
import numpy as np

D_MODEL = 2048
BATCH = 1
SEQ = 256
DEPTH = 1
DEC_BATCH = 8
DEC_SEQ = 4
PAST_LEN = 1024
PAGE_SIZE = 128

D_A = D_MODEL // 2
HEAD_A = 64
N_HEADS_A = D_A // HEAD_A
LORA_W = 64
LORA_A = 64
LORA_G = 160
Z_A = 3 * D_A + LORA_W + LORA_A + LORA_G
LNX_EPS = 64e-5
D_B = D_MODEL // 2
HEAD_B = 128
N_HEADS_B = D_B // HEAD_B
MOBA_BLOCK = 256
MOBA_TOPK = 3
MOBA_Q_CHUNK = 16
ROPE_THETA = 10000.0
Z_IN = Z_A + 3 * D_B + 2 * D_MODEL
D_FF = 5632
CONV_W = 3
RMS_EPS = 1e-6
NEG_INF = -1e30

kernel_name = 'hybrid_rwkv7_moba_convffn_step'

def _rmsnorm(x, g):
    x32 = x.astype(jnp.float32)
    y = x32 * lax.rsqrt(jnp.mean(x32 * x32, axis=-1, keepdims=True) + RMS_EPS)
    return (y * g.astype(jnp.float32)).astype(x.dtype)

def _rope(x, pos):
    half = x.shape[-1] // 2
    inv = ROPE_THETA ** (-jnp.arange(half, dtype=jnp.float32) / half)
    ang = pos.astype(jnp.float32)[:, None] * inv[None, :]
    cos, sin = jnp.cos(ang)[:, None, :], jnp.sin(ang)[:, None, :]
    x32 = x.astype(jnp.float32)
    x1, x2 = x32[..., :half], x32[..., half:]
    return jnp.concatenate([x1 * cos - x2 * sin, x2 * cos + x1 * sin], axis=-1).astype(x.dtype)

def _wkv_scan(s0, r, w, k, v, kk, a):
    xs = tuple(jnp.moveaxis(t.astype(jnp.float32), 1, 0) for t in (r, w, k, v, kk, a))

    def step(s, inp):
        r_t, w_t, k_t, v_t, kk_t, a_t = inp
        s_kk = jnp.einsum('bhvk,bhk->bhv', s, kk_t)
        s = (s * w_t[:, :, None, :] - s_kk[..., None] * (kk_t * a_t)[:, :, None, :]
             + v_t[..., None] * k_t[:, :, None, :])
        return s, jnp.einsum('bhvk,bhk->bhv', s, r_t)

    s, ys = lax.scan(step, s0.astype(jnp.float32), xs)
    return s, jnp.moveaxis(ys, 0, 1)

def _moba_chunk(q, q_pos, k_blk, v_blk, k_mean):
    bsz, n_q, n_h, d = q.shape
    n_blk = k_blk.shape[1]
    own = q_pos // MOBA_BLOCK
    gate = jnp.einsum('bqhd,bnhd->bhqn', q.astype(jnp.float32), k_mean)
    fully_past = jnp.arange(n_blk)[None, :] < own[:, None]
    gate = jnp.where(fully_past[None, None], gate, NEG_INF)
    _, sel = lax.top_k(gate, min(MOBA_TOPK, n_blk))
    sel_ok = sel < own[None, None, :, None]
    own_idx = jnp.broadcast_to(own[None, None, :, None], (bsz, n_h, n_q, 1)).astype(sel.dtype)
    idx = jnp.concatenate([sel, own_idx], axis=-1)
    ok = jnp.concatenate([sel_ok, jnp.ones_like(own_idx, dtype=bool)], axis=-1)
    b_i = jnp.arange(bsz)[:, None, None, None]
    h_i = jnp.arange(n_h)[None, :, None, None]
    k_g = k_blk[b_i, idx, :, h_i]
    v_g = v_blk[b_i, idx, :, h_i]
    key_pos = idx[..., None] * MOBA_BLOCK + jnp.arange(MOBA_BLOCK)
    allowed = ok[..., None] & (key_pos <= q_pos[None, None, :, None, None])
    s = jnp.einsum('bqhd,bhqnjd->bhqnj', q, k_g).astype(jnp.float32) * (d ** -0.5)
    s = jnp.where(allowed, s, NEG_INF)
    p = jax.nn.softmax(s.reshape(bsz, n_h, n_q, -1), axis=-1).reshape(s.shape)
    return jnp.einsum('bhqnj,bhqnjd->bqhd', p.astype(v_g.dtype), v_g)

def _moba(q, q_pos, k_blk, v_blk):
    bsz, t_len, n_h, d = q.shape
    k_mean = jnp.mean(k_blk.astype(jnp.float32), axis=2)
    qc = MOBA_Q_CHUNK if t_len % MOBA_Q_CHUNK == 0 else t_len
    n_chunks = t_len // qc
    q_chunks = q.reshape(bsz, n_chunks, qc, n_h, d).swapaxes(0, 1)
    pos_chunks = q_pos.reshape(n_chunks, qc)
    out = lax.map(lambda args: _moba_chunk(args[0], args[1], k_blk, v_blk, k_mean),
                  (q_chunks, pos_chunks))
    return out.swapaxes(0, 1).reshape(bsz, t_len, n_h, d)

def _layer(x, c, pos, k_past, v_past, wkv0, shift0, conv0, p):
    bsz, t_len, _ = x.shape
    f32 = jnp.float32
    mod = (jax.nn.silu(c) @ p['w_ada'] + p['b_ada']).reshape(bsz, 6, 1, D_MODEL)
    shift1, scale1, gate1, shift2, scale2, gate2 = (mod[:, i] for i in range(6))

    h = _rmsnorm(x, p['norm1_g']) * (1 + scale1) + shift1
    z = h @ p['w_in']
    z_a = z[..., :Z_A]
    ob = Z_A
    q_b = z[..., ob:ob + D_B]
    k_b = z[..., ob + D_B:ob + 2 * D_B]
    v_b = z[..., ob + 2 * D_B:ob + 3 * D_B]
    gate_a = z[..., ob + 3 * D_B:ob + 3 * D_B + D_MODEL]
    gate_b = z[..., ob + 3 * D_B + D_MODEL:]

    z_prev = jnp.concatenate([shift0[:, None].astype(z_a.dtype), z_a[:, :-1]], axis=1)
    z_mix = z_a + (z_prev - z_a) * p['mu_shift']
    new_shift = z_a[:, -1]
    r = z_mix[..., :D_A]
    k_a = z_mix[..., D_A:2 * D_A]
    v_a = z_mix[..., 2 * D_A:3 * D_A]
    oa = 3 * D_A
    x_w = z_mix[..., oa:oa + LORA_W]
    x_aa = z_mix[..., oa + LORA_W:oa + LORA_W + LORA_A]
    x_g = z_mix[..., oa + LORA_W + LORA_A:]
    w_log = -jax.nn.softplus(-(p['rwkv_w0'] + jnp.tanh(x_w) @ p['rwkv_w2']).astype(f32)) - 0.5
    decay = jnp.exp(-jnp.exp(w_log))
    a = jax.nn.sigmoid(p['rwkv_a0'] + x_aa @ p['rwkv_a2'])
    g = jax.nn.sigmoid(x_g) @ p['rwkv_g2']
    heads = lambda t: t.reshape(bsz, t_len, N_HEADS_A, HEAD_A)
    kk = heads(k_a * p['rwkv_kk']).astype(f32)
    kk = kk * lax.rsqrt(jnp.maximum(jnp.sum(kk * kk, axis=-1, keepdims=True), 1e-24))
    k_a = k_a * (1 + (a - 1) * p['rwkv_ka'])
    r_h, k_h, v_h, a_h = heads(r), heads(k_a), heads(v_a), heads(a)
    wkv, y_h = _wkv_scan(wkv0, r_h, heads(decay), k_h, v_h, kk, a_h)
    mu = jnp.mean(y_h, axis=-1, keepdims=True)
    var = jnp.mean(jnp.square(y_h - mu), axis=-1, keepdims=True)
    y_h = (y_h - mu) * lax.rsqrt(var + LNX_EPS)
    bonus = jnp.sum((r_h * k_h * p['rwkv_rk']).astype(f32), axis=-1, keepdims=True) * v_h.astype(f32)
    y_a = (y_h.reshape(bsz, t_len, D_A) * p['lnx_g'] + p['lnx_b']
           + bonus.reshape(bsz, t_len, D_A))
    o_a = (y_a.astype(x.dtype) * g) @ p['w_proj_a']

    q_h = _rope(q_b.reshape(bsz, t_len, N_HEADS_B, HEAD_B), pos)
    k_hb = _rope(k_b.reshape(bsz, t_len, N_HEADS_B, HEAD_B), pos)
    v_hb = v_b.reshape(bsz, t_len, N_HEADS_B, HEAD_B)
    n_ctx = t_len if k_past is None else k_past.shape[1] + t_len
    n_blk = -(-n_ctx // MOBA_BLOCK)
    pad = jnp.zeros((bsz, n_blk * MOBA_BLOCK - n_ctx, N_HEADS_B, HEAD_B), k_hb.dtype)
    if k_past is None:
        k_all = jnp.concatenate([k_hb, pad], axis=1)
        v_all = jnp.concatenate([v_hb, pad], axis=1)
    else:
        k_all = jnp.concatenate([k_past.astype(k_hb.dtype), k_hb, pad], axis=1)
        v_all = jnp.concatenate([v_past.astype(v_hb.dtype), v_hb, pad], axis=1)
    blocks = lambda t: t.reshape(bsz, n_blk, MOBA_BLOCK, N_HEADS_B, HEAD_B)
    o_b = _moba(q_h, pos, blocks(k_all), blocks(v_all)).reshape(bsz, t_len, D_B) @ p['w_proj_b']

    mix = jax.nn.sigmoid(gate_a) * o_a + jax.nn.sigmoid(gate_b) * o_b
    x = x + gate1 * (mix @ p['w_out'])

    h2 = _rmsnorm(x, p['norm2_g']) * (1 + scale2) + shift2
    u = h2 @ p['w_up']
    u_g, u_v = u[..., :D_FF], u[..., D_FF:]
    ext = jnp.concatenate([conv0.astype(u_g.dtype), u_g], axis=1)
    conv = p['conv_b'] + ext[:, 0:t_len] * p['conv_w'][0]
    for j in range(1, CONV_W):
        conv = conv + ext[:, j:j + t_len] * p['conv_w'][j]
    new_conv = ext[:, -(CONV_W - 1):]
    f = jax.nn.gelu(conv) * u_v
    x = x + gate2 * (f @ p['w_down'])
    return x, k_hb, v_hb, wkv, new_shift, new_conv

def setup_inputs(seed: int = 0) -> dict:
    key = jax.random.key(seed)
    ks = iter(jax.random.split(key, 48))
    f32 = jnp.float32

    def nrm(shape, scale):
        return jax.random.normal(next(ks), shape, f32) * scale

    def unif(shape, lo, hi):
        return jax.random.uniform(next(ks), shape, f32, lo, hi)

    n_pages = PAST_LEN // PAGE_SIZE
    n_used = DEC_BATCH * n_pages
    n_pool = n_used + n_used // 4
    page_table = jax.random.permutation(next(ks), n_pool)[:n_used].reshape(DEC_BATCH, n_pages).astype(jnp.int32)
    return {
        'x_prompt': nrm((BATCH, SEQ, D_MODEL), 1.0),
        'x_sample': nrm((DEC_BATCH, DEC_SEQ, D_MODEL), 1.0),
        'cache_k': nrm((n_pool, PAGE_SIZE, N_HEADS_B, HEAD_B), 1.0),
        'cache_v': nrm((n_pool, PAGE_SIZE, N_HEADS_B, HEAD_B), 1.0),
        'state_wkv': nrm((DEC_BATCH, N_HEADS_A, HEAD_A, HEAD_A), 0.3),
        'state_shift': nrm((DEC_BATCH, Z_A), 1.0),
        'state_conv': nrm((DEC_BATCH, CONV_W - 1, D_FF), 1.0),
        'page_table': page_table,
        'c_prompt': nrm((BATCH, D_MODEL), 1.0),
        'c_sample': nrm((DEC_BATCH, D_MODEL), 1.0),
        'w_ada': nrm((D_MODEL, 6 * D_MODEL), 0.5 * D_MODEL ** -0.5),
        'b_ada': nrm((6 * D_MODEL,), 0.01),
        'norm1_g': 1.0 + nrm((D_MODEL,), 0.05),
        'w_in': nrm((D_MODEL, Z_IN), D_MODEL ** -0.5),
        'mu_shift': unif((Z_A,), 0.0, 1.0),
        'rwkv_w0': unif((D_A,), -4.0, 0.0),
        'rwkv_w2': nrm((LORA_W, D_A), 0.1 * LORA_W ** -0.5),
        'rwkv_a0': nrm((D_A,), 0.1),
        'rwkv_a2': nrm((LORA_A, D_A), 0.5 * LORA_A ** -0.5),
        'rwkv_g2': nrm((LORA_G, D_A), LORA_G ** -0.5),
        'rwkv_kk': 1.0 + nrm((D_A,), 0.1),
        'rwkv_ka': 1.0 + nrm((D_A,), 0.1),
        'rwkv_rk': nrm((N_HEADS_A, HEAD_A), 0.1),
        'lnx_g': 1.0 + nrm((D_A,), 0.05),
        'lnx_b': nrm((D_A,), 0.01),
        'w_proj_a': nrm((D_A, D_MODEL), D_A ** -0.5),
        'w_proj_b': nrm((D_B, D_MODEL), D_B ** -0.5),
        'w_out': nrm((D_MODEL, D_MODEL), D_MODEL ** -0.5),
        'norm2_g': 1.0 + nrm((D_MODEL,), 0.05),
        'w_up': nrm((D_MODEL, 2 * D_FF), D_MODEL ** -0.5),
        'conv_w': nrm((CONV_W, D_FF), CONV_W ** -0.5),
        'conv_b': nrm((D_FF,), 0.01),
        'w_down': nrm((D_FF, D_MODEL), D_FF ** -0.5),
        'normf_g': 1.0 + nrm((D_MODEL,), 0.05),
    }

def reference(x_prompt, x_sample, cache_k, cache_v, state_wkv, state_shift, state_conv, page_table,
              c_prompt, c_sample, w_ada, b_ada, norm1_g, w_in, mu_shift, rwkv_w0, rwkv_w2, rwkv_a0,
              rwkv_a2, rwkv_g2, rwkv_kk, rwkv_ka, rwkv_rk, lnx_g, lnx_b, w_proj_a, w_proj_b, w_out,
              norm2_g, w_up, conv_w, conv_b, w_down, normf_g):
    p = {'w_ada': w_ada, 'b_ada': b_ada, 'norm1_g': norm1_g, 'w_in': w_in, 'mu_shift': mu_shift,
         'rwkv_w0': rwkv_w0, 'rwkv_w2': rwkv_w2, 'rwkv_a0': rwkv_a0, 'rwkv_a2': rwkv_a2,
         'rwkv_g2': rwkv_g2, 'rwkv_kk': rwkv_kk, 'rwkv_ka': rwkv_ka, 'rwkv_rk': rwkv_rk,
         'lnx_g': lnx_g, 'lnx_b': lnx_b, 'w_proj_a': w_proj_a, 'w_proj_b': w_proj_b,
         'w_out': w_out, 'norm2_g': norm2_g, 'w_up': w_up, 'conv_w': conv_w, 'conv_b': conv_b,
         'w_down': w_down}

    n_p, t_p = x_prompt.shape[0], x_prompt.shape[1]
    pos_p = jnp.arange(t_p, dtype=jnp.int32)
    h_p, k_prompt, v_prompt, wkv_prompt, shift_prompt, conv_prompt = _layer(
        x_prompt, c_prompt, pos_p, None, None,
        jnp.zeros((n_p, N_HEADS_A, HEAD_A, HEAD_A), jnp.float32),
        jnp.zeros((n_p, Z_A), x_prompt.dtype),
        jnp.zeros((n_p, CONV_W - 1, D_FF), x_prompt.dtype), p)
    y_prompt = _rmsnorm(h_p, normf_g)

    n_s, t_s = x_sample.shape[0], x_sample.shape[1]
    n_pages = page_table.shape[1]
    past_len = n_pages * PAGE_SIZE
    k_past = cache_k[page_table].reshape(n_s, past_len, N_HEADS_B, HEAD_B)
    v_past = cache_v[page_table].reshape(n_s, past_len, N_HEADS_B, HEAD_B)
    pos_s = past_len + jnp.arange(t_s, dtype=jnp.int32)
    h_s, k_sample, v_sample, wkv_sample, shift_sample, conv_sample = _layer(
        x_sample, c_sample, pos_s, k_past, v_past, state_wkv, state_shift, state_conv, p)
    y_sample = _rmsnorm(h_s, normf_g)
    return (y_prompt, y_sample, k_prompt, v_prompt, wkv_prompt, shift_prompt, conv_prompt, k_sample, v_sample, wkv_sample, shift_sample, conv_sample)


_drawn_inputs = setup_inputs


def setup_inputs(seed=0):
    import zlib

    import numpy as np

    out = dict(_drawn_inputs(seed))
    spreads = {}
    factors = {'cache_k': 6.028,
     'cache_v': 5.271,
     'rwkv_w2': 4.05,
     'lnx_g': 8.0,
     'lnx_b': 64.0,
     'conv_b': 33.897}
    for name, (base, spread) in spreads.items():
        noise = np.random.default_rng([zlib.crc32(name.encode()), seed]).standard_normal(out[name].shape)
        drawn = base * np.exp(spread * noise) if base else spread * noise
        out[name] = __import__('jax').numpy.asarray(drawn.astype(out[name].dtype))
    for name, factor in factors.items():
        out[name] = (out[name] * factor).astype(out[name].dtype)
    return out
```

```python
from contextlib import ExitStack

import concourse.bass as bass
import numpy as np
from concourse import mybir

ALU = mybir.AluOpType
ACT = mybir.ActivationFunctionType
AX = mybir.AxisListType
F32 = mybir.dt.float32
F32R = mybir.dt.float32r
I32 = mybir.dt.int32

P = 128
D = 2048
KD = D // P
TP, NB, TS = 256, 8, 4
T = TP + NB * TS
NC = NB + 1
DA, HA, HEAD_A = 1024, 16, 64
DB, HB, HEAD_B = 1024, 8, 128
KA = DA // P
LORA_W, LORA_A, LORA_G = 64, 64, 160
ZA = 3 * DA + LORA_W + LORA_A + LORA_G
ZT = -(-ZA // P)
ZPAD = 1 + TP + NB * (TS + 1)
FF = 5632
KF = FF // P
PAST, PAGE = 1024, 128
NPG = PAST // PAGE
NBLK, BLK = 4, 256
ROW = PAST + NB * TS
EPAD = 2 + TP + NB * (TS + 2)
RMS_EPS, LNX_EPS, NEG = 1e-6, 64e-5, -1e30
DECAY = float(np.exp(-0.5))
SCALE = HEAD_B ** -0.5
CH = 512
LEVELS = 7


def shape_constants():
    cols, parts, n = {}, [], 0

    def add(name, a):
        nonlocal n
        full = np.zeros((P, a.shape[1]), np.float32)
        full[:a.shape[0]] = a
        cols[name] = (n, a.shape[1])
        parts.append(full)
        n += a.shape[1]

    s, t = np.arange(P)[:, None], np.arange(P)[None, :]
    add("ident", (s == t) * 1.0)
    add("mean", np.full((P, P), 1.0 / D))
    add("head", (s // HEAD_A == t // HEAD_A) * 1.0)
    add("rot", np.where(s == t + 64, -1.0, 0.0) + np.where(s == t - 64, 1.0, 0.0))
    add("lt", (s < t) * 1.0)
    add("le", (s <= t) * 1.0)
    add("nle", (s <= t) * -1.0)
    add("cumx", (s < t) * 1.0 - (s < 64))
    add("cumi", (s <= t) * 1.0 - (s < 64))
    for lev in range(LEVELS):
        b = 1 << lev
        add(f"lev{lev}", ((s // (2 * b) == t // (2 * b)) & ((s // b) % 2 == 0) & ((t // b) % 2 == 1)) * 1.0)
    s4, t4 = np.arange(NB * TS)[:, None], np.arange(NB * TS)[None, :]
    same = s4 // TS == t4 // TS
    add("lt4", (same & (s4 < t4)) * 1.0)
    add("lt4b", (same & (s4 < t4)) * 1.0)
    add("le4", (same & (s4 <= t4)) * 1.0)
    add("nle4", (same & (s4 <= t4)) * -1.0)
    add("seq", (s4 // TS == np.arange(NB)[None, :]) * 1.0)
    add("causal", np.where(t <= s, 0.0, NEG))
    r = np.arange(P)
    for g in range(2):
        b, q = 4 * g + r // 32, r % TS
        ok = (t4 // TS == b[:, None]) & (t4 % TS <= q[:, None])
        add(f"own{g}", np.where(ok, 0.0, NEG))
    half = HEAD_B // 2
    inv = np.float32(10000.0) ** (-np.arange(half, dtype=np.float32) / np.float32(half))
    pos = np.concatenate([np.arange(TP), np.tile(PAST + np.arange(TS), NB)]).astype(np.float32)
    ang = np.concatenate([inv, inv])[:, None].astype(np.float32) * pos[None, :]
    add("cos", np.cos(ang))
    add("sin", np.sin(ang))
    add("eps_rms", np.full((P, 1), RMS_EPS))
    add("eps_lnx", np.full((P, 1), LNX_EPS))
    return np.concatenate(parts, axis=1).astype(np.float32), cols


_, CCOLS = shape_constants()
NCONST = sum(w for _, w in CCOLS.values())

PARAM_ROWS = {
    "b_ada": (0, 0, 96), "norm1_g": (0, 96, 16), "norm2_g": (0, 112, 16),
    "normf_g": (1, 0, 16), "rwkv_w0": (1, 16, 8), "rwkv_a0": (1, 24, 8), "rwkv_kk": (1, 32, 8),
    "rwkv_ka": (1, 40, 8), "rwkv_rk": (1, 48, 8), "lnx_g": (1, 56, 8), "lnx_b": (1, 64, 8),
    "mu_shift": (1, 72, ZT), "conv_b": (2, 0, KF), "conv_w0": (2, 44, KF), "conv_w1": (3, 0, KF),
    "conv_w2": (3, 44, KF),
}


def build(nc, d):
    ctx = ExitStack()
    with ctx:
        def sem(name):
            return ctx.enter_context(nc.semaphore(name))

        base = -(-nc.sbuf_base // 32) * 32

        def at(name, shape, off, dt=F32):
            return nc.alloc_sbuf_tensor_at(name, shape, dt, offset=base + off)

        def size(*shape):
            n = 4
            for x in shape:
                n *= x
            return -(-n // 32) * 32

        o = 0
        cst = at("cst", [P, NCONST], o); o_cst = o; o += size(NCONST)
        par = at("par", [P, 4, P], o); o += size(4 * P)
        mod = at("mod", [P, 96, NC], o); o += size(96 * NC)
        xT = at("xT", [P, KD, T], o); o += size(KD * T)
        sconvT = at("sconvT", [P, KF, 2 * NB], o); o += size(KF * 2 * NB)
        newconv = at("newconv", [P, KF, 2 + 2 * NB], o); o += size(KF * (2 + 2 * NB))
        raw = at("raw", [P, 4, 2, CH], o); o += size(4 * 2 * CH)
        whi = at("whi", [P, 2, 2, CH], o, F32R); o += size(2 * 2 * CH)
        wlo = at("wlo", [P, 2, 2, CH], o, F32R); o += size(2 * 2 * CH)
        za_ = o
        hhi = at("hhi", [P, KD, T], za_, F32R)
        hlo = at("hlo", [P, KD, T], za_ + size(KD * T), F32R)
        o += 2 * size(KD * T)
        zb = o
        o += 2 * size(KF * T)
        assert base + o <= nc.sbuf_usable_end, (base + o, nc.sbuf_usable_end)

        def c(name, rows=P):
            n, w = CCOLS[name]
            return cst[0:rows, n:n + w]

        def pcol(name):
            t, r, n = PARAM_ROWS[name]
            return par[:, t, r:r + n]

        ident = c("ident")

        zz = zb + size(ZT * ZPAD)
        za = at("za", [P, ZT, ZPAD], zb)
        xnat = at("xnat", [P, 3, D], zz)
        prow = at("prow", [P, 4, P], zz + size(3 * D))
        cnat = at("cnat", [NC, D], zz + size(3 * D) + 2048)
        shnat = at("shnat", [NB, ZT * P], za_)
        cvnat = at("cvnat", [2 * NB, FF], za_ + size(ZT * P))
        scT = at("scT", [P, KD, NC], zb + 98304)
        o_n = zb + 57344
        sq = at("sq", [P, KD, T], o_n)
        gsc = at("gsc", [P, KD, NC], o_n + size(KD * T))
        rms = at("rms", [P, T], o_n + size(KD * T) + size(KD * NC))
        rstd = at("rstd", [P, T], o_n + size(KD * T) + size(KD * NC) + size(T))
        nsh = at("nsh", [P, ZT, NC], o_n + size(KD * T) + size(KD * NC) + 2 * size(T))
        nshn = at("nshn", [NC, ZT * P], o_n)

        yahi = at("yahi", [P, KA, T], zb, F32R)
        yalo = at("yalo", [P, KA, T], zb + 4 * KA * ZPAD, F32R)
        o_h = zb + 2 * 4 * KA * ZPAD
        o_w = zz
        o = zz

        def nxt(name, shape, dt=F32):
            nonlocal o
            n = 1
            for x in shape[1:]:
                n *= x
            r = at(name, shape, o, dt)
            o += size(n)
            assert o <= zb + 2 * size(KF * T), name
            return r

        lw = nxt("lw", [P, T])
        lsg = nxt("lsg", [P, 2, T])
        lora = nxt("lora", [P, 3, P])
        s0n = nxt("s0n", [HEAD_A, NB, 2, HEAD_A])
        s0T = nxt("s0T", [P, NB, HEAD_A])
        o_dif = o
        dif = nxt("dif", [P, 3, ZPAD])
        endS = at("endS", [P, NB, HEAD_A], o_dif)
        rkv = nxt("rkv", [P, 3, T])
        v_thw = nxt("v_thw", [P, T])
        v_tha = nxt("v_tha", [P, T])
        v_g = nxt("v_g", [P, T])
        v_ld = nxt("v_ld", [P, T])
        v_px = nxt("v_px", [P, T])
        v_pi = nxt("v_pi", [P, T])
        v_pv = nxt("v_pv", [P, T])
        v_kk = nxt("v_kk", [P, T])
        v_sq = nxt("v_sq", [P, T])
        v_k = nxt("v_k", [P, T])
        v_b = nxt("v_b", [P, T])
        v_bon = nxt("v_bon", [P, T])
        ldn = nxt("ldn", [P, 3, P])
        smallc = nxt("smallc", [P, 40])
        midc = nxt("midc", [P, 4])
        Am = nxt("Am", [P, 2, 2, 2, P])
        o_rm = o
        Rm = nxt("Rm", [P, 2, 2, 2, P])
        stout = at("stout", [HEAD_A, NB, 2, HEAD_A], o_rm)
        o_et = o
        ET = nxt("ET", [P, 2, 2, 2, P])
        Vblk = at("Vblk", [NB * TS, 2, NB, HEAD_A], o_et)
        TT = nxt("TT", [P, 2, 2, P])
        o_tn = o
        Tn = nxt("Tn", [P, 2, 2, P])
        Xs = nxt("Xs", [P, 2, 2, P])
        Ublk = at("Ublk", [NB * TS, 2, NB, HEAD_A], o_tn)
        VN = nxt("VN", [P, 3, P])
        KN = nxt("KN", [P, 3, P])
        BN = nxt("BN", [P, 3, P])
        As = nxt("As", [NB * TS, 2, 4, 32])
        ETs = nxt("ETs", [NB * TS, 2, 2, 32])
        Tns = nxt("Tns", [NB * TS, 2, 32])
        TTs = nxt("TTs", [NB * TS, 2, 32])
        Xss = nxt("Xss", [NB * TS, 2, 32])
        Ms = nxt("Ms", [P, P])
        Us = nxt("Us", [P, P])
        S1 = nxt("S1", [P, HEAD_A])
        SE = nxt("SE", [P, HEAD_A])
        stp = nxt("stp", [HEAD_A, 2, HEAD_A])
        MTs = nxt("MTs", [P, 32])
        Mss = nxt("Mss", [NB * TS, P])
        Uss = nxt("Uss", [NB * TS, P])

        ohi = at("ohi", [P, KA, T], o_h, F32R)
        olo = at("olo", [P, KA, T], o_h + size(KA * T), F32R)
        o = o_h + 2 * size(KA * T)
        vT = nxt("vT", [P, T])
        qr = nxt("qr", [P, T])
        kr = nxt("kr", [P, T])
        qs = nxt("qs", [P, HB, NB * TS])
        knh = nxt("knh", [P, 3, P])
        vnh = nxt("vnh", [P, 3, P])
        o_w = o
        qkv = nxt("qkv", [P, 3 * HB, T])
        o_at = o
        vns = nxt("vns", [NB * TS, HB, P])
        STo = nxt("STo", [NB * TS, NB, HB, TS])
        ptab = nxt("ptab", [1, NB * NPG], I32)
        of = nxt("of", [P, HB, T])
        o_at = o
        srow = nxt("srow", [P, 3, P])
        prob = nxt("prob", [P, 3, P])
        pT = nxt("pT", [P, 3, P])
        rtmp = nxt("rtmp", [P, 2, T])
        smallz = nxt("smallz", [P, 8])
        sm = nxt("sm", [P, 2, 4])
        o = o_w
        kpage = nxt("kpage", [P, 2, HB * P])
        kT = nxt("kT", [P, 2, HB, P])
        smg = nxt("smg", [P, 32])
        ST = nxt("ST", [P, NPG, 4, 32])
        assert o <= o_w + size(3 * HB * T)
        o = o_at
        srow2 = nxt("srow2", [P, ROW])
        prob2 = at("prob2", [P, ROW], o_at)
        PT2 = at("PT2", [P, NPG + 1, P], o_at + size(ROW))
        assert o_at + size(ROW) + size(9 * P) <= zb + 2 * size(KF * T)

        o_m = o_h + 2 * size(KA * T)
        mhi = at("mhi", [P, KD, T], o_m, F32R)
        mlo = at("mlo", [P, KD, T], o_m + size(KD * T), F32R)
        o = o_m + 2 * size(KD * T)
        sga = nxt("sga", [P, 4, T])
        sgb = nxt("sgb", [P, 4, T])
        mtmp = nxt("mtmp", [P, 2, T])

        fhi = at("fhi", [P, KF, T], zb, F32R)
        flo = at("flo", [P, KF, T], zb + size(KF * T), F32R)
        o_f = o_cst + size(2 * P)
        ext = at("ext", [P, 2, EPAD], o_f)
        cv = at("cv", [P, 2, EPAD], o_f + size(2 * EPAD))
        gl = at("gl", [P, 2, T], o_f + 2 * size(2 * EPAD))
        rsd = at("rsd", [P, 4, NB * TS], o_f + 2 * size(2 * EPAD))
        ff = at("ff", [P, 2, T], o_f + 2 * size(2 * EPAD) + size(2 * T))
        assert o_f + 2 * size(2 * EPAD) + 2 * size(2 * T) <= o_cst + 4 * CCOLS["eps_rms"][0]
        ynat = at("ynat", [P, 3, D], za_)
        ncn = at("ncn", [2 + 2 * NB, FF], zb)

        ps = ctx.enter_context(nc.psum_tensor("ps", [P, 8, 512], F32))

        def samp(ap):
            return ap.rearrange("p (b t) -> p b t", t=TS)

        def bc(ap, shape):
            return ap.to_broadcast(shape)

        s_cst, s_par, s_c, s_x, s_sh = (sem(n) for n in ("s_cst", "s_par", "s_c", "s_x", "s_sh"))
        s_zero = sem("s_zero")
        s_tp = sem("s_tp")
        s_tev = sem("s_tev")
        s_silu = sem("s_silu")
        s_raw = [sem(f"s_raw{r}") for r in range(4)]
        s_ada, s_adaev = sem("s_ada"), sem("s_adaev")
        s_hi, s_lo, s_mm = sem("s_hi"), sem("s_lo"), sem("s_mm")
        s_sq, s_ssq, s_rms = sem("s_sq"), sem("s_ssq"), sem("s_rms")
        s_hn, s_hhi, s_hlo = sem("s_hn"), sem("s_hhi"), sem("s_hlo")
        s_evz, s_evq, s_ev_out, s_evd = sem("s_evz"), sem("s_evq"), sem("s_ev_out"), sem("s_evd")
        s_nsh, s_nst, s_nse = sem("s_nsh"), sem("s_nst"), sem("s_nse")
        s_out = sem("s_out")

        (s_lora, s_s0, s_lmm, s_s0t, s_s0e, s_stp, s_stpo, s_sto, s_stoo) = (sem(n) for n in (
            "s_lora", "s_s0", "s_lmm", "s_s0t", "s_s0e", "s_stp", "s_stpo", "s_sto", "s_stoo"))
        (s_lin, s_dif, s_mix, s_kkq, s_kkn, s_kkr, s_thw, s_tha, s_ld, s_ldt, s_ldn, s_cum,
         s_px, s_rkk, s_bon, s_bonv, s_dec, s_tr, s_vkb, s_mat, s_am, s_et, s_X, s_Xe, s_XT, s_T) = (sem(n) for n in (
            "s_lin", "s_dif", "s_mix", "s_kkq", "s_kkn", "s_kkr", "s_thw", "s_tha", "s_ld",
            "s_ldt", "s_ldn", "s_cum", "s_px", "s_rkk", "s_bon", "s_bonv", "s_dec", "s_tr", "s_vkb", "s_mat",
            "s_am", "s_et", "s_X", "s_Xe", "s_XT", "s_T"))
        (s_m, s_me, s_u, s_ue, s_y, s_s1, s_se, s_set, s_mt, s_mte, s_mst, s_mse, s_us, s_use, s_blk, s_ys,
         s_ss, s_ses, s_sst, s_yc, s_gm, s_gq, s_gv, s_gr, s_ya, s_yah, s_yal) = (sem(n) for n in (
            "s_m", "s_me", "s_u", "s_ue", "s_y", "s_s1", "s_se", "s_set", "s_mt", "s_mte", "s_mst", "s_mse",
            "s_us", "s_use", "s_blk", "s_ys", "s_ss", "s_ses", "s_sst", "s_yc", "s_gm", "s_gq", "s_gv", "s_gr",
            "s_ya", "s_yah", "s_yal"))
        (s_knh, s_vnh, s_kvo, s_evh, s_page, s_vt, s_rot, s_rope, s_kvt, s_sc, s_smx, s_pr, s_prn, s_prt,
         s_pt2, s_o) = (sem(n) if n != "s_page" else [sem("s_page0"), sem("s_page1")] for n in (
            "s_knh", "s_vnh", "s_kvo", "s_evh", "s_page", "s_vt", "s_rot", "s_rope", "s_kvt", "s_sc",
            "s_smx", "s_pr", "s_prn", "s_prt", "s_pt2", "s_o"))
        (s_kt, s_kte, s_kta, s_ksc, s_st, s_stt, s_srow, s_pe2, s_pn2, s_pt3, s_p3e, s_pv, s_pve, s_oh, s_ol) = (sem(n) for n in (
            "s_kt", "s_kte", "s_kta", "s_ksc", "s_st", "s_stt", "s_srow", "s_pe2", "s_pn2", "s_pt3", "s_p3e",
            "s_pv", "s_pve", "s_oh", "s_ol"))
        (s_gate, s_evm, s_mx, s_mh, s_ml) = (sem(n) for n in ("s_gate", "s_evm", "s_mx", "s_mh", "s_ml"))
        (s_ext, s_cst8, s_cv, s_cv1, s_gl, s_f, s_fh, s_fl, s_ncv, s_ncn, s_nct, s_yt, s_yev) = (sem(n) for n in (
            "s_ext", "s_cst8", "s_cv", "s_cv1", "s_gl", "s_f", "s_fh", "s_fl", "s_ncv", "s_ncn", "s_nct",
            "s_yt", "s_yev"))
        s_lin2, s_kkr2, s_ezero, s_kkp, s_rm = (sem(n) for n in ("s_lin2", "s_kkr2", "s_ezero", "s_kkp", "s_rm"))
        s_rs, s_cv2, s_pvu = (sem(n) for n in ("s_rs", "s_cv2", "s_pvu"))
        s_dve = sem("s_dve")
        s_carry = sem("s_carry")

        stages = {}
        n = 0
        for name, ks, groups in (("za", 8, 7), ("qkv", 8, 6), ("merge", 24, 4), ("out", 8, 4),
                                 ("up", 8, 22), ("down", 22, 4)):
            stages[name] = (n, ks, groups)
            n += ks * groups
            assert n % 4 == 0
        ADA_G, ADA_K = 24, 8
        ADA_SLABS = ADA_G * ADA_K

        banks = [("par", None), ("c", None), ("sh", None)] + [("x", (m, q)) for m in range(3) for q in range(4)] \
            + [("cv", q) for q in range(2)]
        M_ROWS = [P, P, NB * TS]

        block = ctx.enter_context(nc.Block())

        @block.sync
        def _(sp):
            sp.dma_start(cst[:, :], d["consts"]).then_inc(s_cst, 16)
            sp.dma_start(cnat[0:1, :], d["c_prompt"]).then_inc(s_c, 16)
            sp.dma_start(cnat[1:NC, :], d["c_sample"]).then_inc(s_c, 16)

            def slab(n, step, i, src, wait, carry=False):
                r = n % 4
                if wait is not None:
                    s, v = wait
                    sp.wait_ge(s, v)
                    if carry:
                        sp.sem_inc(s_carry, 1)
                sp.dma_start(raw[:, r, :, 0:src.shape[2]], src).then_inc(s_raw[r], 16)

            def wsrc(w, k0, col, n):
                return w[k0:k0 + 2 * P, bass.ds(col, n)].rearrange("(t p) n -> p t n", p=P)

            for s in range(4):
                slab(s, 0, 0, wsrc(d["w_ada"], s * 2 * P, 0, CH), None)
            sp.wait_ge(s_zero, 1)
            for name, (t, r, n) in PARAM_ROWS.items():
                dst = prow[r:r + n, t, :]
                if name == "mu_shift":
                    sp.dma_start(prow[r:r + n - 1, t, :], d[name][0:(n - 1) * P].rearrange("(r c) -> r c", c=P)).then_inc(s_par, 16)
                    w = ZA - (n - 1) * P
                    sp.dma_start(prow[r + n - 1:r + n, t, 0:w], d[name][(n - 1) * P:ZA].rearrange("(r c) -> r c", r=1)).then_inc(s_par, 16)
                elif name == "rwkv_rk":
                    sp.dma_start(dst, d[name].rearrange("(r a) c -> r (a c)", a=2)).then_inc(s_par, 16)
                elif name.startswith("conv_w"):
                    sp.dma_start(dst, d["conv_w"][int(name[-1]), :].rearrange("(r c) -> r c", c=P)).then_inc(s_par, 16)
                else:
                    sp.dma_start(dst, d[name].rearrange("(r c) -> r c", c=P)).then_inc(s_par, 16)
            sp.dma_start(shnat[:, 0:ZA], d["state_shift"]).then_inc(s_sh, 16)
            sp.dma_start(cvnat[:, :], d["state_conv"].rearrange("b r f -> (b r) f")).then_inc(s_sh, 16)
            for m in range(2):
                sp.dma_start(xnat[:, m, :], d["x_prompt"][0, m * P:(m + 1) * P, :]).then_inc(s_x, 16)
            sp.dma_start(xnat[0:NB * TS, 2, :], d["x_sample"].rearrange("b t f -> (b t) f")).then_inc(s_x, 16)
            for s in range(4, ADA_K):
                slab(s, 0, 0, wsrc(d["w_ada"], s * 2 * P, 0, CH), (s_ada, s - 3))
            with sp.Fori(1, ADA_G) as g:
                for s in range(ADA_K):
                    slab(s, ADA_K, g, wsrc(d["w_ada"], s * 2 * P, g * CH, CH), (s_ada, g * ADA_K + (s - 3)))

            def split_group(name, src, loop0=0, groups=None):
                n0, ks, _ = stages[name]
                with sp.Fori(loop0, groups) as g:
                    for s in range(ks):
                        slab(n0 + s, ks, g, src(g, s), (s_lo, g * ks + (n0 + s - 3)))

            def za_src(g, s):
                return wsrc(d["w_in"], s * 2 * P, g * CH, CH)

            for s in range(8):
                slab(s, 0, 0, za_src(0, s), (s_ada, ADA_SLABS) if s < 4 else (s_lo, s - 3))
            split_group("za", za_src, 1, 6)
            n0 = stages["za"][0] + 48
            for s in range(8):
                slab(n0 + s, 0, 0, wsrc(d["w_in"], s * 2 * P, 6 * CH, 3 * P), (s_lo, n0 + s - 3))

            sp.wait_ge(s_nse, 7)
            sp.dma_start(d["shift_prompt"], nshn[0:1, 0:ZA]).then_inc(s_out, 16)
            sp.dma_start(d["shift_sample"], nshn[1:NC, 0:ZA]).then_inc(s_out, 16)
            with sp.Fori(0, KA) as j:
                sp.wait_ge(s_lmm, j)
                sp.wait_ge(s_s0t, j)
                cols = bass.ds(j * P, P)
                sp.dma_start(lora[0:LORA_W, 0, :], d["rwkv_w2"][:, cols]).then_inc(s_lora, 16)
                sp.dma_start(lora[LORA_W:P, 0, :], d["rwkv_a2"][:, cols]).then_inc(s_lora, 16)
                sp.dma_start(lora[:, 1, :], d["rwkv_g2"][0:P, cols]).then_inc(s_lora, 16)
                sp.dma_start(lora[0:LORA_G - P, 2, :], d["rwkv_g2"][P:LORA_G, cols]).then_inc(s_lora, 16)
                for b in range(NB):
                    sp.dma_start(s0n[:, b, :, :], d["state_wkv"][b, bass.ds(j * 2, 2), :, :].rearrange("h v k -> v h k")).then_inc(s_s0, 16)
                sp.wait_ge(s_stp, j + 1)
                sp.dma_start(d["wkv_prompt"][0, bass.ds(j * 2, 2), :, :].rearrange("h v k -> v h k"), stp[:, :, :]).then_inc(s_stpo, 16)
                sp.wait_ge(s_sto, 2 * j + 2)
                for b in range(NB):
                    sp.dma_start(d["wkv_sample"][b, bass.ds(j * 2, 2), :, :].rearrange("h v k -> v h k"), stout[:, b, :, :]).then_inc(s_stoo, 16)

            split_group("qkv", lambda g, s: wsrc(d["w_in"], s * 2 * P, g * CH + ZA, CH), 0, 6)

            sp.dma_start(ptab[:, :], d["page_table"].rearrange("(o b) p -> o (b p)", o=1)).then_inc(s_sh, 16)
            with sp.Fori(0, HB) as h:
                hh = bass.ds(h, 1)
                for nat, ready, po, so in ((knh, s_knh, "k_prompt", "k_sample"), (vnh, s_vnh, "v_prompt", "v_sample")):
                    sp.wait_ge(ready, h + 1)
                    sp.dma_start(d[po][0, :, hh, :].rearrange("(c p) h f -> p c (h f)", p=P), nat[:, 0:2, :]).then_inc(s_kvo, 16)
                    sp.dma_start(d[so][:, :, hh, :].rearrange("b t h f -> (b t) (h f)"), nat[0:NB * TS, 2, :]).then_inc(s_kvo, 16)
            sp.wait_ge(s_sh, 48)
            sp.wait_ge(s_evh, HB)
            for g in range(2):
                for kv, cache in enumerate(("cache_k", "cache_v")):
                    with sp.Fori(0, 16) as i:
                        for r in range(2):
                            n = g * 64 + kv * 32 + r
                            page = sp.value_load(ptab[0:1, bass.ds(i * 2 + (g * 32 + r), 1)], min_val=0, max_val=d[cache].shape[0] - 1)
                            if kv == 0:
                                sp.wait_ge(s_kt, i * 2 + (32 * g))
                                sp.wait_ge(s_pvu, 32 * g)
                            else:
                                sp.wait_ge(s_kt, 32 * (g + 1))
                                sp.wait_ge(s_pvu, i * 2 + (32 * g))
                            sp.dma_start(kpage[:, r, :], d[cache][bass.ds(page, 1), :, :, :].rearrange("o p h f -> p (o h f)")).then_inc(s_page[r], 16)

            g0 = ZA + 3 * DB
            n0 = stages["merge"][0]
            with sp.Fori(0, 4) as g:
                parts = [(d["w_in"], g0, 8), (d["w_in"], g0 + D, 8), (d["w_proj_a"], 0, 4), (d["w_proj_b"], 0, 4)]
                s = 0
                for w, col, ks in parts:
                    for k in range(ks):
                        slab(n0 + s, 24, g, wsrc(w, k * 2 * P, g * CH + col, CH), (s_lo, g * 24 + (n0 + s - 3)), s == 16)
                        s += 1
            split_group("out", lambda g, s: wsrc(d["w_out"], s * 2 * P, g * CH, CH), 0, 4)
            n0 = stages["up"][0]
            with sp.Fori(0, 22) as g:
                for s in range(8):
                    r = (n0 + s) % 4
                    sp.wait_ge(s_lo, g * 8 + (n0 + s - 3))
                    for half in range(2):
                        sp.dma_start(raw[:, r, :, half * 256:half * 256 + 256],
                                     wsrc(d["w_up"], s * 2 * P, g * 256 + half * FF, 256)).then_inc(s_raw[r], 16)
            n0 = stages["down"][0]
            with sp.Fori(0, 2) as i:
                for gg in range(2):
                    for s in range(22):
                        q = gg * 22 + s
                        slab(n0 + q, 44, i, wsrc(d["w_down"], s * 2 * P, i * 1024 + gg * CH, CH), (s_lo, i * 44 + (n0 + q - 3)))
            sp.wait_ge(s_ncn, 11)
            sp.dma_start(d["conv_prompt"][0, :, :], ncn[0:2, :]).then_inc(s_out, 16)
            sp.dma_start(d["conv_sample"].rearrange("b r f -> (b r) f"), ncn[2:2 + 2 * NB, :]).then_inc(s_out, 16)
            for m in range(3):
                sp.wait_ge(s_yev, 4 * (m + 1))
                if m < 2:
                    sp.dma_start(d["y_prompt"][0, m * P:(m + 1) * P, :], ynat[:, m, :]).then_inc(s_out, 16)
                else:
                    sp.dma_start(d["y_sample"].rearrange("b t f -> (b t) f"), ynat[0:NB * TS, 2, :]).then_inc(s_out, 16)
            sp.wait_ge(s_out, 16 * 7)
            sp.wait_ge(s_stpo, 16 * KA)
            sp.wait_ge(s_stoo, 16 * NB * KA)
            sp.wait_ge(s_kvo, 64 * HB)


        def landed(name, g, s):
            n0, ks, _ = stages[name]
            up0 = stages["up"][0]
            n = n0 + ks * g.c + s
            v, per = 16 * (ADA_SLABS // 4 + n // 4 + 1), 4
            if name == "up":
                v, per = v + 16 * ((n - up0) // 4 + 1), 8
            if name == "down":
                v += 16 * (stages["down"][0] - up0) // 4
            return v if g.i is None else g.i * (g.a * ks * per) + v

        class Chain:

            def __init__(self, eng, s):
                self.eng, self.s, self.base, self.n, self.i, self.per = eng, s, 0, 0, 0, 0

            def inc(self, ins):
                ins.then_inc(self.s, 1)
                self.n += 1

            def wait(self):
                self.eng.wait_ge(self.s, self.i * self.per + (self.base + self.n) if self.per else self.base + self.n)

            def __call__(self, ins):
                self.inc(ins)
                self.wait()

            def enter(self, i, per):
                self.base, self.n, self.i, self.per = self.base + self.n, 0, i, per

            def leave(self, trips):
                assert self.n == self.per, ("per", self.n)
                self.base, self.n, self.i, self.per = self.base + self.n * trips, 0, 0, 0

        def pbank(b):
            return ps[:, b, :]

        class G:

            def __init__(self, a, i, c):
                self.a, self.i, self.c = a, i, c
                self.parity = c % 2
                self.first = i is None and c == 0

            def at(self, k, plus=0):
                v = self.c * k + plus
                return v if self.i is None else self.i * (self.a * k) + v

            def prev(self):
                return G(self.a, self.i, self.c - 1)

        def over(eng, ng, body):
            body(G(0, None, 0))
            pairs = (ng - 1) // 2
            if pairs:
                with eng.Fori(0, pairs) as i:
                    body(G(2, i, 1))
                    body(G(2, i, 2))
            if (ng - 1) % 2:
                body(G(0, None, ng - 1))
            return G(0, None, ng - 1)

        @block.gpsimd
        def _(pool):
            pool.wait_ge(s_evz, 7)
            pool.wait_ge(s_nst, 7)
            pool.wait_ge(s_lin, 2)
            zv = za[:, 0:3 * KA, :].rearrange("p (g j) c -> p g j c", g=3)
            with pool.Fori(0, KA) as j:
                jj = bass.ds(j, 1)
                pool.wait_ge(s_ss, j)
                pool.wait_ge(s_sst, 2 * j)
                pool.wait_ge(s_mix, j)
                pool.tensor_tensor(dif[:, :, 1:ZPAD], zv[:, :, jj, 0:ZPAD - 1].rearrange("p g j c -> p g (j c)"),
                                   zv[:, :, jj, 1:ZPAD].rearrange("p g j c -> p g (j c)"), ALU.subtract).then_inc(s_dif, 1)
                pool.wait_ge(s_am, 4 * j + 4)
                for lev in range(LEVELS):
                    b = lev % 2
                    if lev >= 2:
                        pool.wait_ge(s_X, j * LEVELS + (lev - 1))
                    if lev == 2:
                        pool.wait_ge(s_T, j * LEVELS + 1)
                    for e in range(2):
                        i = pool.tensor_tensor(ET[:, b, e, :, :], Am[:, e, 1, :, :],
                                               bc(c(f"lev{lev}").unsqueeze(1), [P, 2, P]), ALU.mult)
                        if lev < 2:
                            i = pool.tensor_tensor(ETs[:, lev, e, :], As[:, e, 1, :],
                                                   c(f"lev{lev}", 32)[:, 0:32], ALU.mult)
                    i.then_inc(s_et, 1)

            pool.wait_ge(s_tev, len(banks) - 1)
            with pool.Fori(0, KF // 2) as g:
                pool.wait_ge(s_cv1, 2 * g)
                e8 = ext[:, :, 2 + TP:EPAD].rearrange("p h (b t) -> p h b t", t=TS + 2)
                for h in range(2):
                    i = pool.tensor_copy(e8[:, h, :, 0:2], sconvT[:, bass.ds(g * 2 + h, 1), :].rearrange("p o (b r) -> p (o b) r", r=2))
                i.then_inc(s_cst8, 1)
                pool.wait_ge(s_ext, g + 1)
                for h in range(2):
                    nv = newconv[:, bass.ds(g * 2 + h, 1), :].rearrange("p o c -> p (o c)")
                    pool.tensor_copy(nv[:, 0:2], ext[:, h, TP:TP + 2])
                    i = pool.tensor_copy(nv[:, 2:].rearrange("p (b r) -> p b r", r=2), e8[:, h, :, TS:TS + 2])
                i.then_inc(s_ncv, 1)

        @block.scalar
        def _(act):

            def copy(o, i, **k):
                return act.activation(o, i, ACT.Copy, **k)

            act.wait_ge(s_tp, 2)
            act.activation(scT[:, :, :], pbank(1)[:, 0:KD * NC].rearrange("p (k c) -> p k c", c=NC), ACT.Silu).then_inc(s_silu, 1)

            def norm(u, lookahead):
                for q in range(4):
                    act.activation(sq[:, 4 * q:4 * q + 4, :], xT[:, 4 * q:4 * q + 4, :], ACT.Square).then_inc(s_sq, 1)
                act.wait_ge(s_ssq, u + 1)
                act.activation(rms[:, :], pbank(0)[:, 0:T], ACT.Sqrt, bias=c("eps_rms")).then_inc(s_rms, 1)
                for q in range(4):
                    if u < 2:
                        act.wait_ge(s_hn, 4 * u + q + 1)
                        copy(hhi[:, 4 * q:4 * q + 4, :], sq[:, 4 * q:4 * q + 4, :]).then_inc(s_hhi, 1)

            def hi(name, g, s, width=CH):
                n0, ks, _ = stages[name]
                n = n0 + ks * g.c + s
                act.wait_ge(s_raw[n % 4], landed(name, g, s))
                if n >= 2:
                    act.wait_ge(s_mm, g.at(ks, n0 + s - 1))
                copy(whi[:, n % 2, :, 0:width], raw[:, n % 4, :, 0:width]).then_inc(s_hi, 1)

            act.wait_ge(s_tev, 2 + 12)
            norm(0, 0)

            def za_evac(g, n=4):
                b4 = 4 * g.parity
                act.wait_ge(s_mm, g.at(8, 8))
                zt = za[:, bass.ds(g.at(4), n), :]
                copy(zt[:, :, 1:1 + TP], ps[:, b4:b4 + n, 0:TP])
                for k in range(n):
                    i = copy(za[:, bass.ds(g.at(4, k), 1), 1 + TP:].rearrange("p o (b t) -> p (o b) t", t=TS + 1)[:, :, 1:],
                             samp(ps[:, b4 + k, TP:T]))
                i.then_inc(s_evz, 1)

            act.wait_ge(s_adaev, ADA_G)

            def za_group(g):
                for s in range(8):
                    hi("za", g, s, 3 * P if g.i is None and g.c == 6 else CH)
                    if s == 1 and not g.first:
                        za_evac(g.prev())
            za_evac(over(act, 7, za_group), 3)
            act.wait_ge(s_lin, 2)
            act.activation(lw[0:LORA_W, :], rkv[0:LORA_W, 0, :], ACT.Tanh)
            copy(lw[LORA_W:P, :], rkv[LORA_W:P, 0, :])
            act.activation(lsg[:, :, :], rkv[:, 1:3, :], ACT.Sigmoid).then_inc(s_lin2, 1)

            act.wait_ge(s_out, 32)
            with act.Fori(0, KA) as j:
                jc = bass.ds(j, 1)
                w0h, a0h = smallc[:, bass.ds(j, 1)], smallc[:, bass.ds(j + 8, 1)]
                act.wait_ge(s_lmm, j + 1)
                act.wait_ge(s_yal, j)
                act.activation(v_thw[:, :], pbank(0)[:, 0:T], ACT.Tanh, bias=w0h, scale=0.5).then_inc(s_thw, 1)
                act.activation(v_tha[:, :], pbank(1)[:, 0:T], ACT.Tanh, bias=a0h, scale=0.5).then_inc(s_tha, 1)
                copy(v_g[:, :], pbank(2)[:, 0:T])
                act.wait_ge(s_kkn, j + 1)
                act.activation(v_pv[:, :], v_pv[:, :], ACT.Sqrt).then_inc(s_kkr, 1)
                act.wait_ge(s_ldt, j + 1)
                copy(ldn[:, 0:2, :], pbank(4)[:, 0:2 * P].rearrange("p (c f) -> p c f", f=P))
                copy(ldn[0:NB * TS, 2, :], pbank(4)[0:NB * TS, 2 * P:3 * P]).then_inc(s_ldn, 1)
                act.wait_ge(s_cum, j + 1)
                act.activation(v_px[:, :], pbank(5)[:, 0:T], ACT.Exp)
                act.activation(v_pi[:, :], pbank(6)[:, 0:T], ACT.Exp)
                act.wait_ge(s_kkr2, j + 1)
                act.activation(v_pv[:, :], pbank(6)[:, 0:T], ACT.Exp, scale=-1.0)
                act.activation(midc[:, 0:2], pbank(5)[:, 0:2 * P:P], ACT.Exp, scale=-1.0).then_inc(s_px, 1)
                act.wait_ge(s_tr, j + 1)
                m = NB * TS
                copy(VN[:, 0:2, :], pbank(0)[:, 0:2 * P].rearrange("p (c f) -> p c f", f=P))
                copy(KN[:, 0:2, :], pbank(0)[:, 2 * P:4 * P].rearrange("p (c f) -> p c f", f=P))
                copy(BN[:, 0:2, :], pbank(1)[:, 0:2 * P].rearrange("p (c f) -> p c f", f=P), scale=-1.0)
                copy(VN[0:m, 2, :], pbank(4)[0:m, 0:P])
                copy(KN[0:m, 2, :], pbank(4)[0:m, P:2 * P])
                copy(BN[0:m, 2, :], pbank(4)[0:m, 2 * P:3 * P], scale=-1.0).then_inc(s_vkb, 1)
                for lev in range(1, LEVELS):
                    act.wait_ge(s_X, j * LEVELS + lev + 1)
                    i = copy(Xs[:, :, :, :], pbank(0).rearrange("p (e c t) -> p e c t", e=2, c=2))
                    if lev == 1:
                        i = copy(Xss[:, :, :], pbank(3)[0:m, 0:64].rearrange("p (e t) -> p e t", e=2))
                    i.then_inc(s_Xe, 1)
                act.wait_ge(s_s0t, j + 1)
                copy(s0T[:, :, :], pbank(2).rearrange("p (b v) -> p b v", b=NB)).then_inc(s_s0e, 1)
                for ck in range(2):
                    act.wait_ge(s_m, 2 * j + ck + 1)
                    if ck == 0:
                        copy(Ms[:, :], pbank(5)[:, 0:P]).then_inc(s_me, 1)
                    else:
                        copy(Ms[:, 0:64], pbank(5)[:, 0:64])
                        copy(Ms[:, 64:P], pbank(6)[:, 0:64]).then_inc(s_me, 1)
                    act.wait_ge(s_u, 2 * j + ck + 1)
                    copy(Us[:, :], pbank(7)[:, 0:P]).then_inc(s_ue, 1)
                act.wait_ge(s_mt, j + 1)
                copy(MTs[0:64, :], pbank(5)[0:64, P:P + m])
                copy(MTs[64:P, :], pbank(6)[64:P, P:P + m]).then_inc(s_mte, 1)
                act.wait_ge(s_mst, j + 1)
                copy(Mss[:, :], pbank(0)[0:m, 0:P]).then_inc(s_mse, 1)
                act.wait_ge(s_us, j + 1)
                copy(Uss[:, :], pbank(7)[0:m, 2 * P:3 * P]).then_inc(s_use, 1)
                act.wait_ge(s_set, j + 1)
                act.wait_ge(s_stpo, 16 * j)
                copy(stp[:, :, :], pbank(2)[0:64, 0:P].rearrange("p (h k) -> p h k", h=2)).then_inc(s_stp, 1)
                for h in range(2):
                    act.wait_ge(s_sst, 2 * j + h + 1)
                    act.wait_ge(s_ys, j + 1)
                    act.wait_ge(s_stoo, 16 * NB * j)
                    copy(stout[:, 4 * h:4 * h + 4, :, :].rearrange("p b h k -> p (b h k)"), pbank(5 + h)[0:64, :]).then_inc(s_sto, 1)
                act.wait_ge(s_gq, j + 1)
                act.activation(v_px[:, :], pbank(7)[:, 0:T], ACT.Sqrt, bias=c("eps_lnx"), scale=1.0 / HEAD_A).then_inc(s_gr, 1)
                act.wait_ge(s_ya, j + 1)
                act.activation(yahi[:, jc, :].rearrange("p o t -> p (o t)"), v_thw[:, :], ACT.Copy).then_inc(s_yah, 1)

            def plain(name):
                def group(g):
                    for s in range(stages[name][1]):
                        hi(name, g, s)
                over(act, stages[name][2], group)

            plain("qkv")

            with act.Fori(0, HB) as h:
                act.wait_ge(s_evq, 6)
                act.wait_ge(s_kvt, h)
                copy(vT[:, :], qkv[:, bass.ds(h + 2 * HB, 1), :].rearrange("p o t -> p (o t)")).then_inc(s_vt, 1)
                act.wait_ge(s_kvt, h + 1)
                act.wait_ge(s_kvo, 64 * h)
                act.wait_ge(s_o, h)
                m = NB * TS
                copy(knh[:, 0:2, :], pbank(2)[:, 0:2 * P].rearrange("p (c f) -> p c f", f=P))
                copy(knh[0:m, 2, :], pbank(2)[0:m, 2 * P:3 * P]).then_inc(s_knh, 1)
                copy(vnh[:, 0:2, :], pbank(3)[:, 0:2 * P].rearrange("p (c f) -> p c f", f=P))
                copy(vnh[0:m, 2, :], pbank(3)[0:m, 2 * P:3 * P])
                copy(vns[:, bass.ds(h, 1), :].rearrange("p o f -> p (o f)"), pbank(3)[0:m, 2 * P:3 * P]).then_inc(s_vnh, 1)
                act.wait_ge(s_smx, h + 1)
                act.activation(prob[:, 0, :], srow[:, 0, :], ACT.Exp, bias=sm[:, 0, 0:1], accum_out=sm[:, 1, 0:1])
                act.activation(prob[:, 1:3, :], srow[:, 1:3, :], ACT.Exp, bias=sm[:, 0, 1:2], accum_out=sm[:, 1, 1:2]).then_inc(s_pr, 1)
                act.wait_ge(s_prt, h + 1)
                copy(pT[:, :, :], pbank(6)[:, 0:3 * P].rearrange("p (c f) -> p c f", f=P)).then_inc(s_pt2, 1)

            m = NB * TS
            for g in range(2):
                with act.Fori(0, 16) as i:
                    for r in range(2):
                        act.wait_ge(s_kt, i * 2 + (32 * g + r + 1))
                        act.wait_ge(s_ksc, i * 2 + max(32 * g + r - 1, 0))
                        copy(kT[:, r, 4:8, :].rearrange("p h f -> p (h f)"), pbank(2 * r + 1)).then_inc(s_kta, 1)
                act.wait_ge(s_srow, g + 1)
                act.activation(prob2[:, :], srow2[:, :], ACT.Exp, bias=smg[:, 0:1], accum_out=smg[:, 1:2]).then_inc(s_pe2, 1)
            act.wait_ge(s_pve, 8)
            copy(ohi[:, :, :], of[:, :, :]).then_inc(s_oh, 1)

            with act.Fori(0, 4) as i:
                g = G(1, i, 0)
                m0 = stages["merge"][0]
                for s in range(24):
                    hi("merge", g, s)
                    if s == 9:
                        act.wait_ge(s_mm, g.at(24, m0 + 8))
                        act.wait_ge(s_ml, g.at(4))
                        act.activation(sga[:, :, :], ps[:, 0:4, 0:T], ACT.Sigmoid).then_inc(s_gate, 1)
                    if s == 17:
                        act.wait_ge(s_mm, g.at(24, m0 + 16))
                        act.activation(sgb[:, :, :], ps[:, 4:8, 0:T], ACT.Sigmoid).then_inc(s_gate, 1)
                for q in range(4):
                    act.wait_ge(s_mx, g.at(4, q + 1))
                    copy(mhi[:, bass.ds(g.at(4, q), 1), :].rearrange("p o t -> p (o t)"), sga[:, q, :]).then_inc(s_mh, 1)
            plain("out")
            act.wait_ge(s_ev_out, 4)
            norm(1, 0)

            cb, w0 = pcol("conv_b"), pcol("conv_w0")

            def up_in(g):
                b4 = 4 * g.parity
                act.wait_ge(s_mm, g.at(8, stages["up"][0] + 8))
                act.wait_ge(s_cv1, g.at(2))
                act.wait_ge(s_ncv, g.at(1))
                copy(ext[:, :, 2:2 + TP], ps[:, b4:b4 + 2, 0:TP])
                for h in range(2):
                    e8 = ext[:, h, 2 + TP:EPAD].rearrange("p (b t) -> p b t", t=TS + 2)
                    i = copy(e8[:, :, 2:], samp(ps[:, b4 + h, TP:T]))
                i.then_inc(s_ext, 1)
                act.wait_ge(s_ext, g.at(1, 1))
                act.wait_ge(s_cst8, g.at(1, 1))
                act.wait_ge(s_ezero, 1)
                act.wait_ge(s_gl, g.at(1))
                for h in range(2):
                    act.activation(cv[:, h, 0:EPAD - 2], ext[:, h, 0:EPAD - 2], ACT.Identity, bias=cb[:, bass.ds(g.at(2, h), 1)],
                                   scale=w0[:, bass.ds(g.at(2, h), 1)]).then_inc(s_cv, 1)

            def up_gelu(g):
                act.wait_ge(s_cv1, g.at(2, 2))
                act.wait_ge(s_f, g.at(1))
                act.activation(gl[:, :, 0:TP], cv[:, :, 0:TP], ACT.Gelu_apprx_tanh)
                for h in range(2):
                    i = act.activation(samp(gl[:, h, TP:T]), cv[:, h, 2 + TP:EPAD].rearrange("p (b t) -> p b t", t=TS + 2)[:, :, 0:TS],
                                       ACT.Gelu_apprx_tanh)
                i.then_inc(s_gl, 1)

            def up_hi(g):
                act.wait_ge(s_f, g.at(1, 1))
                copy(fhi[:, bass.ds(g.at(2), 2), :], ff[:, :, :]).then_inc(s_fh, 1)

            def up_group(g):
                for s in range(8):
                    hi("up", g, s)
                    if not g.first and s in (1, 3, 5):
                        (up_in if s == 1 else up_gelu if s == 3 else up_hi)(g.prev())

            last = over(act, 22, up_group)
            up_in(last)
            up_gelu(last)
            up_hi(last)
            plain("down")
            act.wait_ge(s_evd, 4)
            norm(2, 0)

        @block.vector
        def _(dve):
            own = Chain(dve, s_dve)
            TTn, STT, TS_ = dve.tensor_tensor, dve.scalar_tensor_tensor, dve.tensor_scalar
            m = NB * TS
            dve.memset(prow[:, :, :], 0.0).then_inc(s_zero, 1)
            own(dve.memset(shnat[:, ZA:], 0.0))
            own(dve.memset(za[:, :, 0:1], 0.0))
            for bi, (kind, at_) in enumerate(banks):
                src = pbank(bi % 8)
                if kind == "c":
                    continue
                dve.wait_ge(s_tp, bi + 1)
                if kind == "par":
                    i = dve.tensor_copy(par[:, :, :], src.rearrange("p (t c) -> p t c", t=4))
                elif kind == "sh":
                    i = dve.tensor_copy(za[:, :, 1 + TP:ZPAD].rearrange("p k (b t) -> p k b t", t=TS + 1)[:, :, :, 0],
                                        src[:, 0:ZT * NB].rearrange("p (k b) -> p k b", b=NB))
                elif kind == "x":
                    mt, q = at_
                    w = M_ROWS[mt]
                    i = dve.tensor_copy(xT[:, 4 * q:4 * q + 4, mt * P:mt * P + w],
                                        src.rearrange("p (i t) -> p i t", i=4)[:, :, 0:w])
                else:
                    i = dve.tensor_copy(sconvT[:, 22 * at_:22 * at_ + 22, :],
                                        src[:, 0:22 * 2 * NB].rearrange("p (k b) -> p k b", b=2 * NB))
                i.then_inc(s_tev, 1)

            bada = pcol("b_ada")
            dve.wait_ge(s_tev, 1)

            def ada_evac(g):
                b4 = 4 * g.parity
                dve.wait_ge(s_ada, g.at(ADA_K, ADA_K))
                TTn(mod[:, bass.ds(g.at(4), 4), :], ps[:, b4:b4 + 4, 0:NC],
                    bc(bada[:, bass.ds(g.at(4), 4)].unsqueeze(2), [P, 4, NC]), ALU.add).then_inc(s_adaev, 1)

            over(dve, ADA_G, ada_evac)
            dve.wait_ge(s_adaev, ADA_G)

            def norm(u, gname, shift, scale):
                if u < 2:
                    own(STT(gsc[:, :, :], mod[:, scale:scale + KD, :], 1.0,
                            bc(pcol(gname).unsqueeze(2), [P, KD, NC]), ALU.add, ALU.mult))
                dve.wait_ge(s_rms, u + 1)
                own(dve.reciprocal(rstd[:, :], rms[:, :]))
                for q in range(4):
                    k4 = slice(4 * q, 4 * q + 4)
                    own(TTn(sq[:, k4, :], xT[:, k4, :], bc(rstd[:, :].unsqueeze(1), [P, 4, T]), ALU.mult))
                    if u == 2:
                        TTn(sq[:, k4, :], sq[:, k4, :], bc(pcol(gname)[:, k4].unsqueeze(2), [P, 4, T]), ALU.mult).then_inc(s_hn, 1)
                        continue
                    for k in range(4 * q, 4 * q + 4):
                        own.inc(TS_(sq[:, k, 0:TP], sq[:, k, 0:TP], gsc[:, k, 0:1], mod[:, shift + k, 0:1], ALU.mult, ALU.add))
                        own.inc(TTn(samp(sq[:, k, TP:T]), samp(sq[:, k, TP:T]), bc(gsc[:, k, 1:NC].unsqueeze(2), [P, NB, TS]), ALU.mult))
                    own.wait()
                    for k in range(4 * q, 4 * q + 4):
                        i = TTn(samp(sq[:, k, TP:T]), samp(sq[:, k, TP:T]), bc(mod[:, shift + k, 1:NC].unsqueeze(2), [P, NB, TS]), ALU.add)
                    i.then_inc(s_hn, 1)
                    if q:
                        norm_lo(u, q - 1)
                if u < 2:
                    norm_lo(u, 3)

            def norm_lo(u, q):
                k4 = slice(4 * q, 4 * q + 4)
                dve.wait_ge(s_hhi, 4 * u + q + 1)
                TTn(hlo[:, k4, :], sq[:, k4, :], hhi[:, k4, :].bitcast(F32), ALU.subtract).then_inc(s_hlo, 1)

            norm(0, "norm1_g", 0, KD)

            def lo(name, g, s, width=CH):
                n0, ks, _ = stages[name]
                n = n0 + ks * g.c + s
                dve.wait_ge(s_hi, g.at(ks, n0 + s + 1))
                TTn(wlo[:, n % 2, :, 0:width], raw[:, n % 4, :, 0:width], whi[:, n % 2, :, 0:width].bitcast(F32),
                    ALU.subtract).then_inc(s_lo, 1)

            def plain(name, evac):
                ks = stages[name][1]

                def group(g):
                    for s in range(ks):
                        lo(name, g, s, 3 * P if name == "za" and g.i is None and g.c == 6 else CH)
                        if s == 1 and evac and not g.first:
                            evac(g.prev())
                last = over(dve, stages[name][2], group)
                if evac:
                    evac(last)

            plain("za", None)
            dve.wait_ge(s_evz, 7)
            own(dve.tensor_copy(nsh[:, :, 0:1], za[:, :, TP:TP + 1]))
            dve.tensor_copy(nsh[:, :, 1:NC], za[:, :, 1 + TP:].rearrange("p k (b t) -> p k b t", t=TS + 1)[:, :, :, TS]).then_inc(s_nsh, 1)
            for b in range(7):
                w = min(4, ZT - 4 * b) * P
                dve.wait_ge(s_nst, b + 1)
                dve.tensor_copy(nshn[:, 4 * b * P:4 * b * P + w], pbank(b)[0:NC, 0:w]).then_inc(s_nse, 1)

            dve.wait_ge(s_out, 32)
            own.inc(TS_(smallc[:, 0:8], pcol("rwkv_w0"), 0.5, None, ALU.mult))
            own.inc(TS_(smallc[:, 8:16], pcol("rwkv_a0"), 0.5, None, ALU.mult))
            own.inc(TS_(smallc[:, 16:24], pcol("rwkv_ka"), 0.5, None, ALU.mult))
            own.inc(TS_(smallc[:, 24:32], pcol("rwkv_ka"), -0.5, 1.0, ALU.mult, ALU.add))
            own.wait()
            own(dve.memset(smallc[:, 32:40], 0.0))
            mu = pcol("mu_shift")

            def mix(dst, df, z, muc):
                STT(dst[:, 0:TP], df[:, 1:1 + TP], muc, z[:, 1:1 + TP], ALU.mult, ALU.add)
                dv, zv = (a[:, 1 + TP:ZPAD].rearrange("p (b t) -> p b t", t=TS + 1)[:, :, 1:] for a in (df, z))
                return STT(samp(dst[:, TP:T]), dv, muc, zv, ALU.mult, ALU.add)

            for q in range(3):
                z = za[:, 3 * KA + q, :]
                own(TTn(dif[:, q, 1:ZPAD], z[:, 0:ZPAD - 1], z[:, 1:ZPAD], ALU.subtract))
                i = mix(rkv[:, q, :], dif[:, q, :], z, mu[:, 3 * KA + q:3 * KA + q + 1])
                if q:
                    i.then_inc(s_lin, 1)
            dve.wait_ge(s_lin2, 1)

            def pc(name, j):
                return pcol(name)[:, bass.ds(j, 1)]

            with dve.Fori(0, KA) as j:
                own.enter(j, 37)
                r_, k_, v_ = rkv[:, 0, :], rkv[:, 1, :], rkv[:, 2, :]
                dve.wait_ge(s_dif, j + 1)
                for q in range(3):
                    z = za[:, bass.ds(j + q * KA, 1), :].rearrange("p o t -> p (o t)")
                    i = mix(rkv[:, q, :], dif[:, q, :], z, mu[:, bass.ds(j + q * KA, 1)])
                i.then_inc(s_mix, 1)
                dve.wait_ge(s_mix, j + 1)
                own(TS_(v_kk[:, :], k_, pc("rwkv_kk", j), None, ALU.mult))
                TTn(v_sq[:, :], v_kk[:, :], v_kk[:, :], ALU.mult).then_inc(s_kkq, 1)
                dve.wait_ge(s_thw, j + 1)
                TS_(v_ld[:, :], v_thw[:, :], -0.5 * DECAY, -0.5 * DECAY, ALU.mult, ALU.add).then_inc(s_ld, 1)
                dve.wait_ge(s_kkp, j + 1)
                TS_(v_pv[:, :], pbank(3)[:, 0:T], 1e-24, None, ALU.max).then_inc(s_kkn, 1)
                dve.wait_ge(s_tha, j + 1)
                own(TS_(v_k[:, :], v_tha[:, :], smallc[:, bass.ds(j + 16, 1)], smallc[:, bass.ds(j + 24, 1)], ALU.mult, ALU.add))
                own(TTn(v_k[:, :], v_k[:, :], k_, ALU.mult))
                own(TS_(v_tha[:, :], v_tha[:, :], 0.5, 0.5, ALU.mult, ALU.add))
                STT(v_sq[:, :], r_, pc("rwkv_rk", j), v_k[:, :], ALU.mult, ALU.mult).then_inc(s_rkk, 1)
                dve.wait_ge(s_kkr, j + 1)
                own(dve.reciprocal(v_pv[:, :], v_pv[:, :]))
                TTn(v_kk[:, :], v_kk[:, :], v_pv[:, :], ALU.mult).then_inc(s_kkr2, 1)
                dve.wait_ge(s_kkr2, j + 1)
                own(TTn(v_b[:, :], v_kk[:, :], v_tha[:, :], ALU.mult))
                dve.wait_ge(s_bon, j + 1)
                TTn(v_bon[:, :], pbank(7)[:, 0:T], v_, ALU.mult).then_inc(s_bonv, 1)
                dve.wait_ge(s_px, j + 1)
                own.inc(TTn(v_k[:, :], v_k[:, :], v_pv[:, :], ALU.mult))
                own.inc(TTn(v_b[:, :], v_b[:, :], v_pv[:, :], ALU.mult))
                own.inc(TTn(v_kk[:, :], v_kk[:, :], v_px[:, :], ALU.mult))
                own(TTn(r_, r_, v_pi[:, :], ALU.mult))
                TTn(midc[:, 2:3], midc[:, 1:2], v_pi[:, P - 1:P], ALU.mult).then_inc(s_dec, 1)
                dve.wait_ge(s_mat, j + 1)
                for e in range(2):
                    TTn(Am[:, e, :, :, :].rearrange("p a c t -> p (a c) t"), pbank(2 + e).rearrange("p (a t) -> p a t", t=P),
                        bc(c("lt").unsqueeze(1), [P, 4, P]), ALU.mult).then_inc(s_am, 1)
                n4 = CCOLS["lt4"][0]
                for e in range(2):
                    src = pbank(7)[0:m, 0:P] if e == 0 else pbank(4)[0:m, 3 * P:4 * P]
                    TTn(As[:, e, :, :].rearrange("p a t -> p (a t)"), src, cst[0:m, n4:n4 + P], ALU.mult).then_inc(s_am, 1)
                nle = CCOLS["le"][0]
                for e in range(2):
                    for a in range(2):
                        own.inc(TTn(Rm[:, e, a, :, :], pbank(5 + e)[:, 2 * a * P:2 * a * P + 2 * P].rearrange("p (c t) -> p c t", t=P),
                                    bc(cst[:, nle + a * P:nle + (a + 1) * P].unsqueeze(1), [P, 2, P]), ALU.mult))
                own.wait()
                dve.memset(smallc[:, 39:40], 0.0).then_inc(s_rm, 1)
                for lev in range(LEVELS):
                    if lev == 0:
                        dve.wait_ge(s_X, j * LEVELS + 1)
                        idb = bc(ident.unsqueeze(1), [P, 4, P])
                        v4 = lambda a: a.rearrange("p e c t -> p (e c) t")
                        own.inc(TTn(v4(Tn[:, :, :, :]), idb, pbank(0).rearrange("p (a t) -> p a t", t=P), ALU.subtract))
                        own.inc(TTn(v4(TT[:, :, :, :]), idb, v4(ET[:, 0, :, :, :]), ALU.subtract))
                        ids = bc(ident[0:m, 0:m].unsqueeze(1), [m, 2, m])
                        own(TTn(Tns[:, :, :], ids, pbank(3)[0:m, 0:64].rearrange("p (e t) -> p e t", e=2), ALU.subtract))
                        TTn(TTs[:, :, :], ids, ETs[:, 0, :, :], ALU.subtract).then_inc(s_T, 1)
                    else:
                        dve.wait_ge(s_XT, j * (LEVELS - 1) + lev)
                        f = lambda a: a.rearrange("p e c t -> p (e c t)")
                        if lev < LEVELS - 1:
                            own.inc(TTn(f(Tn[:, :, :, :]), f(Tn[:, :, :, :]), pbank(1), ALU.subtract))
                        if lev == 1:
                            own.inc(TTn(TTs[:, :, :], TTs[:, :, :], pbank(3)[0:m, 128:192].rearrange("p (e t) -> p e t", e=2), ALU.subtract))
                        own.inc(TTn(f(TT[:, :, :, :]), f(TT[:, :, :, :]), pbank(2), ALU.subtract))
                        own.wait()
                        dve.memset(smallc[:, 38:39], 0.0).then_inc(s_T, 1)
                def blocks(dst, src):
                    seq = bc(c("seq", m).unsqueeze(2), [m, NB, HEAD_A])
                    for e in range(2):
                        i = TTn(dst[:, e, :, :], bc(src[:, e * HEAD_A:(e + 1) * HEAD_A].unsqueeze(1), [m, NB, HEAD_A]), seq, ALU.mult)
                    return i
                own(blocks(Vblk, VN[0:m, 2, :]))
                dve.wait_ge(s_y, 2 * j + 1)
                TS_(S1[:, :], pbank(4)[:, 0:HEAD_A], midc[:, 2:3], None, ALU.mult).then_inc(s_s1, 1)
                dve.wait_ge(s_s1, j + 1)
                dve.wait_ge(s_y, 2 * j + 2)
                own(TTn(SE[:, :], pbank(4)[:, HEAD_A:2 * HEAD_A], S1[:, :], ALU.add))
                TS_(SE[:, :], SE[:, :], v_pi[:, TP - 1:TP], None, ALU.mult).then_inc(s_se, 1)
                dve.wait_ge(s_use, j + 1)
                blocks(Ublk, Uss[:, :]).then_inc(s_blk, 1)
                dve.wait_ge(s_ss, j + 1)
                own(TTn(endS[:, :, :], pbank(1).rearrange("p (b v) -> p b v", b=NB), s0T[:, :, :], ALU.add))
                TTn(endS[:, :, :], endS[:, :, :], bc(samp(v_pi[:, TP:T])[:, :, TS - 1:TS], [P, NB, HEAD_A]), ALU.mult).then_inc(s_ses, 1)
                dve.wait_ge(s_ys, j + 1)
                dve.tensor_copy(v_thw[:, :], pbank(3)[:, 0:T]).then_inc(s_yc, 1)
                dve.wait_ge(s_gm, j + 1)
                own(STT(v_ld[:, :], pbank(7)[:, 0:T], -1.0 / HEAD_A, v_thw[:, :], ALU.mult, ALU.add))
                TTn(v_sq[:, :], v_ld[:, :], v_ld[:, :], ALU.mult).then_inc(s_gv, 1)
                dve.wait_ge(s_gr, j + 1)
                own(dve.reciprocal(v_px[:, :], v_px[:, :]))
                own(TTn(v_ld[:, :], v_ld[:, :], v_px[:, :], ALU.mult))
                own(TS_(v_ld[:, :], v_ld[:, :], pc("lnx_g", j), pc("lnx_b", j), ALU.mult, ALU.add))
                own(TTn(v_ld[:, :], v_ld[:, :], v_bon[:, :], ALU.add))
                TTn(v_thw[:, :], v_ld[:, :], v_g[:, :], ALU.mult).then_inc(s_ya, 1)
                dve.wait_ge(s_yah, j + 1)
                jc = bass.ds(j, 1)
                TTn(yalo[:, jc, :].rearrange("p o t -> p (o t)"), v_thw[:, :],
                    yahi[:, jc, :].rearrange("p o t -> p (o t)").bitcast(F32), ALU.subtract).then_inc(s_yal, 1)
            own.leave(KA)

            def qkv_evac(g):
                b4 = 4 * g.parity
                dve.wait_ge(s_mm, g.at(8, stages["qkv"][0] + 8))
                dve.tensor_copy(qkv[:, bass.ds(g.at(4), 4), :], ps[:, b4:b4 + 4, 0:T]).then_inc(s_evq, 1)

            plain("qkv", qkv_evac)
            dve.wait_ge(s_evq, 6)

            def fl(ap):
                return ap.rearrange("p o t -> p (o t)")

            with dve.Fori(0, HB) as h:
                own.enter(h, 16)
                q_, k_ = fl(qkv[:, bass.ds(h, 1), :]), fl(qkv[:, bass.ds(h + HB, 1), :])
                dve.wait_ge(s_rot, h + 1)
                own.inc(TTn(rtmp[:, 0, :], pbank(0)[:, 0:T], c("sin"), ALU.mult))
                own.inc(TTn(rtmp[:, 1, :], pbank(1)[:, 0:T], c("sin"), ALU.mult))
                own.inc(TTn(qr[:, :], q_, c("cos"), ALU.mult))
                own(TTn(kr[:, :], k_, c("cos"), ALU.mult))
                own.inc(TTn(qr[:, :], qr[:, :], rtmp[:, 0, :], ALU.add))
                own(TTn(kr[:, :], kr[:, :], rtmp[:, 1, :], ALU.add))
                dve.tensor_copy(fl(qs[:, bass.ds(h, 1), :]), qr[:, TP:T]).then_inc(s_rope, 1)
                dve.wait_ge(s_sc, h + 1)
                own.inc(STT(srow[:, 0, :], pbank(4)[:, 0:P], SCALE, c("causal"), ALU.mult, ALU.add))
                own.inc(TS_(srow[:, 1, :], pbank(5)[:, 0:P], SCALE, None, ALU.mult))
                own.inc(STT(srow[:, 2, :], pbank(5)[:, P:2 * P], SCALE, c("causal"), ALU.mult, ALU.add))
                own(dve.tensor_copy(STo[:, :, bass.ds(h, 1), :].rearrange("p b o t -> p b (o t)"), samp(pbank(7)[0:m, 0:m])))
                own(dve.tensor_reduce(sm[:, 0, 0:1], srow[:, 0, :], AX.X, ALU.max, negate=True))
                dve.tensor_reduce(sm[:, 0, 1:2], srow[:, 1:3, :], AX.XY, ALU.max, negate=True).then_inc(s_smx, 1)
                dve.wait_ge(s_pr, h + 1)
                own(dve.reciprocal(sm[:, 1, 2:4], sm[:, 1, 0:2]))
                own(TS_(prob[:, 0, :], prob[:, 0, :], sm[:, 1, 2:3], None, ALU.mult))
                TS_(prob[:, 1:3, :], prob[:, 1:3, :], sm[:, 1, 3:4], None, ALU.mult).then_inc(s_prn, 1)
                dve.wait_ge(s_o, h + 1)
                own(dve.tensor_copy(of[:, bass.ds(h, 1), 0:TP].rearrange("p o t -> p (o t)"), pbank(6)[:, 0:TP]))
                own(dve.memset(smallz[:, 0:1], 0.0))
                own(dve.memset(smallz[:, 0:1], 0.0))
                dve.memset(smallz[:, 1:2], 0.0).then_inc(s_evh, 1)
            own.leave(HB)

            dve.wait_ge(s_evh, HB)
            for g in range(2):
                with dve.Fori(0, 4) as bb:
                    with dve.Fori(0, 4) as ii:
                        for r in range(2):
                            n = bb * 8 + ii * 2
                            dve.wait_ge(s_kt, n + (32 * g + r + 1))
                            dve.wait_ge(s_ksc, n + max(32 * g + r - 1, 0))
                            dve.tensor_copy(kT[:, r, 0:4, :].rearrange("p h f -> p (h f)"), pbank(2 * r)).then_inc(s_kte, 1)
                            dve.wait_ge(s_ksc, n + (32 * g + r + 1))
                            dve.tensor_copy(ST[:, bass.ds(ii * 2 + r, 1), bass.ds(bb, 1), :].rearrange("p o a t -> p (o a t)"),
                                            pbank(4 + r)[:, 0:32]).then_inc(s_st, 1)
                dve.wait_ge(s_stt, g + 1)
                own.inc(TS_(srow2[:, 0:PAST], ps[:, 0:2, :].rearrange("p a t -> p (a t)"), SCALE, None, ALU.mult))
                own.inc(STT(srow2[:, PAST:], pbank(2)[:, 0:m], SCALE, c(f"own{g}"), ALU.mult, ALU.add))
                own.wait()
                blk = srow2[:, 0:PAST].rearrange("p (n k) -> p n k", n=NBLK)
                own(dve.tensor_reduce(smg[:, 4:8], blk, AX.X, ALU.add))
                own(dve.tensor_reduce(smg[:, 8:9], smg[:, 4:8], AX.X, ALU.min))
                own(TS_(smg[:, 12:16], smg[:, 4:8], smg[:, 8:9], None, ALU.is_equal))
                own(TS_(smg[:, 20:24], smg[:, 12:16], -1.0, 1.0, ALU.mult, ALU.add))
                own(dve.memset(smg[:, 19:20], 1.0))
                for n in (2, 1, 0):
                    own(TTn(smg[:, 16 + n:17 + n], smg[:, 17 + n:18 + n], smg[:, 21 + n:22 + n], ALU.mult))
                own(STT(smg[:, 24:28], smg[:, 12:16], NEG, smg[:, 16:20], ALU.mult, ALU.mult))
                own(TTn(blk, blk, bc(smg[:, 24:28].unsqueeze(2), [P, NBLK, BLK]), ALU.add))
                dve.tensor_reduce(smg[:, 0:1], srow2[:, :], AX.X, ALU.max, negate=True).then_inc(s_srow, 1)
                dve.wait_ge(s_pe2, g + 1)
                own(dve.reciprocal(smg[:, 2:3], smg[:, 1:2]))
                TS_(prob2[:, :], prob2[:, :], smg[:, 2:3], None, ALU.mult).then_inc(s_pn2, 1)
                dve.wait_ge(s_pt3, g + 1)
                own(dve.tensor_copy(PT2[:, 0:NPG, :], ps[:, 4:6, :].rearrange("p a (b t) -> p (a b) t", t=P)))
                dve.tensor_copy(PT2[0:m, NPG, :], pbank(6)[0:m, 0:P]).then_inc(s_p3e, 1)
                with dve.Fori(0, 4) as bb:
                    dve.wait_ge(s_pv, bb + (4 * g + 1))
                    dve.tensor_copy(of[:, :, bass.ds(bb * 4 + (TP + 16 * g), 4)], pbank(7)[:, 0:32].rearrange("p (h t) -> p h t", t=TS)).then_inc(s_pve, 1)
            dve.wait_ge(s_oh, 1)
            TTn(olo[:, :, :], of[:, :, :], ohi[:, :, :].bitcast(F32), ALU.subtract).then_inc(s_ol, 1)

            m0 = stages["merge"][0]
            own.base = own.base
            with dve.Fori(0, 4) as i:
                own.enter(i, 1)
                g = G(1, i, 0)
                for s in range(24):
                    lo("merge", g, s)
                    if s == 21:
                        dve.wait_ge(s_mm, g.at(24, m0 + 20))
                        dve.wait_ge(s_gate, g.at(2, 1))
                        TTn(sga[:, :, :], sga[:, :, :], ps[:, 0:4, 0:T], ALU.mult).then_inc(s_evm, 1)
                dve.wait_ge(s_mm, g.at(24, m0 + 24))
                dve.wait_ge(s_gate, g.at(2, 2))
                TTn(sgb[:, :, :], sgb[:, :, :], ps[:, 4:8, 0:T], ALU.mult).then_inc(s_evm, 1)
                dve.wait_ge(s_evm, g.at(2, 2))
                for q in range(4):
                    TTn(sga[:, q, :], sga[:, q, :], sgb[:, q, :], ALU.add).then_inc(s_mx, 1)
                for q in range(4):
                    dve.wait_ge(s_mh, g.at(4, q + 1))
                    qc = bass.ds(g.at(4, q), 1)
                    TTn(fl(mlo[:, qc, :]), sga[:, q, :], fl(mhi[:, qc, :]).bitcast(F32), ALU.subtract).then_inc(s_ml, 1)
                own(dve.memset(smallz[:, 2:3], 0.0))
            own.leave(4)

            def residual(name, gate, done):
                n0, ks, _ = stages[name]

                def evac(g):
                    b4 = 4 * g.parity
                    dve.wait_ge(s_mm, g.at(ks, n0 + ks))
                    for q in range(4):
                        kc = bass.ds(g.at(4, q), 1)
                        x = fl(xT[:, kc, :])
                        STT(x[:, 0:TP], ps[:, b4 + q, 0:TP], mod[:, bass.ds(g.at(4, gate + q), 1), 0], x[:, 0:TP], ALU.mult, ALU.add)
                        i = TTn(samp(rsd[:, q, :]), samp(ps[:, b4 + q, TP:T]),
                                bc(mod[:, bass.ds(g.at(4, gate + q), 1), 1:NC].rearrange("p o b -> p (o b)").unsqueeze(2), [P, NB, TS]), ALU.mult)
                    i.then_inc(s_rs, 1)
                    dve.wait_ge(s_rs, g.at(1, 1 + (4 if name == "down" else 0)))
                    k4 = bass.ds(g.at(4), 4)
                    TTn(xT[:, k4, TP:T], xT[:, k4, TP:T], rsd[:, :, :], ALU.add).then_inc(done, 1)
                plain(name, evac)

            residual("out", 32, s_ev_out)
            dve.wait_ge(s_ev_out, 4)
            norm(1, "norm2_g", 48, 64)
            own(dve.memset(ext[:, :, 0:2], 0.0))
            dve.memset(cv[:, :, EPAD - 2:], 0.0).then_inc(s_ezero, 1)

            w1, w2 = pcol("conv_w1"), pcol("conv_w2")

            def up_taps(g):
                for h in range(2):
                    dve.wait_ge(s_cv, g.at(2, h + 1))
                    STT(cv[:, h, 0:EPAD - 2], ext[:, h, 1:EPAD - 1], w1[:, bass.ds(g.at(2, h), 1)], cv[:, h, 0:EPAD - 2], ALU.mult, ALU.add).then_inc(s_cv2, 1)
                for h in range(2):
                    dve.wait_ge(s_cv2, g.at(2, h + 1))
                    STT(cv[:, h, 0:EPAD - 2], ext[:, h, 2:EPAD], w2[:, bass.ds(g.at(2, h), 1)], cv[:, h, 0:EPAD - 2], ALU.mult, ALU.add).then_inc(s_cv1, 1)

            def up_f(g):
                dve.wait_ge(s_gl, g.at(1, 1))
                b4 = 4 * g.parity
                TTn(ff[:, :, :], gl[:, :, :], ps[:, b4 + 2:b4 + 4, 0:T], ALU.mult).then_inc(s_f, 1)

            def up_lo(g):
                dve.wait_ge(s_fh, g.at(1, 1))
                TTn(flo[:, bass.ds(g.at(2), 2), :], ff[:, :, :], fhi[:, bass.ds(g.at(2), 2), :].bitcast(F32), ALU.subtract).then_inc(s_fl, 1)

            def up_group(g):
                for s in range(8):
                    lo("up", g, s)
                    if not g.first and s in (2, 4, 6):
                        (up_taps if s == 2 else up_f if s == 4 else up_lo)(g.prev())

            last = over(dve, 22, up_group)
            up_taps(last)
            up_f(last)
            up_lo(last)
            residual("down", 80, s_evd)
            dve.wait_ge(s_evd, 4)
            norm(2, "normf_g", 0, 0)
            for b in range(11):
                dve.wait_ge(s_nct, b + 1)
                dve.tensor_copy(ncn[:, b * 512:(b + 1) * 512], pbank(b % 8)[0:2 + 2 * NB, :]).then_inc(s_ncn, 1)
            for b in range(12):
                mt, q = b // 4, b % 4
                w = M_ROWS[mt]
                dve.wait_ge(s_yt, b + 1)
                dve.tensor_copy(ynat[0:w, mt, q * 512:(q + 1) * 512], pbank((b + 11) % 8)[0:w, :]).then_inc(s_yev, 1)

        @block.tensor
        def _(pe):
            m = NB * TS

            def mm(out, lhsT, rhs, start=True, stop=True, **k):
                return pe.matmul(out, lhsT, rhs, start=start, stop=stop, **k)

            def carry_wait():
                pe.sem_inc(s_carry, 1)

            pe.wait_ge(s_cst, 16)
            pe.wait_ge(s_dve, 2)
            for bi, (kind, at_) in enumerate(banks):
                dst = pbank(bi % 8)
                if bi >= 8:
                    pe.wait_ge(s_tev, bi - 8 if bi - 8 > 1 else 1)
                    if bi == 9:
                        pe.wait_ge(s_silu, 1)
                if kind == "par":
                    pe.wait_ge(s_par, 16 * (len(PARAM_ROWS) + 1))
                    for t in range(4):
                        i = pe.transpose(dst[:, t * P:(t + 1) * P], prow[:, t, :], ident)
                elif kind == "c":
                    pe.wait_ge(s_c, 32)
                    for k in range(KD):
                        i = pe.transpose(dst[:, k * NC:(k + 1) * NC], cnat[:, k * P:(k + 1) * P], ident[0:NC, 0:NC])
                elif kind == "sh":
                    pe.wait_ge(s_sh, 32)
                    for k in range(ZT):
                        i = pe.transpose(dst[:, k * NB:(k + 1) * NB], shnat[:, k * P:(k + 1) * P], ident[0:NB, 0:NB])
                elif kind == "x":
                    mt, q = at_
                    w = M_ROWS[mt]
                    if mt == 0 and q == 0:
                        pe.wait_ge(s_x, 48)
                    for t in range(4):
                        k = 4 * q + t
                        i = pe.transpose(dst[:, t * P:t * P + w], xnat[0:w, mt, k * P:(k + 1) * P], ident[0:w, 0:w])
                else:
                    for t in range(22):
                        k = 22 * at_ + t
                        i = pe.transpose(dst[:, t * 2 * NB:(t + 1) * 2 * NB], cvnat[:, k * P:(k + 1) * P], ident[0:2 * NB, 0:2 * NB])
                i.then_inc(s_tp, 1)

            pe.wait_ge(s_tev, len(banks) - 1)
            pe.wait_ge(s_silu, 1)

            def ada_group(g):
                b4 = 4 * g.parity
                if not (g.i is None and g.c < 1):
                    pe.wait_ge(s_adaev, g.at(1, -1))
                for s in range(ADA_K):
                    pe.wait_ge(s_raw[s % 4], g.at(ADA_K * 4, 16 * (s // 4 + 1)))
                    for kt in range(2):
                        for q in range(4):
                            i = mm(ps[:, b4 + q, 0:NC], raw[:, s % 4, kt, q * P:(q + 1) * P], scT[:, 2 * s + kt, :],
                                   s == 0 and kt == 0, s == ADA_K - 1 and kt == 1)
                    i.then_inc(s_ada, 1)

            over(pe, ADA_G, ada_group)
            pe.wait_ge(s_adaev, ADA_G)

            def norm(u):
                for k in range(KD):
                    if k % 4 == 0:
                        pe.wait_ge(s_sq, 4 * u + k // 4 + 1)
                    i = mm(pbank(0)[:, 0:T], c("mean"), sq[:, k, :], k == 0, k == KD - 1)
                i.then_inc(s_ssq, 1)

            def products(name, g, s0, ks, b4, hi_, lo_, nt=4, off=0):
                n0, per, _ = stages[name]
                for s in range(ks):
                    n = n0 + per * g.c + s0 + s
                    pe.wait_ge(s_lo, g.at(per, n0 + s0 + s + 1))
                    for kt in range(2):
                        k = 2 * s + kt
                        for q in range(nt):
                            w = slice(q * P, (q + 1) * P)
                            out = ps[:, b4 + q, 0:T]
                            mm(out, whi[:, n % 2, kt, w], hi_[:, k, :], k == 0, False)
                            mm(out, whi[:, n % 2, kt, w], lo_[:, k, :], False, False)
                            i = mm(out, wlo[:, n % 2, kt, w], hi_[:, k, :], False, k == 2 * ks - 1)
                    i.then_inc(s_mm, 1)

            def stage(name, hi_, lo_, done, base=0, before=None):
                _, ks, ng = stages[name]

                def group(g):
                    if not g.first:
                        if not (g.i is None and g.c < 2):
                            pe.wait_ge(done, g.at(1, base - 1))
                    products(name, g, 0, ks, 4 * g.parity, hi_, lo_, 3 if name == "za" and g.i is None and g.c == 6 else 4)
                over(pe, ng, group)
                pe.wait_ge(done, base + ng)

            norm(0)
            pe.wait_ge(s_hlo, 4)
            stage("za", hhi, hlo, s_evz)
            pe.wait_ge(s_nsh, 1)
            for b in range(7):
                for k in range(4 * b, min(4 * b + 4, ZT)):
                    i = pe.transpose(pbank(b)[0:NC, (k % 4) * P:(k % 4 + 1) * P], nsh[:, k, :], ident)
                i.then_inc(s_nst, 1)
            pe.wait_ge(s_nse, 7)
            pe.wait_ge(s_lin2, 1)

            with pe.Fori(0, KA) as j:
                pe.wait_ge(s_yal, j)
                pe.wait_ge(s_stp, j)
                pe.wait_ge(s_sto, 2 * j)
                pe.wait_ge(s_lora, j * 64 + 64)
                mm(pbank(0)[:, 0:T], lora[0:LORA_W, 0, :], lw[0:LORA_W, :])
                mm(pbank(1)[:, 0:T], lora[LORA_W:P, 0, :], lw[LORA_W:P, :])
                mm(pbank(2)[:, 0:T], lora[:, 1, :], lsg[:, 0, :], True, False)
                mm(pbank(2)[:, 0:T], lora[0:LORA_G - P, 2, :], lsg[0:LORA_G - P, 1, :], False, True).then_inc(s_lmm, 1)
                pe.wait_ge(s_kkq, j + 1)
                mm(pbank(3)[:, 0:T], c("head"), v_sq[:, :]).then_inc(s_kkp, 1)
                pe.wait_ge(s_ld, j + 1)
                pe.transpose(pbank(4)[:, 0:P], v_ld[:, 0:P], ident)
                pe.transpose(pbank(4)[:, P:2 * P], v_ld[:, P:2 * P], ident)
                pe.transpose(pbank(4)[0:m, 2 * P:3 * P], v_ld[:, TP:T], ident).then_inc(s_ldt, 1)
                pe.wait_ge(s_ldn, j + 1)
                for b, cum, cum4 in ((5, "cumx", "lt4"), (6, "cumi", "le4")):
                    for ck in range(2):
                        mm(pbank(b)[:, ck * P:(ck + 1) * P], ldn[:, ck, :], c(cum))
                    i = mm(pbank(b)[:, TP:T], ldn[0:m, 2, :], c(cum4, m))
                i.then_inc(s_cum, 1)
                pe.wait_ge(s_rkk, j + 1)
                mm(pbank(7)[:, 0:T], c("head"), v_sq[:, :]).then_inc(s_bon, 1)
                pe.wait_ge(s_dec, j + 1)
                v_ = rkv[:, 2, :]
                for ck in range(2):
                    pe.transpose(pbank(0)[:, ck * P:(ck + 1) * P], v_[:, ck * P:(ck + 1) * P], ident)
                    pe.transpose(pbank(0)[:, (2 + ck) * P:(3 + ck) * P], v_k[:, ck * P:(ck + 1) * P], ident)
                    pe.transpose(pbank(1)[:, ck * P:(ck + 1) * P], v_b[:, ck * P:(ck + 1) * P], ident)
                for q, a in enumerate((v_, v_k[:, :], v_b[:, :])):
                    i = pe.transpose(pbank(4)[0:m, q * P:(q + 1) * P], a[:, TP:T], ident)
                i.then_inc(s_tr, 1)
                pe.wait_ge(s_kkr, j + 1)
                pe.wait_ge(s_bonv, j + 1)
                r_ = rkv[:, 0, :]
                carry_wait()
                for e in range(2):
                    f = slice(64 * e, 64 * e + 64)
                    for b, right in ((2 + e, v_kk), (5 + e, r_)):
                        for a, left in enumerate((v_k, v_b)):
                            for ck in range(2):
                                t = slice(ck * P, (ck + 1) * P)
                                mm(pbank(b)[:, (2 * a + ck) * P:(2 * a + ck + 1) * P], left[f, t], right[f, t])
                pe.wait_ge(s_vkb, j + 1)
                carry_wait()
                for e in range(2):
                    f = slice(64 * e, 64 * e + 64)
                    dst = pbank(7)[0:m, 0:P] if e == 0 else pbank(4)[0:m, 3 * P:4 * P]
                    for a, (left, right) in enumerate(((v_k, v_kk), (v_b, v_kk), (v_k, r_), (v_b, r_))):
                        i = mm(dst[:, 32 * a:32 * a + 32], left[f, TP:T], right[f, TP:T])
                i.then_inc(s_mat, 1)
                for lev in range(LEVELS):
                    pe.wait_ge(s_et, j * LEVELS + lev + 1)
                    if lev:
                        pe.wait_ge(s_T, j * LEVELS + lev)
                    b = lev % 2
                    for e in range(2):
                        for ck in range(2):
                            p = 2 * e + ck
                            i = mm(pbank(0)[:, p * P:(p + 1) * P], ET[:, b, e, ck, :], Tn[:, e, ck, :] if lev else ident)
                        if lev < 2:
                            i = mm(pbank(3)[0:m, 32 * e:32 * e + 32], ETs[:, lev, e, :], Tns[:, e, :] if lev else ident[0:m, 0:m])
                    i.then_inc(s_X, 1)
                    if not lev:
                        continue
                    pe.wait_ge(s_Xe, j * (LEVELS - 1) + lev)
                    for e in range(2):
                        for ck in range(2):
                            p = 2 * e + ck
                            if lev < LEVELS - 1:
                                mm(pbank(1)[:, p * P:(p + 1) * P], TT[:, e, ck, :], Xs[:, e, ck, :])
                            i = mm(pbank(2)[:, p * P:(p + 1) * P], Xs[:, e, ck, :], TT[:, e, ck, :])
                        if lev == 1:
                            i = mm(pbank(3)[0:m, 128 + 32 * e:160 + 32 * e], Xss[:, e, :], TTs[:, e, :])
                    i.then_inc(s_XT, 1)
                pe.wait_ge(s_s0, j * (16 * NB) + 16 * NB)
                pe.wait_ge(s_T, j * LEVELS + LEVELS)
                carry_wait()
                for b in range(NB):
                    i = pe.transpose(pbank(2)[:, b * 64:b * 64 + 64], s0n[:, b, :, :].rearrange("p h k -> p (h k)"), ident[0:64, 0:64])
                i.then_inc(s_s0t, 1)
                pe.wait_ge(s_rm, j + 1)
                E = [slice(0, 64), slice(64, P)]
                for ck in range(2):
                    t = slice(ck * P, (ck + 1) * P)
                    if ck:
                        pe.wait_ge(s_s1, j + 1)
                    for e in range(2):
                        dst = pbank(5)[:, E[e]] if ck == 0 else pbank(5 + e)[:, 0:64]
                        i = mm(dst, Am[:, e, 0, ck, :], VN[:, ck, E[e]], True, ck == 0)
                        if ck:
                            i = mm(dst, v_kk[E[e], t], S1[E[e], :], False, True)
                    i.then_inc(s_m, 1)
                    pe.wait_ge(s_me, 2 * j + ck + 1)
                    carry_wait()
                    for e in range(2):
                        i = mm(pbank(7)[:, E[e]], TT[:, e, ck, :], Ms[:, E[e]])
                    i.then_inc(s_u, 1)
                    pe.wait_ge(s_ue, 2 * j + ck + 1)
                    for e in range(2):
                        y = pbank(3)[E[e], t]
                        mm(y, VN[:, ck, E[e]], Rm[:, e, 0, ck, :], True, False)
                        mm(y, Us[:, E[e]], Rm[:, e, 1, ck, :], False, ck == 0)
                        if ck:
                            mm(y, S1[E[e], :], r_[E[e], t], False, True)
                        st = pbank(4)[E[e], ck * 64:ck * 64 + 64]
                        mm(st, KN[:, ck, E[e]], VN[:, ck, E[e]], True, False)
                        i = mm(st, BN[:, ck, E[e]], Us[:, E[e]], False, True)
                    i.then_inc(s_y, 1)
                pe.wait_ge(s_s0e, j + 1)
                carry_wait()
                for e in range(2):
                    mt = pbank(5 + e)[E[e], P:P + m]
                    for b in range(NB):
                        mm(mt[:, 4 * b:4 * b + 4], s0T[E[e], b, :], v_kk[E[e], TP + 4 * b:TP + 4 * b + 4], b == 0, False,
                           skip_group_check=True)
                    i = mm(mt, VN[0:m, 2, E[e]], As[:, e, 0, :], False, True, skip_group_check=True)
                i.then_inc(s_mt, 1)
                pe.wait_ge(s_mte, j + 1)
                pe.transpose(pbank(0)[0:m, 0:P], MTs[:, :], ident).then_inc(s_mst, 1)
                pe.wait_ge(s_mse, j + 1)
                carry_wait()
                for e in range(2):
                    i = mm(pbank(7)[0:m, 2 * P + 64 * e:2 * P + 64 * e + 64], TTs[:, e, :], Mss[:, E[e]])
                i.then_inc(s_us, 1)
                pe.wait_ge(s_use, j + 1)
                carry_wait()
                for e in range(2):
                    y = pbank(3)[E[e], TP:T]
                    for b in range(NB):
                        mm(y[:, 4 * b:4 * b + 4], s0T[E[e], b, :], r_[E[e], TP + 4 * b:TP + 4 * b + 4], b == 0, False,
                           skip_group_check=True)
                    mm(y, VN[0:m, 2, E[e]], As[:, e, 2, :], False, False, skip_group_check=True)
                    i = mm(y, Uss[:, E[e]], As[:, e, 3, :], False, True, skip_group_check=True)
                i.then_inc(s_ys, 1)
                pe.wait_ge(s_se, j + 1)
                carry_wait()
                pe.transpose(pbank(2)[0:64, 0:P], SE[:, :], ident).then_inc(s_set, 1)
                pe.wait_ge(s_blk, j + 1)
                for e in range(2):
                    st = pbank(1)[E[e], :]
                    mm(st, KN[0:m, 2, E[e]], Vblk[:, e, :, :].rearrange("p b v -> p (b v)"), True, False)
                    i = mm(st, BN[0:m, 2, E[e]], Ublk[:, e, :, :].rearrange("p b v -> p (b v)"), False, True)
                i.then_inc(s_ss, 1)
                pe.wait_ge(s_ses, j + 1)
                carry_wait()
                for b in range(NB):
                    i = pe.transpose(pbank(5 + b // 4)[0:64, (b % 4) * P:(b % 4 + 1) * P], endS[:, b, :], ident)
                    if b % 4 == 3:
                        i.then_inc(s_sst, 1)
                pe.wait_ge(s_yc, j + 1)
                mm(pbank(7)[:, 0:T], c("head"), v_thw[:, :]).then_inc(s_gm, 1)
                pe.wait_ge(s_gv, j + 1)
                mm(pbank(7)[:, 0:T], c("head"), v_sq[:, :]).then_inc(s_gq, 1)

            pe.wait_ge(s_yal, KA)
            pe.wait_ge(s_sto, 2 * KA)
            pe.wait_ge(s_stp, KA)
            stage("qkv", hhi, hlo, s_evq)

            with pe.Fori(0, HB) as h:
                pe.wait_ge(s_evh, h)
                pe.wait_ge(s_vnh, h)
                fl = lambda a: a.rearrange("p o t -> p (o t)")
                mm(pbank(0)[:, 0:T], c("rot"), fl(qkv[:, bass.ds(h, 1), :]))
                mm(pbank(1)[:, 0:T], c("rot"), fl(qkv[:, bass.ds(h + HB, 1), :])).then_inc(s_rot, 1)
                pe.wait_ge(s_rope, h + 1)
                pe.wait_ge(s_vt, h + 1)
                for b, a in ((2, kr), (3, vT)):
                    pe.transpose(pbank(b)[:, 0:P], a[:, 0:P], ident)
                    pe.transpose(pbank(b)[:, P:2 * P], a[:, P:2 * P], ident)
                    i = pe.transpose(pbank(b)[0:m, 2 * P:3 * P], a[:, TP:T], ident)
                i.then_inc(s_kvt, 1)
                mm(pbank(4)[:, 0:P], qr[:, 0:P], kr[:, 0:P])
                mm(pbank(5)[:, 0:TP], qr[:, P:TP], kr[:, 0:TP])
                mm(pbank(7)[0:m, 0:m], kr[:, TP:T], qr[:, TP:T]).then_inc(s_sc, 1)
                pe.wait_ge(s_prn, h + 1)
                for q in range(3):
                    i = pe.transpose(pbank(6)[:, q * P:(q + 1) * P], prob[:, q, :], ident)
                i.then_inc(s_prt, 1)
                pe.wait_ge(s_pt2, h + 1)
                pe.wait_ge(s_vnh, h + 1)
                mm(pbank(6)[:, 0:P], vnh[:, 0, :], pT[:, 0, :])
                mm(pbank(6)[:, P:TP], vnh[:, 0, :], pT[:, 1, :], True, False)
                mm(pbank(6)[:, P:TP], vnh[:, 1, :], pT[:, 2, :], False, True).then_inc(s_o, 1)

            pe.wait_ge(s_evh, HB)
            for g in range(2):
                with pe.Fori(0, 4) as bb:
                    with pe.Fori(0, 4) as ii:
                        for r in range(2):
                            n = bb * 8 + ii * 2
                            pe.wait_ge(s_page[r], (bb * 4 + ii) * 16 + 16 * (32 * g + 1))
                            pe.wait_ge(s_kte, n + 32 * g)
                            pe.wait_ge(s_kta, n + 32 * g)
                            for h in range(HB):
                                i = pe.transpose(pbank(2 * r + h // 4)[:, (h % 4) * P:(h % 4 + 1) * P], kpage[:, r, h * P:(h + 1) * P], ident)
                            i.then_inc(s_kt, 1)
                            pe.wait_ge(s_kte, n + (32 * g + r + 1))
                            pe.wait_ge(s_kta, n + (32 * g + r + 1))
                            pe.wait_ge(s_st, n + 32 * g)
                            for h in range(HB):
                                i = mm(pbank(4 + r)[:, 4 * h:4 * h + 4], kT[:, r, h, :], qs[:, h, bass.ds(bb * 4 + 16 * g, 4)])
                            i.then_inc(s_ksc, 1)
                pe.wait_ge(s_st, 32 * (g + 1))
                for p in range(NPG):
                    pe.transpose(pbank(p // 4)[:, (p % 4) * P:(p % 4 + 1) * P], ST[:, p, :, :].rearrange("p a t -> p (a t)"), ident)
                pe.transpose(pbank(2)[:, 0:m], STo[:, 4 * g:4 * g + 4, :, :].rearrange("p b h t -> p (b h t)"), ident[0:m, 0:m]).then_inc(s_stt, 1)
                pe.wait_ge(s_pn2, g + 1)
                for p in range(NPG):
                    pe.transpose(pbank(4 + p // 4)[:, (p % 4) * P:(p % 4 + 1) * P], prob2[:, p * P:(p + 1) * P], ident)
                pe.transpose(pbank(6)[0:m, 0:P], prob2[:, PAST:], ident).then_inc(s_pt3, 1)
                pe.wait_ge(s_p3e, g + 1)
                with pe.Fori(0, 4) as bb:
                    pe.wait_ge(s_pve, bb + 4 * g)
                    for p in range(NPG):
                        r = p % 2
                        pe.wait_ge(s_page[r], bb * 64 + 16 * (32 * g + 16 + p // 2 + 1))
                        for h in range(HB):
                            i = mm(pbank(7)[:, 4 * h:4 * h + 4], kpage[:, r, h * P:(h + 1) * P], PT2[:, p, bass.ds(bb * 32 + 4 * h, 4)],
                                   p == 0 and h == 0, False, skip_group_check=True)
                        i.then_inc(s_pvu, 1)
                    for h in range(HB):
                        i = mm(pbank(7)[:, 4 * h:4 * h + 4], vns[:, h, :], PT2[0:m, NPG, bass.ds(bb * 32 + 4 * h, 4)], False, True,
                               skip_group_check=True)
                    i.then_inc(s_pv, 1)

            pe.wait_ge(s_pve, 8)
            pe.wait_ge(s_ol, 1)
            with pe.Fori(0, 4) as i:
                g = G(1, i, 0)
                pe.wait_ge(s_evm, g.at(2))
                products("merge", g, 0, 8, 0, hhi, hlo)
                products("merge", g, 8, 8, 4, hhi, hlo)
                pe.wait_ge(s_gate, g.at(2, 1))
                products("merge", g, 16, 4, 0, yahi, yalo)
                pe.wait_ge(s_gate, g.at(2, 2))
                products("merge", g, 20, 4, 4, ohi, olo)
            pe.wait_ge(s_evm, 8)
            pe.wait_ge(s_ml, 16)
            stage("out", mhi, mlo, s_ev_out)
            norm(1)
            pe.wait_ge(s_hlo, 8)
            stage("up", hhi, hlo, s_f)
            pe.wait_ge(s_fl, 22)
            stage("down", fhi, flo, s_evd)
            norm(2)
            pe.wait_ge(s_ncv, 22)
            pe.wait_ge(s_rms, 3)
            for b in range(11):
                if b >= 8:
                    pe.wait_ge(s_ncn, b - 7)
                for q in range(4):
                    i = pe.transpose(pbank(b % 8)[0:2 + 2 * NB, q * P:(q + 1) * P], newconv[:, 4 * b + q, :], ident)
                i.then_inc(s_nct, 1)
            for b in range(12):
                mt, q = b // 4, b % 4
                w = M_ROWS[mt]
                pe.wait_ge(s_hn, 8 + q + 1)
                pe.wait_ge(s_ncn, min(b + 4, 11))
                if b + 4 > 11:
                    pe.wait_ge(s_yev, b - 7)
                for t in range(4):
                    i = pe.transpose(pbank((b + 11) % 8)[0:w, t * P:(t + 1) * P], sq[:, 4 * q + t, mt * P:mt * P + w], ident)
                i.then_inc(s_yt, 1)


_INS = ['x_prompt', 'x_sample', 'cache_k', 'cache_v', 'state_wkv', 'state_shift', 'state_conv', 'page_table',
        'c_prompt', 'c_sample', 'w_ada', 'b_ada', 'norm1_g', 'w_in', 'mu_shift', 'rwkv_w0', 'rwkv_w2', 'rwkv_a0',
        'rwkv_a2', 'rwkv_g2', 'rwkv_kk', 'rwkv_ka', 'rwkv_rk', 'lnx_g', 'lnx_b', 'w_proj_a', 'w_proj_b', 'w_out',
        'norm2_g', 'w_up', 'conv_w', 'conv_b', 'w_down', 'normf_g']
_OUTS = [("y_prompt", (1, TP, D)), ("y_sample", (NB, TS, D)), ("k_prompt", (1, TP, HB, HEAD_B)),
         ("v_prompt", (1, TP, HB, HEAD_B)), ("wkv_prompt", (1, HA, HEAD_A, HEAD_A)), ("shift_prompt", (1, ZA)),
         ("conv_prompt", (1, 2, FF)), ("k_sample", (NB, TS, HB, HEAD_B)), ("v_sample", (NB, TS, HB, HEAD_B)),
         ("wkv_sample", (NB, HA, HEAD_A, HEAD_A)), ("shift_sample", (NB, ZA)), ("conv_sample", (NB, 2, FF))]


def kernel(**inputs):
    import concourse.bacc as _bacc
    from concourse.bass_utils import run_bass_kernel_spmd as _run

    nc = _bacc.Bacc("TRN2", target_bir_lowering=False, num_devices=1)
    arrays, d = {}, {}
    for name in _INS:
        a = np.ascontiguousarray(inputs[name])
        arrays[f"in_{name}"] = a
        d[name] = nc.dram_tensor(f"in_{name}", a.shape, mybir.dt.from_np(a.dtype), kind="ExternalInput").ap()
    consts, _cols = shape_constants()
    arrays["in_consts"] = consts
    d["consts"] = nc.dram_tensor("in_consts", consts.shape, F32, kind="ExternalInput").ap()
    for name, shape in _OUTS:
        d[name] = nc.dram_tensor(f"out_{name}", shape, F32, kind="ExternalOutput").ap()
    build(nc, d)
    r = _run(nc, [arrays], core_ids=[0])
    return tuple(r.results[0][f"out_{name}"] for name, _shape in _OUTS)
```

```python
from contextlib import ExitStack

import concourse.bass as bass
import numpy as np
from concourse import mybir

ALU = mybir.AluOpType
ACT = mybir.ActivationFunctionType
AX = mybir.AxisListType
F32 = mybir.dt.float32
F32R = mybir.dt.float32r
I32 = mybir.dt.int32

P = 128
D = 2048
KD = D // P
TP, NB, TS = 256, 8, 4
T = TP + NB * TS
NC = NB + 1
DA, HA, HEAD_A = 1024, 16, 64
DB, HB, HEAD_B = 1024, 8, 128
KA = DA // P
LORA_W, LORA_A, LORA_G = 64, 64, 160
ZA = 3 * DA + LORA_W + LORA_A + LORA_G
ZT = -(-ZA // P)
ZPAD = 1 + TP + NB * (TS + 1)
FF = 5632
KF = FF // P
PAST, PAGE = 1024, 128
NPG = PAST // PAGE
NBLK, BLK = 4, 256
ROW = PAST + NB * TS
EPAD = 2 + TP + NB * (TS + 2)
RMS_EPS, LNX_EPS, NEG = 1e-6, 64e-5, -1e30
DECAY = float(np.exp(-0.5))
SCALE = HEAD_B ** -0.5
CH = 512
LEVELS = 7


def shape_constants():
    cols, parts, n = {}, [], 0

    def add(name, a):
        nonlocal n
        full = np.zeros((P, a.shape[1]), np.float32)
        full[:a.shape[0]] = a
        cols[name] = (n, a.shape[1])
        parts.append(full)
        n += a.shape[1]

    s, t = np.arange(P)[:, None], np.arange(P)[None, :]
    add("ident", (s == t) * 1.0)
    add("mean", np.full((P, P), 1.0 / D))
    add("head", (s // HEAD_A == t // HEAD_A) * 1.0)
    add("rot", np.where(s == t + 64, -1.0, 0.0) + np.where(s == t - 64, 1.0, 0.0))
    add("lt", (s < t) * 1.0)
    add("le", (s <= t) * 1.0)
    add("nle", (s <= t) * -1.0)
    add("cumx", (s < t) * 1.0 - (s < 64))
    add("cumi", (s <= t) * 1.0 - (s < 64))
    for lev in range(LEVELS):
        b = 1 << lev
        add(f"lev{lev}", ((s // (2 * b) == t // (2 * b)) & ((s // b) % 2 == 0) & ((t // b) % 2 == 1)) * 1.0)
    s4, t4 = np.arange(NB * TS)[:, None], np.arange(NB * TS)[None, :]
    same = s4 // TS == t4 // TS
    add("lt4", (same & (s4 < t4)) * 1.0)
    add("lt4b", (same & (s4 < t4)) * 1.0)
    add("le4", (same & (s4 <= t4)) * 1.0)
    add("nle4", (same & (s4 <= t4)) * -1.0)
    add("seq", (s4 // TS == np.arange(NB)[None, :]) * 1.0)
    add("causal", np.where(t <= s, 0.0, NEG))
    add("own", np.where(same & (s4 <= t4), 0.0, NEG))
    half = HEAD_B // 2
    inv = np.float32(10000.0) ** (-np.arange(half, dtype=np.float32) / np.float32(half))
    pos = np.concatenate([np.arange(TP), np.tile(PAST + np.arange(TS), NB)]).astype(np.float32)
    ang = np.concatenate([inv, inv])[:, None].astype(np.float32) * pos[None, :]
    add("cos", np.cos(ang))
    add("sin", np.sin(ang))
    add("eps_rms", np.full((P, 1), RMS_EPS))
    add("eps_lnx", np.full((P, 1), LNX_EPS))
    return np.concatenate(parts, axis=1).astype(np.float32), cols


_, CCOLS = shape_constants()
NCONST = sum(w for _, w in CCOLS.values())

PARAM_ROWS = {
    "b_ada": (0, 0, 96), "norm1_g": (0, 96, 16), "norm2_g": (0, 112, 16),
    "normf_g": (1, 0, 16), "rwkv_w0": (1, 16, 8), "rwkv_a0": (1, 24, 8), "rwkv_kk": (1, 32, 8),
    "rwkv_ka": (1, 40, 8), "rwkv_rk": (1, 48, 8), "lnx_g": (1, 56, 8), "lnx_b": (1, 64, 8),
    "mu_shift": (1, 72, ZT), "conv_b": (2, 0, KF), "conv_w0": (2, 44, KF), "conv_w1": (3, 0, KF),
    "conv_w2": (3, 44, KF),
}


def build(nc, d):
    ctx = ExitStack()
    with ctx:
        def sem(name):
            return ctx.enter_context(nc.semaphore(name))

        base = -(-nc.sbuf_base // 32) * 32

        def at(name, shape, off, dt=F32):
            return nc.alloc_sbuf_tensor_at(name, shape, dt, offset=base + off)

        def size(*shape):
            n = 4
            for x in shape:
                n *= x
            return -(-n // 32) * 32

        o = 0
        cst = at("cst", [P, NCONST], o); o_cst = o; o += size(NCONST)
        par = at("par", [P, 4, P], o); o += size(4 * P)
        mod = at("mod", [P, 96, NC], o); o += size(96 * NC)
        xT = at("xT", [P, KD, T], o); o += size(KD * T)
        sconvT = at("sconvT", [P, KF, 2 * NB], o); o += size(KF * 2 * NB)
        newconv = at("newconv", [P, KF, 2 + 2 * NB], o); o += size(KF * (2 + 2 * NB))
        o_ring = o
        raw = at("raw", [P, 4, 2, CH], o); o += size(4 * 2 * CH)
        whi = at("whi", [P, 2, 2, CH], o, F32R); o += size(2 * 2 * CH)
        wlo = at("wlo", [P, 2, 2, CH], o, F32R); o += size(2 * 2 * CH)
        kpage = at("kpage", [P, NPG, HB * P], o_ring)
        assert size(NPG * HB * P) == o - o_ring
        za_ = o
        hhi = at("hhi", [P, KD, T], za_, F32R)
        hlo = at("hlo", [P, KD, T], za_ + size(KD * T), F32R)
        o += 2 * size(KD * T)
        zb = o
        o += 2 * size(KF * T)
        assert base + o <= nc.sbuf_usable_end, (base + o, nc.sbuf_usable_end)

        def c(name, rows=P):
            n, w = CCOLS[name]
            return cst[0:rows, n:n + w]

        def pcol(name):
            t, r, n = PARAM_ROWS[name]
            return par[:, t, r:r + n]

        ident = c("ident")

        zz = zb + size(ZT * ZPAD)
        za = at("za", [P, ZT, ZPAD], zb)
        xnat = at("xnat", [P, 3, D], zz)
        prow = at("prow", [P, 4, P], zz + size(3 * D))
        cnat = at("cnat", [NC, D], zz + size(3 * D) + 2048)
        shnat = at("shnat", [NB, ZT * P], za_)
        cvnat = at("cvnat", [2 * NB, FF], za_ + size(ZT * P))
        adr = at("adr", [NC, CH], zb + 96256)
        scT = at("scT", [P, KD, NC], zb + 98304)
        o_n = zb + 57344
        sq = at("sq", [P, KD, T], o_n)
        gsc = at("gsc", [P, KD, NC], o_n + size(KD * T))
        rms = at("rms", [P, T], o_n + size(KD * T) + size(KD * NC))
        rstd = at("rstd", [P, T], o_n + size(KD * T) + size(KD * NC) + size(T))
        nsh = at("nsh", [P, ZT, NC], o_n + size(KD * T) + size(KD * NC) + 2 * size(T))
        nshn = at("nshn", [NC, ZT * P], o_ring + size(4 * 2 * CH))
        assert ZT * P <= 8 * CH

        yahi = at("yahi", [P, KA, T], zb, F32R)
        yalo = at("yalo", [P, KA, T], zb + 4 * KA * ZPAD, F32R)
        o_h = zb + 2 * 4 * KA * ZPAD
        o_w = zz
        o = zz
        top = zb + 96256

        def nxt(name, shape, dt=F32):
            nonlocal o
            n = 1
            for x in shape[1:]:
                n *= x
            r = at(name, shape, o, dt)
            o += size(n)
            assert o <= top, name
            return r

        lw = nxt("lw", [P, T])
        lsg = nxt("lsg", [P, 2, T])
        lora = nxt("lora", [P, 3, P])
        s0n = nxt("s0n", [HEAD_A, NB, 2, HEAD_A])
        s0T = nxt("s0T", [P, NB, HEAD_A])
        o_dif = o
        dif = nxt("dif", [P, 3, ZPAD])
        endS = at("endS", [P, NB, HEAD_A], o_dif)
        rkv = nxt("rkv", [P, 3, T])
        v_thw = nxt("v_thw", [P, T])
        v_tha = nxt("v_tha", [P, T])
        v_g = nxt("v_g", [P, T])
        v_ld = nxt("v_ld", [P, T])
        v_px = nxt("v_px", [P, T])
        v_pi = nxt("v_pi", [P, T])
        v_pv = nxt("v_pv", [P, T])
        v_kk = nxt("v_kk", [P, T])
        v_sq = nxt("v_sq", [P, T])
        v_k = nxt("v_k", [P, T])
        v_b = nxt("v_b", [P, T])
        v_bon = nxt("v_bon", [P, T])
        ldn = nxt("ldn", [P, 3, P])
        smallc = nxt("smallc", [P, 40])
        midc = nxt("midc", [P, 4])
        Am = nxt("Am", [P, 2, 2, 2, P])
        o_rm = o
        Rm = nxt("Rm", [P, 2, 2, 2, P])
        stout = at("stout", [HEAD_A, NB, 2, HEAD_A], o_rm)
        o_et = o
        ET = nxt("ET", [P, 2, 2, 2, P])
        Vblk = at("Vblk", [NB * TS, 2, NB, HEAD_A], o_et)
        TT = nxt("TT", [P, 2, 2, P])
        o_tn = o
        Tn = nxt("Tn", [P, 2, 2, P])
        Xs = nxt("Xs", [P, 2, 2, P])
        Ublk = at("Ublk", [NB * TS, 2, NB, HEAD_A], o_tn)
        VN = nxt("VN", [P, 3, P])
        KN = nxt("KN", [P, 3, P])
        BN = nxt("BN", [P, 3, P])
        As = nxt("As", [NB * TS, 2, 4, 32])
        ETs = nxt("ETs", [NB * TS, 2, 2, 32])
        Tns = nxt("Tns", [NB * TS, 2, 32])
        TTs = nxt("TTs", [NB * TS, 2, 32])
        Xss = nxt("Xss", [NB * TS, 2, 32])
        Ms = nxt("Ms", [P, P])
        Us = nxt("Us", [P, P])
        S1 = nxt("S1", [P, HEAD_A])
        SE = nxt("SE", [P, HEAD_A])
        stp = nxt("stp", [HEAD_A, 2, HEAD_A])
        MTs = nxt("MTs", [P, 32])
        Mss = nxt("Mss", [NB * TS, P])
        Uss = nxt("Uss", [NB * TS, P])

        top = zb + 2 * size(KF * T)
        ohi = at("ohi", [P, KA, T], o_h, F32R)
        olo = at("olo", [P, KA, T], o_h + size(KA * T), F32R)
        o = o_h + 2 * size(KA * T)
        vT = nxt("vT", [P, T])
        qr = nxt("qr", [P, T])
        kr = nxt("kr", [P, T])
        qs = nxt("qs", [P, HB, NB * TS])
        knh = nxt("knh", [P, 3, P])
        vnh = nxt("vnh", [P, 3, P])
        o_w = o
        qkv = nxt("qkv", [P, 3 * HB, T])
        o_at = o
        vns = nxt("vns", [NB * TS, HB, P])
        STo = nxt("STo", [NB * TS, NB, HB, TS])
        ptab = nxt("ptab", [1, NB * NPG], I32)
        of = nxt("of", [P, HB, T])
        o_at = o
        srow = nxt("srow", [P, 3, P])
        prob = nxt("prob", [P, 3, P])
        pT = nxt("pT", [P, 3, P])
        rtmp = nxt("rtmp", [P, 2, T])
        smallz = nxt("smallz", [P, 8])
        sm = nxt("sm", [P, 2, 4])
        o = o_w
        kT = nxt("kT", [P, 2, HB, P])
        smg = nxt("smg", [NB * TS, 32])
        srow2 = nxt("srow2", [NB * TS, ROW])
        PT2 = nxt("PT2", [P, NPG + 1, 32])
        osb = nxt("osb", [NB * TS, HB * P])
        Snew = nxt("Snew", [NB * TS, HB, TS])
        qz = nxt("qz", [P, HB, HB * TS + TS])
        assert o <= o_w + size(3 * HB * T)

        o_m = o_h + 2 * size(KA * T)
        mhi = at("mhi", [P, KD, T], o_m, F32R)
        mlo = at("mlo", [P, KD, T], o_m + size(KD * T), F32R)
        o = o_m + 2 * size(KD * T)
        sga = nxt("sga", [P, 4, T])
        sgb = nxt("sgb", [P, 4, T])
        mtmp = nxt("mtmp", [P, 2, T])

        fhi = at("fhi", [P, KF, T], zb, F32R)
        flo = at("flo", [P, KF, T], zb + size(KF * T), F32R)
        o_f = o_cst + size(2 * P)
        ext = at("ext", [P, 2, EPAD], o_f)
        cv = at("cv", [P, 2, EPAD], o_f + size(2 * EPAD))
        gl = at("gl", [P, 2, T], o_f + 2 * size(2 * EPAD))
        rsd = at("rsd", [P, 4, NB * TS], o_f + 2 * size(2 * EPAD))
        ff = at("ff", [P, 2, T], o_f + 2 * size(2 * EPAD) + size(2 * T))
        assert o_f + 2 * size(2 * EPAD) + 2 * size(2 * T) <= o_cst + 4 * CCOLS["eps_rms"][0]
        ynat = at("ynat", [P, 3, D], za_)
        ncn = at("ncn", [2 + 2 * NB, FF], zb)

        ps = ctx.enter_context(nc.psum_tensor("ps", [P, 8, 512], F32))

        def samp(ap):
            return ap.rearrange("p (b t) -> p b t", t=TS)

        def bc(ap, shape):
            return ap.to_broadcast(shape)

        s_cst, s_par, s_x, s_sh = (sem(n) for n in ("s_cst", "s_par", "s_x", "s_sh"))
        s_zero = sem("s_zero")
        s_tp = sem("s_tp")
        s_tev = sem("s_tev")
        s_silu = sem("s_silu")
        s_raw = [sem(f"s_raw{r}") for r in range(4)]
        s_ada, s_adr, s_adt, s_adaev = sem("s_ada"), sem("s_adr"), sem("s_adt"), sem("s_adaev")
        s_hi, s_lo, s_mm = sem("s_hi"), sem("s_lo"), sem("s_mm")
        s_sq, s_ssq, s_rms = sem("s_sq"), sem("s_ssq"), sem("s_rms")
        s_hn, s_hhi, s_hlo = sem("s_hn"), sem("s_hhi"), sem("s_hlo")
        s_evz, s_evq, s_ev_out, s_evd = sem("s_evz"), sem("s_evq"), sem("s_ev_out"), sem("s_evd")
        s_nsh, s_nst, s_nse = sem("s_nsh"), sem("s_nst"), sem("s_nse")
        s_out = sem("s_out")

        (s_lora, s_s0, s_lmm, s_s0t, s_s0e, s_stp, s_stpo, s_sto, s_stoo) = (sem(n) for n in (
            "s_lora", "s_s0", "s_lmm", "s_s0t", "s_s0e", "s_stp", "s_stpo", "s_sto", "s_stoo"))
        (s_lin, s_dif, s_mix, s_kkq, s_g, s_kkr, s_thw, s_tha, s_ld, s_ldt, s_ldn, s_cum,
         s_px, s_rkk, s_bon, s_bonv, s_dec, s_tr, s_vkb, s_mat, s_am, s_et, s_X, s_Xe, s_XT, s_T) = (sem(n) for n in (
            "s_lin", "s_dif", "s_mix", "s_kkq", "s_g", "s_kkr", "s_thw", "s_tha", "s_ld",
            "s_ldt", "s_ldn", "s_cum", "s_px", "s_rkk", "s_bon", "s_bonv", "s_dec", "s_tr", "s_vkb", "s_mat",
            "s_am", "s_et", "s_X", "s_Xe", "s_XT", "s_T"))
        (s_m, s_me, s_u, s_ue, s_y, s_s1, s_se, s_set, s_mt, s_mte, s_mst, s_mse, s_us, s_use, s_blk, s_ys,
         s_ss, s_ses, s_sst, s_yc, s_gm, s_gq, s_gv, s_gr, s_ya, s_yah, s_yal) = (sem(n) for n in (
            "s_m", "s_me", "s_u", "s_ue", "s_y", "s_s1", "s_se", "s_set", "s_mt", "s_mte", "s_mst", "s_mse",
            "s_us", "s_use", "s_blk", "s_ys", "s_ss", "s_ses", "s_sst", "s_yc", "s_gm", "s_gq", "s_gv", "s_gr",
            "s_ya", "s_yah", "s_yal"))
        (s_knh, s_vnh, s_kvo, s_evh, s_page, s_vt, s_rot, s_rope, s_kvt, s_sc, s_smx, s_pr, s_prn, s_prt,
         s_pt2, s_o) = (sem(n) if n != "s_page" else [sem(f"s_page{r}") for r in range(NPG // 2)] for n in (
            "s_knh", "s_vnh", "s_kvo", "s_evh", "s_page", "s_vt", "s_rot", "s_rope", "s_kvt", "s_sc",
            "s_smx", "s_pr", "s_prn", "s_prt", "s_pt2", "s_o"))
        (s_kt, s_kta, s_ksc, s_st, s_srow, s_pe2, s_pn2, s_pt3, s_p3e, s_pv, s_oc, s_ot, s_pve, s_oh) = (sem(n) for n in (
            "s_kt", "s_kta", "s_ksc", "s_st", "s_srow", "s_pe2", "s_pn2", "s_pt3", "s_p3e",
            "s_pv", "s_oc", "s_ot", "s_pve", "s_oh"))
        (s_gate, s_evm, s_mx, s_mh, s_ml) = (sem(n) for n in ("s_gate", "s_evm", "s_mx", "s_mh", "s_ml"))
        (s_ext, s_cst8, s_cv, s_cv1, s_gl, s_f, s_fh, s_fl, s_ncv, s_ncn, s_nct, s_yt, s_yev) = (sem(n) for n in (
            "s_ext", "s_cst8", "s_cv", "s_cv1", "s_gl", "s_f", "s_fh", "s_fl", "s_ncv", "s_ncn", "s_nct",
            "s_yt", "s_yev"))
        s_lin2, s_kkr2, s_kkp, s_q, s_new = (sem(n) for n in ("s_lin2", "s_kkr2", "s_kkp", "s_q", "s_new"))
        s_rs, s_cv2, s_pvu = (sem(n) for n in ("s_rs", "s_cv2", "s_pvu"))
        s_dve = sem("s_dve")
        s_carry = sem("s_carry")

        stages = {}
        n = 0
        for name, ks, groups in (("za", 8, 7), ("qkv", 8, 6), ("merge", 24, 4), ("out", 8, 4),
                                 ("up", 8, 22), ("down", 22, 4)):
            stages[name] = (n, ks, groups)
            n += ks * groups
            assert n % 4 == 0
        ADA_K, ADA_1, ADA_G = 8, 8, 24
        ADA_J = (ADA_G - ADA_1) // KA * ADA_K
        assert ADA_J == 16
        N_XT, N_T = 2 * LEVELS - 3, 2 * LEVELS - 2
        ADA_ROWS1 = 2

        banks = [("par", None), ("c", None), ("sh", None)] + [("x", (m, q)) for m in range(3) for q in range(4)] \
            + [("cv", q) for q in range(2)]
        M_ROWS = [P, P, NB * TS]

        block = ctx.enter_context(nc.Block())

        def one(h, n=1, step=1, off=0):
            return slice(h * step + off, h * step + off + n) if isinstance(h, int) else bass.ds(h * step + off, n)

        @block.sync
        def _(sp):
            sp.dma_start(cst[:, :], d["consts"]).then_inc(s_cst, 16)
            sp.dma_start(cnat[0:1, :], d["c_prompt"]).then_inc(s_cst, 16)
            sp.dma_start(cnat[1:NC, :], d["c_sample"]).then_inc(s_cst, 16)

            def slab(n, step, i, src, wait, carry=False):
                r = n % 4
                if wait is not None:
                    s, v = wait
                    sp.wait_ge(s, v)
                    if carry:
                        sp.sem_inc(s_carry, 1)
                sp.dma_start(raw[:, r, :, 0:src.shape[2]], src).then_inc(s_raw[r], 16)

            def wsrc(w, k0, col, n):
                return w[k0:k0 + 2 * P, bass.ds(col, n)].rearrange("(t p) n -> p t n", p=P)

            for s in range(4):
                slab(s, 0, 0, wsrc(d["w_ada"], s * 2 * P, 0, CH), None)
            sp.wait_ge(s_zero, 1)
            for name, (t, r, n) in PARAM_ROWS.items():
                dst = prow[r:r + n, t, :]
                if name == "mu_shift":
                    sp.dma_start(prow[r:r + n - 1, t, :], d[name][0:(n - 1) * P].rearrange("(r c) -> r c", c=P)).then_inc(s_par, 16)
                    w = ZA - (n - 1) * P
                    sp.dma_start(prow[r + n - 1:r + n, t, 0:w], d[name][(n - 1) * P:ZA].rearrange("(r c) -> r c", r=1)).then_inc(s_par, 16)
                elif name == "rwkv_rk":
                    sp.dma_start(dst, d[name].rearrange("(r a) c -> r (a c)", a=2)).then_inc(s_par, 16)
                elif name.startswith("conv_w"):
                    sp.dma_start(dst, d["conv_w"][int(name[-1]), :].rearrange("(r c) -> r c", c=P)).then_inc(s_par, 16)
                else:
                    sp.dma_start(dst, d[name].rearrange("(r c) -> r c", c=P)).then_inc(s_par, 16)
            sp.dma_start(shnat[:, 0:ZA], d["state_shift"]).then_inc(s_sh, 16)
            sp.dma_start(cvnat[:, :], d["state_conv"].rearrange("b r f -> (b r) f")).then_inc(s_sh, 16)
            for m in range(2):
                sp.dma_start(xnat[:, m, :], d["x_prompt"][0, m * P:(m + 1) * P, :]).then_inc(s_x, 16)
            sp.dma_start(xnat[0:NB * TS, 2, :], d["x_sample"].rearrange("b t f -> (b t) f")).then_inc(s_x, 16)
            for s in range(4, ADA_K):
                slab(s, 0, 0, wsrc(d["w_ada"], s * 2 * P, 0, CH), (s_ada, s - 3))
            with sp.Fori(1, ADA_1) as g:
                for s in range(ADA_K):
                    slab(s, ADA_K, g, wsrc(d["w_ada"], s * 2 * P, g * CH, CH), (s_ada, g * ADA_K + (s - 3)))

            def split_group(name, src, loop0=0, groups=None):
                n0, ks, _ = stages[name]
                with sp.Fori(loop0, groups) as g:
                    for s in range(ks):
                        slab(n0 + s, ks, g, src(g, s), (s_lo, g * ks + (n0 + s - 3)))

            def za_src(g, s):
                return wsrc(d["w_in"], s * 2 * P, g * CH, CH)

            for s in range(8):
                slab(s, 0, 0, za_src(0, s), (s_ada, ADA_1 * ADA_K + (s - 3)) if s < 4 else (s_lo, s - 3))
            split_group("za", za_src, 1, 6)
            n0 = stages["za"][0] + 48
            for s in range(8):
                slab(n0 + s, 0, 0, wsrc(d["w_in"], s * 2 * P, 6 * CH, 3 * P), (s_lo, n0 + s - 3))

            sp.wait_ge(s_nse, 7)
            sp.dma_start(d["shift_prompt"], nshn[0:1, 0:ZA]).then_inc(s_out, 16)
            sp.dma_start(d["shift_sample"], nshn[1:NC, 0:ZA]).then_inc(s_out, 16)
            def pair_loads(j):
                cols, pair = (bass.ds(0, P), bass.ds(0, 2)) if j is None else (bass.ds(j * P + P, P), bass.ds(j * 2 + 2, 2))
                if j is not None:
                    sp.wait_ge(s_lmm, j + 1)
                    sp.wait_ge(s_s0t, j + 1)
                sp.dma_start(lora[0:LORA_W, 0, :], d["rwkv_w2"][:, cols]).then_inc(s_lora, 16)
                sp.dma_start(lora[LORA_W:P, 0, :], d["rwkv_a2"][:, cols]).then_inc(s_lora, 16)
                sp.dma_start(lora[:, 1, :], d["rwkv_g2"][0:P, cols]).then_inc(s_lora, 16)
                sp.dma_start(lora[0:LORA_G - P, 2, :], d["rwkv_g2"][P:LORA_G, cols]).then_inc(s_lora, 16)
                for b in range(NB):
                    sp.dma_start(s0n[:, b, :, :], d["state_wkv"][b, pair, :, :].rearrange("h v k -> v h k")).then_inc(s_s0, 16)

            def ada_pair(j, s0, s1):
                for s in range(s0, s1):
                    src = wsrc(d["w_ada"], s % ADA_K * 2 * P, j * (2 * CH) + (ADA_1 + s // ADA_K) * CH, CH)
                    slab(s, 0, 0, src, (s_ada, j * ADA_J + (ADA_1 * ADA_K + s - 3)))

            pair_loads(None)
            sp.wait_ge(s_lo, stages["za"][1] * stages["za"][2])

            def pair_stores(j):
                sp.wait_ge(s_stp, j + 1)
                sp.dma_start(d["wkv_prompt"][0, one(j, 2, 2), :, :].rearrange("h v k -> v h k"), stp[:, :, :]).then_inc(s_stpo, 16)
                sp.wait_ge(s_sto, 2 * j + 2)
                for b in range(NB):
                    sp.dma_start(d["wkv_sample"][b, one(j, 2, 2), :, :].rearrange("h v k -> v h k"), stout[:, b, :, :]).then_inc(s_stoo, 16)

            with sp.Fori(0, 1) as j:
                ada_pair(j, 0, ADA_J)
                pair_loads(j)
            with sp.Fori(1, KA - 1) as j:
                ada_pair(j, 0, 6)
                pair_stores(j - 1)
                ada_pair(j, 6, ADA_J)
                pair_loads(j)
            with sp.Fori(KA - 1, KA) as j:
                ada_pair(j, 0, 6)
                pair_stores(j - 1)
                ada_pair(j, 6, ADA_J)

            n0 = stages["qkv"][0]

            def qkv_src(g, s):
                return wsrc(d["w_in"], s * 2 * P, g * CH + ZA, CH)

            for s in range(8):
                slab(n0 + s, 0, 0, qkv_src(0, s), (s_ada, ADA_G * ADA_K + (s - 3)) if s < 4 else (s_lo, n0 + s - 3))
                if s == 3:
                    pair_stores(KA - 1)
            split_group("qkv", qkv_src, 1, 6)

            sp.dma_start(ptab[:, :], d["page_table"].rearrange("(o b) p -> o (b p)", o=1)).then_inc(s_sh, 16)
            with sp.Fori(0, HB) as h:
                hh = bass.ds(h, 1)
                for nat, ready, po, so in ((knh, s_knh, "k_prompt", "k_sample"), (vnh, s_vnh, "v_prompt", "v_sample")):
                    sp.wait_ge(ready, h + 1)
                    sp.dma_start(d[po][0, :, hh, :].rearrange("(c p) h f -> p c (h f)", p=P), nat[:, 0:2, :]).then_inc(s_kvo, 16)
                    sp.dma_start(d[so][:, :, hh, :].rearrange("b t h f -> (b t) (h f)"), nat[0:NB * TS, 2, :]).then_inc(s_kvo, 16)
            sp.wait_ge(s_sh, 48)
            sp.wait_ge(s_mm, stages["merge"][0])

            def pages(cache, R, used, value):
                for p in range(NPG):
                    col = slice(R * NPG + p, R * NPG + p + 1) if isinstance(R, int) else bass.ds(R * NPG + p, 1)
                    page = sp.value_load(ptab[0:1, col], min_val=0, max_val=d[cache].shape[0] - 1)
                    if used is not None:
                        sp.wait_ge(used, value(p))
                    sp.dma_start(kpage[:, p, :], d[cache][bass.ds(page, 1), :, :, :].rearrange("o p h f -> p (o h f)")).then_inc(s_page[p // 2], 16)

            pages("cache_k", 0, None, None)
            pages("cache_k", 1, s_kt, lambda p: p + 1)
            pages("cache_v", 0, s_kt, lambda p: NPG + p + 1)
            with sp.Fori(1, NB - 1) as b:
                pages("cache_k", b + 1, s_pvu, lambda p: b * NPG + (p - 7))
                pages("cache_v", b, s_kt, lambda p: b * NPG + (NPG + p + 1))
            pages("cache_v", NB - 1, s_pvu, lambda p: (NB - 2) * NPG + p + 1)

            g0 = ZA + 3 * DB
            n0 = stages["merge"][0]
            sp.wait_ge(s_pvu, NB * NPG)
            with sp.Fori(0, 4) as g:
                parts = [(d["w_in"], g0, 8), (d["w_in"], g0 + D, 8), (d["w_proj_a"], 0, 4), (d["w_proj_b"], 0, 4)]
                s = 0
                for w, col, ks in parts:
                    for k in range(ks):
                        slab(n0 + s, 24, g, wsrc(w, k * 2 * P, g * CH + col, CH), (s_lo, g * 24 + (n0 + s - 3)), s == 16)
                        s += 1
            split_group("out", lambda g, s: wsrc(d["w_out"], s * 2 * P, g * CH, CH), 0, 4)
            n0 = stages["up"][0]
            with sp.Fori(0, 22) as g:
                for s in range(8):
                    r = (n0 + s) % 4
                    sp.wait_ge(s_lo, g * 8 + (n0 + s - 3))
                    for half in range(2):
                        sp.dma_start(raw[:, r, :, half * 256:half * 256 + 256],
                                     wsrc(d["w_up"], s * 2 * P, g * 256 + half * FF, 256)).then_inc(s_raw[r], 16)
            n0 = stages["down"][0]
            with sp.Fori(0, 2) as i:
                for gg in range(2):
                    for s in range(22):
                        q = gg * 22 + s
                        slab(n0 + q, 44, i, wsrc(d["w_down"], s * 2 * P, i * 1024 + gg * CH, CH), (s_lo, i * 44 + (n0 + q - 3)))
            sp.wait_ge(s_ncn, 11)
            sp.dma_start(d["conv_prompt"][0, :, :], ncn[0:2, :]).then_inc(s_out, 16)
            sp.dma_start(d["conv_sample"].rearrange("b r f -> (b r) f"), ncn[2:2 + 2 * NB, :]).then_inc(s_out, 16)
            for m in range(3):
                sp.wait_ge(s_yev, 4 * (m + 1))
                if m < 2:
                    sp.dma_start(d["y_prompt"][0, m * P:(m + 1) * P, :], ynat[:, m, :]).then_inc(s_out, 16)
                else:
                    sp.dma_start(d["y_sample"].rearrange("b t f -> (b t) f"), ynat[0:NB * TS, 2, :]).then_inc(s_out, 16)
            sp.wait_ge(s_out, 16 * 7)
            sp.wait_ge(s_stpo, 16 * KA)
            sp.wait_ge(s_stoo, 16 * NB * KA)
            sp.wait_ge(s_kvo, 64 * HB)


        def landed(name, g, s):
            n0, ks, _ = stages[name]
            up0 = stages["up"][0]
            n = n0 + ks * g.c + s
            before = (ADA_1 if name == "za" else ADA_G) * ADA_K
            v, per = 16 * (before // 4 + n // 4 + 1), 4
            if name == "up":
                v, per = v + 16 * ((n - up0) // 4 + 1), 8
            if name == "down":
                v += 16 * (stages["down"][0] - up0) // 4
            return v if g.i is None else g.i * (g.a * ks * per) + v

        class Chain:

            def __init__(self, eng, s):
                self.eng, self.s, self.base, self.n, self.i, self.per = eng, s, 0, 0, 0, 0

            def inc(self, ins):
                ins.then_inc(self.s, 1)
                self.n += 1

            def wait(self):
                self.eng.wait_ge(self.s, self.i * self.per + (self.base + self.n) if self.per else self.base + self.n)

            def __call__(self, ins):
                self.inc(ins)
                self.wait()

            def enter(self, i, per, i0=0):
                self.base, self.n, self.i, self.per, self.i0 = self.base + self.n - i0 * per, 0, i, per, i0

            def leave(self, trips):
                assert self.n == self.per, ("per", self.n)
                self.base, self.n, self.i, self.per = self.base + self.per * (trips + self.i0), 0, 0, 0

        def pbank(b):
            return ps[:, b, :]

        def heads(eng, first, body, last, own=None, per=0):
            first()
            with eng.Fori(1, HB - 1) as h:
                if own:
                    own.enter(h, per, 1)
                body(h)
            if own:
                own.leave(HB - 2)
            last()

        class G:

            def __init__(self, a, i, c):
                self.a, self.i, self.c = a, i, c
                self.parity = c % 2
                self.first = i is None and c == 0

            def at(self, k, plus=0):
                v = self.c * k + plus
                return v if self.i is None else self.i * (self.a * k) + v

            def prev(self):
                return G(self.a, self.i, self.c - 1)

        def over(eng, ng, body):
            body(G(0, None, 0))
            pairs = (ng - 1) // 2
            if pairs:
                with eng.Fori(0, pairs) as i:
                    body(G(2, i, 1))
                    body(G(2, i, 2))
            if (ng - 1) % 2:
                body(G(0, None, ng - 1))
            return G(0, None, ng - 1)

        def singles(eng, ng, body):
            body(G(0, None, 0))
            with eng.Fori(1, ng) as i:
                body(G(1, i, 0))
            return G(0, None, ng - 1)

        @block.gpsimd
        def _(pool):
            pool.wait_ge(s_evz, 7)
            pool.wait_ge(s_nst, 7)
            pool.wait_ge(s_lin, 2)
            zv = za[:, 0:3 * KA, :].rearrange("p (g j) c -> p g j c", g=3)
            with pool.Fori(0, KA) as j:
                jj = bass.ds(j, 1)
                pool.wait_ge(s_ss, j)
                pool.wait_ge(s_sst, 2 * j)
                pool.wait_ge(s_mix, j)
                pool.tensor_tensor(dif[:, :, 1:ZPAD], zv[:, :, jj, 0:ZPAD - 1].rearrange("p g j c -> p g (j c)"),
                                   zv[:, :, jj, 1:ZPAD].rearrange("p g j c -> p g (j c)"), ALU.subtract).then_inc(s_dif, 1)
                pool.wait_ge(s_am, 8 * j + 4)
                for lev in range(LEVELS):
                    b = lev % 2
                    if lev >= 2:
                        pool.wait_ge(s_X, j * LEVELS + (lev - 1))
                    if lev == 2:
                        pool.wait_ge(s_T, j * N_T + 1)
                    for e in range(2):
                        i = pool.tensor_tensor(ET[:, b, e, :, :], Am[:, e, 1, :, :],
                                               bc(c(f"lev{lev}").unsqueeze(1), [P, 2, P]), ALU.mult)
                        if lev < 2:
                            i = pool.tensor_tensor(ETs[:, lev, e, :], As[:, e, 1, :],
                                                   c(f"lev{lev}", 32)[:, 0:32], ALU.mult)
                    i.then_inc(s_et, 1)

            pool.wait_ge(s_tev, len(banks) - 1)
            with pool.Fori(0, KF // 2) as g:
                pool.wait_ge(s_cv1, 2 * g)
                e8 = ext[:, :, 2 + TP:EPAD].rearrange("p h (b t) -> p h b t", t=TS + 2)
                for h in range(2):
                    i = pool.tensor_copy(e8[:, h, :, 0:2], sconvT[:, bass.ds(g * 2 + h, 1), :].rearrange("p o (b r) -> p (o b) r", r=2))
                i.then_inc(s_cst8, 1)
                pool.wait_ge(s_ext, g + 1)
                for h in range(2):
                    nv = newconv[:, bass.ds(g * 2 + h, 1), :].rearrange("p o c -> p (o c)")
                    pool.tensor_copy(nv[:, 0:2], ext[:, h, TP:TP + 2])
                    i = pool.tensor_copy(nv[:, 2:].rearrange("p (b r) -> p b r", r=2), e8[:, h, :, TS:TS + 2])
                i.then_inc(s_ncv, 1)

        @block.scalar
        def _(act):

            def copy(o, i, **k):
                return act.activation(o, i, ACT.Copy, **k)

            act.wait_ge(s_tp, 2)
            act.activation(scT[:, :, :], pbank(1)[:, 0:KD * NC].rearrange("p (k c) -> p k c", c=NC), ACT.Silu).then_inc(s_silu, 1)

            def hi(name, g, s, width=CH):
                n0, ks, _ = stages[name]
                n = n0 + ks * g.c + s
                act.wait_ge(s_raw[n % 4], landed(name, g, s))
                if n >= 2:
                    act.wait_ge(s_mm, g.at(ks, n0 + s - 1))
                copy(whi[:, n % 2, :, 0:width], raw[:, n % 4, :, 0:width]).then_inc(s_hi, 1)

            def norm_sums(u):
                for q in range(4):
                    act.activation(sq[:, 4 * q:4 * q + 4, :], xT[:, 4 * q:4 * q + 4, :], ACT.Square).then_inc(s_sq, 1)
                act.wait_ge(s_ssq, u + 1)
                act.activation(rms[:, :], pbank(0)[:, 0:T], ACT.Sqrt, bias=c("eps_rms")).then_inc(s_rms, 1)

            def norm_hi(u, name):
                first = G(0, None, 0)
                hi(name, first, 0)
                hi(name, first, 1)
                for q in range(4):
                    act.wait_ge(s_hn, 4 * u + q + 1)
                    copy(hhi[:, 4 * q:4 * q + 4, :], sq[:, 4 * q:4 * q + 4, :]).then_inc(s_hhi, 1)
                    if q in (1, 2):
                        hi(name, first, q + 1)

            def ada_rows(n, bank):
                act.wait_ge(s_ada, n * ADA_K + ADA_K)
                copy(adr[:, :], pbank(bank)[0:NC, :]).then_inc(s_adr, 1)

            act.wait_ge(s_tev, 2 + 12)
            norm_sums(0)
            for g in range(ADA_1):
                if g:
                    act.wait_ge(s_adt, g)
                ada_rows(g, 1 + g % 2)
            norm_hi(0, "za")

            def za_evac(g, n=4):
                b4 = 4 * g.parity
                act.wait_ge(s_mm, g.at(8, 8))
                zt = za[:, bass.ds(g.at(4), n), :]
                copy(zt[:, :, 1:1 + TP], ps[:, b4:b4 + n, 0:TP])
                for k in range(n):
                    i = copy(za[:, bass.ds(g.at(4, k), 1), 1 + TP:].rearrange("p o (b t) -> p (o b) t", t=TS + 1)[:, :, 1:],
                             samp(ps[:, b4 + k, TP:T]))
                i.then_inc(s_evz, 1)

            def za_group(g):
                for s in range(4 if g.first else 0, 8):
                    hi("za", g, s, 3 * P if g.i is None and g.c == 6 else CH)
                    if s == 1 and not g.first:
                        za_evac(g.prev())
            za_evac(over(act, 7, za_group), 3)
            act.wait_ge(s_lin, 2)
            act.activation(lw[0:LORA_W, :], rkv[0:LORA_W, 0, :], ACT.Tanh)
            copy(lw[LORA_W:P, :], rkv[LORA_W:P, 0, :])
            act.activation(lsg[:, :, :], rkv[:, 1:3, :], ACT.Sigmoid).then_inc(s_lin2, 1)

            with act.Fori(0, KA) as j:
                jc = bass.ds(j, 1)
                w0h, a0h = smallc[:, bass.ds(j, 1)], smallc[:, bass.ds(j + 8, 1)]
                act.wait_ge(s_lmm, j + 1)
                act.wait_ge(s_yal, j)
                act.activation(v_thw[:, :], pbank(0)[:, 0:T], ACT.Tanh, bias=w0h, scale=0.5).then_inc(s_thw, 1)
                act.activation(v_tha[:, :], pbank(1)[:, 0:T], ACT.Tanh, bias=a0h, scale=0.5).then_inc(s_tha, 1)
                copy(v_g[:, :], pbank(2)[:, 0:T]).then_inc(s_g, 1)
                act.wait_ge(s_kkp, j + 1)
                act.activation(v_pv[:, :], pbank(3)[:, 0:T], ACT.Sqrt).then_inc(s_kkr, 1)
                act.wait_ge(s_ldt, j + 1)
                copy(ldn[:, 0:2, :], pbank(4)[:, 0:2 * P].rearrange("p (c f) -> p c f", f=P))
                copy(ldn[0:NB * TS, 2, :], pbank(4)[0:NB * TS, 2 * P:3 * P]).then_inc(s_ldn, 1)
                act.wait_ge(s_cum, j + 1)
                act.activation(v_px[:, :], pbank(5)[:, 0:T], ACT.Exp)
                act.activation(v_pi[:, :], pbank(6)[:, 0:T], ACT.Exp)
                act.wait_ge(s_kkr2, j + 1)
                act.activation(v_pv[:, :], pbank(6)[:, 0:T], ACT.Exp, scale=-1.0)
                act.activation(midc[:, 0:2], pbank(5)[:, 0:2 * P:P], ACT.Exp, scale=-1.0).then_inc(s_px, 1)
                act.wait_ge(s_tr, j + 1)
                m = NB * TS
                copy(VN[:, 0:2, :], pbank(0)[:, 0:2 * P].rearrange("p (c f) -> p c f", f=P))
                copy(KN[:, 0:2, :], pbank(0)[:, 2 * P:4 * P].rearrange("p (c f) -> p c f", f=P))
                copy(BN[:, 0:2, :], pbank(1)[:, 0:2 * P].rearrange("p (c f) -> p c f", f=P), scale=-1.0)
                copy(VN[0:m, 2, :], pbank(4)[0:m, 0:P])
                copy(KN[0:m, 2, :], pbank(4)[0:m, P:2 * P])
                copy(BN[0:m, 2, :], pbank(4)[0:m, 2 * P:3 * P], scale=-1.0).then_inc(s_vkb, 1)
                for lev in range(1, LEVELS):
                    act.wait_ge(s_X, j * LEVELS + lev + 1)
                    i = copy(Xs[:, :, :, :], pbank(0).rearrange("p (e c t) -> p e c t", e=2, c=2))
                    if lev == 1:
                        i = copy(Xss[:, :, :], pbank(3)[0:m, 0:64].rearrange("p (e t) -> p e t", e=2))
                    i.then_inc(s_Xe, 1)
                    if lev == ADA_ROWS1:
                        act.wait_ge(s_adt, 2 * j + ADA_1)
                        act.wait_ge(s_ada, j * ADA_J + (ADA_1 + 1) * ADA_K)
                        copy(adr[:, :], pbank(7)[0:NC, :]).then_inc(s_adr, 1)
                act.wait_ge(s_s0t, j + 1)
                copy(s0T[:, :, :], pbank(2).rearrange("p (b v) -> p b v", b=NB)).then_inc(s_s0e, 1)
                def right_sides(ck):
                    act.wait_ge(s_m, 2 * j + ck + 1)
                    if ck == 0:
                        copy(Ms[:, :], pbank(5)[:, 0:P]).then_inc(s_me, 1)
                    else:
                        copy(Ms[:, 0:64], pbank(5)[:, 0:64])
                        copy(Ms[:, 64:P], pbank(6)[:, 0:64]).then_inc(s_me, 1)

                def solved(ck):
                    act.wait_ge(s_u, 2 * j + ck + 1)
                    copy(Us[:, :], pbank(0)[:, 0:P]).then_inc(s_ue, 1)

                right_sides(0)
                act.wait_ge(s_mt, j + 1)
                copy(MTs[0:64, :], pbank(1)[0:64, P:P + m])
                copy(MTs[64:P, :], pbank(2)[64:P, P:P + m]).then_inc(s_mte, 1)
                solved(0)
                act.wait_ge(s_mst, j + 1)
                copy(Mss[:, :], pbank(1)[0:m, 0:P]).then_inc(s_mse, 1)
                act.wait_ge(s_us, j + 1)
                copy(Uss[:, :], pbank(2)[0:m, 0:P]).then_inc(s_use, 1)
                right_sides(1)
                solved(1)
                act.wait_ge(s_set, j + 1)
                act.wait_ge(s_stpo, 16 * j)
                copy(stp[:, :, :], pbank(2)[0:64, 0:P].rearrange("p (h k) -> p h k", h=2)).then_inc(s_stp, 1)
                for h in range(2):
                    act.wait_ge(s_sst, 2 * j + h + 1)
                    act.wait_ge(s_ys, j + 1)
                    act.wait_ge(s_stoo, 16 * NB * j)
                    copy(stout[:, 4 * h:4 * h + 4, :, :].rearrange("p b h k -> p (b h k)"), pbank(5 + h)[0:64, :]).then_inc(s_sto, 1)
                act.wait_ge(s_gq, j + 1)
                act.activation(v_px[:, :], pbank(0)[:, 0:T], ACT.Sqrt, bias=c("eps_lnx"), scale=1.0 / HEAD_A).then_inc(s_gr, 1)
                act.wait_ge(s_adt, 2 * j + (ADA_1 + 1))
                act.wait_ge(s_ada, j * ADA_J + (ADA_1 + 2) * ADA_K)
                copy(adr[:, :], pbank(7)[0:NC, :]).then_inc(s_adr, 1)
                act.wait_ge(s_ya, j + 1)
                act.activation(yahi[:, jc, :].rearrange("p o t -> p (o t)"), v_thw[:, :], ACT.Copy).then_inc(s_yah, 1)

            def plain(name):
                def group(g):
                    for s in range(stages[name][1]):
                        hi(name, g, s)
                over(act, stages[name][2], group)

            act.wait_ge(s_out, 32)
            plain("qkv")

            m = NB * TS

            def v_tile(h):
                act.wait_ge(s_kvt, h)
                copy(vT[:, :], qkv[:, one(h, off=2 * HB), :].rearrange("p o t -> p (o t)")).then_inc(s_vt, 1)

            def kv_rows(h):
                act.wait_ge(s_kvt, h + 1)
                act.wait_ge(s_kvo, 64 * h)
                act.wait_ge(s_o, h)
                copy(knh[:, 0:2, :], pbank(2)[:, 0:2 * P].rearrange("p (c f) -> p c f", f=P))
                copy(knh[0:m, 2, :], pbank(2)[0:m, 2 * P:3 * P]).then_inc(s_knh, 1)
                copy(vnh[:, 0:2, :], pbank(3)[:, 0:2 * P].rearrange("p (c f) -> p c f", f=P))
                copy(vnh[0:m, 2, :], pbank(3)[0:m, 2 * P:3 * P])
                copy(vns[:, one(h), :].rearrange("p o f -> p (o f)"), pbank(3)[0:m, 2 * P:3 * P]).then_inc(s_vnh, 1)

            def head_exp(h):
                act.wait_ge(s_smx, h + 1)
                act.activation(prob[:, 0, :], srow[:, 0, :], ACT.Exp, bias=sm[:, 0, 0:1], accum_out=sm[:, 1, 0:1])
                act.activation(prob[:, 1:3, :], srow[:, 1:3, :], ACT.Exp, bias=sm[:, 0, 1:2], accum_out=sm[:, 1, 1:2]).then_inc(s_pr, 1)

            def head_pT(h):
                act.wait_ge(s_prt, h + 1)
                copy(pT[:, :, :], pbank(6)[:, 0:3 * P].rearrange("p (c f) -> p c f", f=P)).then_inc(s_pt2, 1)

            def head_first():
                act.wait_ge(s_evq, 6)
                v_tile(0)
                kv_rows(0)
                head_exp(0)
                v_tile(1)

            def head(h, last=False):
                head_pT(h - 1)
                head_exp(h)
                if not last:
                    v_tile(h + 1)
                kv_rows(h)

            def head_last():
                head(HB - 1, True)
                head_pT(HB - 1)

            heads(act, head_first, head, head_last)

            m = NB * TS
            def keys(b):
                for p in range(NPG):
                    act.wait_ge(s_kt, b * NPG + (p + 1))
                    act.wait_ge(s_ksc, b * NPG + (p - 1 if p else 0))
                    copy(kT[:, p % 2, :, :].rearrange("p (a h) f -> p a (h f)", a=2), ps[:, 2 * (p % 2):2 * (p % 2) + 2, :]).then_inc(s_kta, 1)

            def exps(b):
                act.wait_ge(s_srow, b + 1)
                act.activation(srow2[:, :], srow2[:, :], ACT.Exp, bias=smg[:, 0:1], accum_out=smg[:, 1:2]).then_inc(s_pe2, 1)

            def outs(b):
                act.wait_ge(s_pv, b + 1)
                copy(osb[:, 0:CH], pbank(6)[0:m, :]).then_inc(s_oc, 1)

            keys(0)
            with act.Fori(0, NB - 1) as b:
                exps(b)
                keys(b + 1)
                outs(b)
            exps(NB - 1)
            outs(NB - 1)
            act.wait_ge(s_pve, 8)
            copy(ohi[:, :, :], of[:, :, :]).then_inc(s_oh, 1)

            m0 = stages["merge"][0]

            def merged_hi(g):
                for q in range(4):
                    act.wait_ge(s_mx, g.at(4, q + 1))
                    copy(mhi[:, bass.ds(g.at(4, q), 1), :].rearrange("p o t -> p (o t)"), sga[:, q, :]).then_inc(s_mh, 1)

            def merge(g):
                for s in range(24):
                    hi("merge", g, s)
                    if s == 2 and not g.first:
                        merged_hi(g.prev())
                    if s == 9:
                        act.wait_ge(s_mm, g.at(24, m0 + 8))
                        act.wait_ge(s_ml, g.at(4))
                        act.activation(sga[:, :, :], ps[:, 0:4, 0:T], ACT.Sigmoid).then_inc(s_gate, 1)
                    if s == 17:
                        act.wait_ge(s_mm, g.at(24, m0 + 16))
                        act.activation(sgb[:, :, :], ps[:, 4:8, 0:T], ACT.Sigmoid).then_inc(s_gate, 1)

            merged_hi(singles(act, 4, merge))
            plain("out")
            act.wait_ge(s_ev_out, 4)
            norm_sums(1)
            norm_hi(1, "up")

            cb, w0 = pcol("conv_b"), pcol("conv_w0")

            def up_in(g):
                b4 = 4 * g.parity
                act.wait_ge(s_mm, g.at(8, stages["up"][0] + 8))
                act.wait_ge(s_cv1, g.at(2))
                act.wait_ge(s_ncv, g.at(1))
                copy(ext[:, :, 2:2 + TP], ps[:, b4:b4 + 2, 0:TP])
                for h in range(2):
                    e8 = ext[:, h, 2 + TP:EPAD].rearrange("p (b t) -> p b t", t=TS + 2)
                    i = copy(e8[:, :, 2:], samp(ps[:, b4 + h, TP:T]))
                i.then_inc(s_ext, 1)
                act.wait_ge(s_ext, g.at(1, 1))
                act.wait_ge(s_cst8, g.at(1, 1))
                act.wait_ge(s_zero, 2)
                act.wait_ge(s_gl, g.at(1))
                for h in range(2):
                    act.activation(cv[:, h, 0:EPAD - 2], ext[:, h, 0:EPAD - 2], ACT.Identity, bias=cb[:, bass.ds(g.at(2, h), 1)],
                                   scale=w0[:, bass.ds(g.at(2, h), 1)]).then_inc(s_cv, 1)

            def up_gelu(g):
                act.wait_ge(s_cv1, g.at(2, 2))
                act.wait_ge(s_f, g.at(1))
                act.activation(gl[:, :, 0:TP], cv[:, :, 0:TP], ACT.Gelu_apprx_tanh)
                for h in range(2):
                    i = act.activation(samp(gl[:, h, TP:T]), cv[:, h, 2 + TP:EPAD].rearrange("p (b t) -> p b t", t=TS + 2)[:, :, 0:TS],
                                       ACT.Gelu_apprx_tanh)
                i.then_inc(s_gl, 1)

            def up_hi(g):
                act.wait_ge(s_f, g.at(1, 1))
                copy(fhi[:, bass.ds(g.at(2), 2), :], ff[:, :, :]).then_inc(s_fh, 1)

            def up_group(g):
                for s in range(4 if g.first else 0, 8):
                    hi("up", g, s)
                    if not g.first and s in (1, 3, 5):
                        (up_in if s == 1 else up_gelu if s == 3 else up_hi)(g.prev())

            last = over(act, 22, up_group)
            up_in(last)
            up_gelu(last)
            up_hi(last)
            plain("down")
            act.wait_ge(s_evd, 4)
            norm_sums(2)

        @block.vector
        def _(dve):
            own = Chain(dve, s_dve)
            TTn, STT, TS_ = dve.tensor_tensor, dve.scalar_tensor_tensor, dve.tensor_scalar
            m = NB * TS
            dve.memset(prow[:, :, :], 0.0).then_inc(s_zero, 1)
            own(dve.memset(shnat[:, ZA:], 0.0))
            own(dve.memset(za[:, :, 0:1], 0.0))
            for bi, (kind, at_) in enumerate(banks):
                src = pbank(bi % 8)
                if kind == "c":
                    continue
                dve.wait_ge(s_tp, bi + 1)
                if kind == "par":
                    i = dve.tensor_copy(par[:, :, :], src.rearrange("p (t c) -> p t c", t=4))
                elif kind == "sh":
                    i = dve.tensor_copy(za[:, :, 1 + TP:ZPAD].rearrange("p k (b t) -> p k b t", t=TS + 1)[:, :, :, 0],
                                        src[:, 0:ZT * NB].rearrange("p (k b) -> p k b", b=NB))
                elif kind == "x":
                    mt, q = at_
                    w = M_ROWS[mt]
                    i = dve.tensor_copy(xT[:, 4 * q:4 * q + 4, mt * P:mt * P + w],
                                        src.rearrange("p (i t) -> p i t", i=4)[:, :, 0:w])
                else:
                    i = dve.tensor_copy(sconvT[:, 22 * at_:22 * at_ + 22, :],
                                        src[:, 0:22 * 2 * NB].rearrange("p (k b) -> p k b", b=2 * NB))
                i.then_inc(s_tev, 1)

            bada = pcol("b_ada")
            dve.wait_ge(s_tev, 1)

            def ada_cols(g, n, bank):
                dve.wait_ge(s_adt, n)
                TTn(mod[:, bass.ds(g * 4, 4), :], pbank(bank)[:, 0:4 * NC].rearrange("p (q c) -> p q c", c=NC),
                    bc(bada[:, bass.ds(g * 4, 4)].unsqueeze(2), [P, 4, NC]), ALU.add).then_inc(s_adaev, 1)

            def lo(name, g, s, width=CH):
                n0, ks, _ = stages[name]
                n = n0 + ks * g.c + s
                dve.wait_ge(s_hi, g.at(ks, n0 + s + 1))
                TTn(wlo[:, n % 2, :, 0:width], raw[:, n % 4, :, 0:width], whi[:, n % 2, :, 0:width].bitcast(F32),
                    ALU.subtract).then_inc(s_lo, 1)

            def norm_x(u):
                dve.wait_ge(s_rms, u + 1)
                own(dve.reciprocal(rstd[:, :], rms[:, :]))
                for q in range(4):
                    k4 = slice(4 * q, 4 * q + 4)
                    own.inc(TTn(sq[:, k4, :], xT[:, k4, :], bc(rstd[:, :].unsqueeze(1), [P, 4, T]), ALU.mult))

            def norm_h(u, gname, shift, scale, name):
                first = G(0, None, 0)
                lo(name, first, 0)
                lo(name, first, 1)
                own(STT(gsc[:, :, :], mod[:, scale:scale + KD, :], 1.0,
                        bc(pcol(gname).unsqueeze(2), [P, KD, NC]), ALU.add, ALU.mult))
                for q in range(4):
                    for k in range(4 * q, 4 * q + 4):
                        own.inc(TS_(sq[:, k, 0:TP], sq[:, k, 0:TP], gsc[:, k, 0:1], mod[:, shift + k, 0:1], ALU.mult, ALU.add))
                        own.inc(TTn(samp(sq[:, k, TP:T]), samp(sq[:, k, TP:T]), bc(gsc[:, k, 1:NC].unsqueeze(2), [P, NB, TS]), ALU.mult))
                    own.wait()
                    for k in range(4 * q, 4 * q + 4):
                        i = TTn(samp(sq[:, k, TP:T]), samp(sq[:, k, TP:T]), bc(mod[:, shift + k, 1:NC].unsqueeze(2), [P, NB, TS]), ALU.add)
                    i.then_inc(s_hn, 1)
                    if q:
                        norm_lo(u, q - 1)
                        if q > 1:
                            lo(name, first, q)
                norm_lo(u, 3)

            def norm_lo(u, q):
                k4 = slice(4 * q, 4 * q + 4)
                dve.wait_ge(s_hhi, 4 * u + q + 1)
                TTn(hlo[:, k4, :], sq[:, k4, :], hhi[:, k4, :].bitcast(F32), ALU.subtract).then_inc(s_hlo, 1)

            norm_x(0)
            for g in range(ADA_1):
                ada_cols(g, g + 1, 3 + g % 2)
            dve.wait_ge(s_adaev, ADA_1)
            norm_h(0, "norm1_g", 0, KD, "za")

            def plain(name, evac):
                ks = stages[name][1]

                def group(g):
                    for s in range(4 if g.first and name == "za" else 0, ks):
                        lo(name, g, s, 3 * P if name == "za" and g.i is None and g.c == 6 else CH)
                        if s == 1 and evac and not g.first:
                            evac(g.prev())
                last = over(dve, stages[name][2], group)
                if evac:
                    evac(last)

            plain("za", None)
            dve.wait_ge(s_evz, 7)
            own(dve.tensor_copy(nsh[:, :, 0:1], za[:, :, TP:TP + 1]))
            dve.tensor_copy(nsh[:, :, 1:NC], za[:, :, 1 + TP:].rearrange("p k (b t) -> p k b t", t=TS + 1)[:, :, :, TS]).then_inc(s_nsh, 1)
            own.inc(TS_(smallc[:, 0:8], pcol("rwkv_w0"), 0.5, None, ALU.mult))
            own.inc(TS_(smallc[:, 8:16], pcol("rwkv_a0"), 0.5, None, ALU.mult))
            own.inc(TS_(smallc[:, 16:24], pcol("rwkv_ka"), 0.5, None, ALU.mult))
            own.inc(TS_(smallc[:, 24:32], pcol("rwkv_ka"), -0.5, 1.0, ALU.mult, ALU.add))
            own.wait()
            own(dve.memset(smallc[:, 32:40], 0.0))
            mu = pcol("mu_shift")

            def mix(dst, df, z, muc):
                STT(dst[:, 0:TP], df[:, 1:1 + TP], muc, z[:, 1:1 + TP], ALU.mult, ALU.add)
                dv, zv = (a[:, 1 + TP:ZPAD].rearrange("p (b t) -> p b t", t=TS + 1)[:, :, 1:] for a in (df, z))
                return STT(samp(dst[:, TP:T]), dv, muc, zv, ALU.mult, ALU.add)

            for q in range(3):
                z = za[:, 3 * KA + q, :]
                own(TTn(dif[:, q, 1:ZPAD], z[:, 0:ZPAD - 1], z[:, 1:ZPAD], ALU.subtract))
                i = mix(rkv[:, q, :], dif[:, q, :], z, mu[:, 3 * KA + q:3 * KA + q + 1])
                if q:
                    i.then_inc(s_lin, 1)
            for b in range(7):
                w = min(4, ZT - 4 * b) * P
                dve.wait_ge(s_nst, b + 1)
                dve.tensor_copy(nshn[:, 4 * b * P:4 * b * P + w], pbank(b)[0:NC, 0:w]).then_inc(s_nse, 1)
            dve.wait_ge(s_lin2, 1)

            def pc(name, j):
                return pcol(name)[:, bass.ds(j, 1)]

            with dve.Fori(0, KA) as j:
                own.enter(j, 19)
                r_, k_, v_ = rkv[:, 0, :], rkv[:, 1, :], rkv[:, 2, :]
                dve.wait_ge(s_dif, j + 1)
                for q in range(3):
                    z = za[:, bass.ds(j + q * KA, 1), :].rearrange("p o t -> p (o t)")
                    i = mix(rkv[:, q, :], dif[:, q, :], z, mu[:, bass.ds(j + q * KA, 1)])
                i.then_inc(s_mix, 1)
                dve.wait_ge(s_mix, j + 1)
                own(TS_(v_kk[:, :], k_, pc("rwkv_kk", j), None, ALU.mult))
                TTn(v_sq[:, :], v_kk[:, :], v_kk[:, :], ALU.mult).then_inc(s_kkq, 1)
                dve.wait_ge(s_thw, j + 1)
                TS_(v_ld[:, :], v_thw[:, :], -0.5 * DECAY, -0.5 * DECAY, ALU.mult, ALU.add).then_inc(s_ld, 1)
                dve.wait_ge(s_tha, j + 1)
                own(TS_(v_k[:, :], v_tha[:, :], smallc[:, bass.ds(j + 16, 1)], smallc[:, bass.ds(j + 24, 1)], ALU.mult, ALU.add))
                own(TTn(v_k[:, :], v_k[:, :], k_, ALU.mult))
                own(TS_(v_tha[:, :], v_tha[:, :], 0.5, 0.5, ALU.mult, ALU.add))
                dve.wait_ge(s_kkp, j + 1)
                STT(v_sq[:, :], r_, pc("rwkv_rk", j), v_k[:, :], ALU.mult, ALU.mult).then_inc(s_rkk, 1)
                dve.wait_ge(s_kkr, j + 1)
                own(TS_(v_pv[:, :], v_pv[:, :], 1e-12, None, ALU.max))
                own(dve.reciprocal(v_pv[:, :], v_pv[:, :]))
                TTn(v_kk[:, :], v_kk[:, :], v_pv[:, :], ALU.mult).then_inc(s_kkr2, 1)
                dve.wait_ge(s_kkr2, j + 1)
                own(TTn(v_b[:, :], v_kk[:, :], v_tha[:, :], ALU.mult))
                dve.wait_ge(s_bon, j + 1)
                TTn(v_bon[:, :], pbank(3)[:, 0:T], v_, ALU.mult).then_inc(s_bonv, 1)
                dve.wait_ge(s_px, j + 1)
                own.inc(TTn(v_k[:, :], v_k[:, :], v_pv[:, :], ALU.mult))
                own.inc(TTn(v_b[:, :], v_b[:, :], v_pv[:, :], ALU.mult))
                own.inc(TTn(v_kk[:, :], v_kk[:, :], v_px[:, :], ALU.mult))
                own(TTn(r_, r_, v_pi[:, :], ALU.mult))
                TTn(midc[:, 2:3], midc[:, 1:2], v_pi[:, P - 1:P], ALU.mult).then_inc(s_dec, 1)
                dve.wait_ge(s_mat, j + 1)
                for e in range(2):
                    TTn(Am[:, e, :, :, :].rearrange("p a c t -> p (a c) t"), pbank(2 + e).rearrange("p (a t) -> p a t", t=P),
                        bc(c("lt").unsqueeze(1), [P, 4, P]), ALU.mult).then_inc(s_am, 1)
                n4 = CCOLS["lt4"][0]
                for e in range(2):
                    src = pbank(4 * e)[0:m, 3 * e * P:(3 * e + 1) * P]
                    TTn(As[:, e, :, :].rearrange("p a t -> p (a t)"), src, cst[0:m, n4:n4 + P], ALU.mult).then_inc(s_am, 1)
                dve.wait_ge(s_stoo, 16 * NB * j)
                nle = CCOLS["le"][0]
                for e in range(2):
                    for a in range(2):
                        TTn(Rm[:, e, a, :, :], pbank(5 + e)[:, 2 * a * P:2 * a * P + 2 * P].rearrange("p (c t) -> p c t", t=P),
                            bc(cst[:, nle + a * P:nle + (a + 1) * P].unsqueeze(1), [P, 2, P]), ALU.mult).then_inc(s_am, 1)
                for lev in range(LEVELS):
                    if lev == 0:
                        dve.wait_ge(s_X, j * LEVELS + 1)
                        idb = bc(ident.unsqueeze(1), [P, 4, P])
                        v4 = lambda a: a.rearrange("p e c t -> p (e c) t")
                        TTn(v4(Tn[:, :, :, :]), idb, pbank(0).rearrange("p (a t) -> p a t", t=P), ALU.subtract)
                        TTn(v4(TT[:, :, :, :]), idb, v4(ET[:, 0, :, :, :]), ALU.subtract)
                        ids = bc(ident[0:m, 0:m].unsqueeze(1), [m, 2, m])
                        TTn(Tns[:, :, :], ids, pbank(3)[0:m, 0:64].rearrange("p (e t) -> p e t", e=2), ALU.subtract)
                        TTn(TTs[:, :, :], ids, ETs[:, 0, :, :], ALU.subtract).then_inc(s_T, 1)
                    else:
                        n = j * N_XT + 2 * lev
                        f = lambda a: a.rearrange("p e c t -> p (e c t)")
                        if lev < LEVELS - 1:
                            dve.wait_ge(s_XT, n - 1)
                            TTn(f(Tn[:, :, :, :]), f(Tn[:, :, :, :]), pbank(1), ALU.subtract).then_inc(s_T, 1)
                        dve.wait_ge(s_XT, n if lev < LEVELS - 1 else n - 1)
                        if lev == 1:
                            TTn(TTs[:, :, :], TTs[:, :, :], pbank(3)[0:m, 128:192].rearrange("p (e t) -> p e t", e=2), ALU.subtract)
                        TTn(f(TT[:, :, :, :]), f(TT[:, :, :, :]), pbank(2), ALU.subtract).then_inc(s_T, 1)
                    if lev == ADA_ROWS1 + 1:
                        ada_cols(2 * j + ADA_1, 2 * j + (ADA_1 + 1), 7)
                def blocks(dst, src):
                    seq = bc(c("seq", m).unsqueeze(2), [m, NB, HEAD_A])
                    for e in range(2):
                        i = TTn(dst[:, e, :, :], bc(src[:, e * HEAD_A:(e + 1) * HEAD_A].unsqueeze(1), [m, NB, HEAD_A]), seq, ALU.mult)
                    return i
                own(blocks(Vblk, VN[0:m, 2, :]))
                dve.wait_ge(s_y, 2 * j + 1)
                TS_(S1[:, :], pbank(4)[:, 0:HEAD_A], midc[:, 2:3], None, ALU.mult).then_inc(s_s1, 1)
                dve.wait_ge(s_use, j + 1)
                blocks(Ublk, Uss[:, :]).then_inc(s_blk, 1)
                dve.wait_ge(s_ss, j + 1)
                own(TTn(endS[:, :, :], pbank(1).rearrange("p (b v) -> p b v", b=NB), s0T[:, :, :], ALU.add))
                TTn(endS[:, :, :], endS[:, :, :], bc(samp(v_pi[:, TP:T])[:, :, TS - 1:TS], [P, NB, HEAD_A]), ALU.mult).then_inc(s_ses, 1)
                dve.wait_ge(s_y, 2 * j + 2)
                own(TTn(SE[:, :], pbank(4)[:, HEAD_A:2 * HEAD_A], S1[:, :], ALU.add))
                TS_(SE[:, :], SE[:, :], v_pi[:, TP - 1:TP], None, ALU.mult).then_inc(s_se, 1)
                dve.wait_ge(s_ys, j + 1)
                dve.tensor_copy(v_thw[:, :], pbank(3)[:, 0:T]).then_inc(s_yc, 1)
                dve.wait_ge(s_gm, j + 1)
                own(STT(v_ld[:, :], pbank(0)[:, 0:T], -1.0 / HEAD_A, v_thw[:, :], ALU.mult, ALU.add))
                TTn(v_sq[:, :], v_ld[:, :], v_ld[:, :], ALU.mult).then_inc(s_gv, 1)
                dve.wait_ge(s_gr, j + 1)
                own(dve.reciprocal(v_px[:, :], v_px[:, :]))
                own(TTn(v_ld[:, :], v_ld[:, :], v_px[:, :], ALU.mult))
                own(TS_(v_ld[:, :], v_ld[:, :], pc("lnx_g", j), pc("lnx_b", j), ALU.mult, ALU.add))
                own(TTn(v_ld[:, :], v_ld[:, :], v_bon[:, :], ALU.add))
                TTn(v_thw[:, :], v_ld[:, :], v_g[:, :], ALU.mult).then_inc(s_ya, 1)
                dve.wait_ge(s_yah, j + 1)
                jc = bass.ds(j, 1)
                TTn(yalo[:, jc, :].rearrange("p o t -> p (o t)"), v_thw[:, :],
                    yahi[:, jc, :].rearrange("p o t -> p (o t)").bitcast(F32), ALU.subtract).then_inc(s_yal, 1)
                ada_cols(2 * j + (ADA_1 + 1), 2 * j + (ADA_1 + 2), 7)
            own.leave(KA)

            def qkv_evac(g):
                b4 = 4 * g.parity
                dve.wait_ge(s_mm, g.at(8, stages["qkv"][0] + 8))
                dve.tensor_copy(qkv[:, bass.ds(g.at(4), 4), :], ps[:, b4:b4 + 4, 0:T]).then_inc(s_evq, 1)

            dve.wait_ge(s_stpo, 16 * KA)
            dve.wait_ge(s_stoo, 16 * NB * KA)
            dve.wait_ge(s_out, 32)
            plain("qkv", qkv_evac)
            dve.wait_ge(s_evq, 6)

            def fl(ap):
                return ap.rearrange("p o t -> p (o t)")

            def rope(h):
                q_, k_ = fl(qkv[:, one(h), :]), fl(qkv[:, one(h, off=HB), :])
                own.inc(TTn(qr[:, :], q_, c("cos"), ALU.mult))
                own.inc(TTn(kr[:, :], k_, c("cos"), ALU.mult))
                dve.wait_ge(s_rot, h + 1)
                own.inc(TTn(rtmp[:, 0, :], pbank(0)[:, 0:T], c("sin"), ALU.mult))
                own(TTn(rtmp[:, 1, :], pbank(1)[:, 0:T], c("sin"), ALU.mult))
                own.inc(TTn(qr[:, :], qr[:, :], rtmp[:, 0, :], ALU.add))
                own(TTn(kr[:, :], kr[:, :], rtmp[:, 1, :], ALU.add))
                dve.tensor_copy(fl(qs[:, one(h), :]), qr[:, TP:T]).then_inc(s_rope, 1)

            def head_scores(h):
                dve.wait_ge(s_sc, h + 1)
                own.inc(STT(srow[:, 0, :], pbank(4)[:, 0:P], SCALE, c("causal"), ALU.mult, ALU.add))
                own.inc(TS_(srow[:, 1, :], pbank(5)[:, 0:P], SCALE, None, ALU.mult))
                own(STT(srow[:, 2, :], pbank(5)[:, P:2 * P], SCALE, c("causal"), ALU.mult, ALU.add))
                own.inc(dve.tensor_reduce(sm[:, 0, 0:1], srow[:, 0, :], AX.X, ALU.max, negate=True))
                dve.tensor_reduce(sm[:, 0, 1:2], srow[:, 1:3, :], AX.XY, ALU.max, negate=True).then_inc(s_smx, 1)
                STT(STo[:, :, one(h), :].rearrange("p b o t -> p b (o t)"), samp(pbank(7)[0:m, 0:m]), SCALE,
                    samp(c("own", m)), ALU.mult, ALU.add).then_inc(s_new, 1)

            def head_norm(h):
                dve.wait_ge(s_pr, h + 1)
                own(dve.reciprocal(sm[:, 1, 2:4], sm[:, 1, 0:2]))
                TS_(prob[:, 0, :], prob[:, 0, :], sm[:, 1, 2:3], None, ALU.mult)
                TS_(prob[:, 1:3, :], prob[:, 1:3, :], sm[:, 1, 3:4], None, ALU.mult).then_inc(s_prn, 1)

            def head_out(h):
                dve.wait_ge(s_o, h + 1)
                dve.tensor_copy(of[:, one(h), 0:TP].rearrange("p o t -> p (o t)"), pbank(6)[:, 0:TP]).then_inc(s_evh, 1)

            def head_first():
                rope(0)
                head_scores(0)
                rope(1)
                head_norm(0)

            def head(h, last=False):
                head_scores(h)
                if not last:
                    rope(h + 1)
                head_out(h - 1)
                head_norm(h)

            def head_last():
                head(HB - 1, True)
                head_out(HB - 1)

            heads(dve, head_first, head, head_last, own, 11)
            dve.wait_ge(s_new, HB)

            dve.wait_ge(s_evh, HB)
            def queries(b):
                col = slice(TS * b, TS * b + TS) if isinstance(b, int) else bass.ds(b * TS, TS)
                one = slice(b, b + 1) if isinstance(b, int) else bass.ds(b, 1)
                dve.tensor_copy(Snew[:, :, :], STo[:, one, :, :].rearrange("p o h t -> p (o h) t"))
                diag = qz[:, :, :].rearrange("p h x -> p (h x)")[:, 0:HB * (HB * TS + TS)]
                dve.tensor_copy(diag.rearrange("p (h x) -> p h x", x=HB * TS + TS)[:, :, 0:TS], qs[:, :, col]).then_inc(s_q, 1)

            def select(b):
                row, sg = srow2, smg
                dve.wait_ge(s_st, b + 1)
                own.inc(dve.tensor_copy(row[:, PAST:], pbank(3)[0:m, 0:m]))
                own(TS_(row[:, 0:PAST], ps[0:m, 4:6, :].rearrange("p a t -> p (a t)"), SCALE, None, ALU.mult))
                blk = row[:, 0:PAST].rearrange("p (n k) -> p n k", n=NBLK)
                own(dve.tensor_reduce(sg[:, 4:8], blk, AX.X, ALU.add))
                own(dve.tensor_reduce(sg[:, 8:9], sg[:, 4:8], AX.X, ALU.min))
                own(TS_(sg[:, 12:16], sg[:, 4:8], sg[:, 8:9], None, ALU.is_equal))
                own(TS_(sg[:, 20:24], sg[:, 12:16], -1.0, 1.0, ALU.mult, ALU.add))
                own(dve.memset(sg[:, 19:20], 1.0))
                for n in (2, 1, 0):
                    own(TTn(sg[:, 16 + n:17 + n], sg[:, 17 + n:18 + n], sg[:, 21 + n:22 + n], ALU.mult))
                own(STT(sg[:, 24:28], sg[:, 12:16], NEG, sg[:, 16:20], ALU.mult, ALU.mult))
                own(TTn(blk, blk, bc(sg[:, 24:28].unsqueeze(2), [m, NBLK, BLK]), ALU.add))
                dve.tensor_reduce(sg[:, 0:1], row[:, :], AX.X, ALU.max, negate=True).then_inc(s_srow, 1)

            def normalise(b):
                dve.wait_ge(s_pe2, b + 1)
                own(dve.reciprocal(smg[:, 2:3], smg[:, 1:2]))
                TS_(srow2[:, :], srow2[:, :], smg[:, 2:3], None, ALU.mult).then_inc(s_pn2, 1)
                dve.wait_ge(s_pt3, b + 1)
                own.inc(dve.tensor_copy(PT2[:, 0:NPG, :], pbank(0)[:, 0:NPG * 32].rearrange("p (b t) -> p b t", t=32)))
                dve.tensor_copy(PT2[0:m, NPG, :], pbank(0)[0:m, NPG * 32:NPG * 32 + 32]).then_inc(s_p3e, 1)

            def outs(b):
                dve.wait_ge(s_pv, b + 1)
                dve.tensor_copy(osb[:, CH:], pbank(7)[0:m, :]).then_inc(s_oc, 1)
                dve.wait_ge(s_ot, b + 1)
                col = slice(TP + TS * b, TP + TS * b + TS) if isinstance(b, int) else bass.ds(b * TS + TP, TS)
                dve.tensor_copy(of[:, :, col], pbank(2)[:, 0:HB * 36].rearrange("p (h x) -> p h x", x=36)[:, :, 0:TS]).then_inc(s_pve, 1)

            own(dve.memset(qz[:, :, :], 0.0))
            queries(0)
            select(0)
            with dve.Fori(0, NB - 1) as b:
                own.enter(b, 14)
                queries(b + 1)
                normalise(b)
                select(b + 1)
                outs(b)
            own.leave(NB - 1)
            normalise(NB - 1)
            outs(NB - 1)
            dve.wait_ge(s_oh, 1)
            TTn(olo[:, :, :], of[:, :, :], ohi[:, :, :].bitcast(F32), ALU.subtract).then_inc(s_evm, 1)

            m0 = stages["merge"][0]

            def merge_end(g):
                dve.wait_ge(s_mm, g.at(24, m0 + 24))
                dve.wait_ge(s_gate, g.at(2, 2))
                TTn(sgb[:, :, :], sgb[:, :, :], ps[:, 4:8, 0:T], ALU.mult).then_inc(s_evm, 1)
                dve.wait_ge(s_evm, g.at(2, 3))
                for q in range(4):
                    TTn(sga[:, q, :], sga[:, q, :], sgb[:, q, :], ALU.add).then_inc(s_mx, 1)
                for q in range(4):
                    dve.wait_ge(s_mh, g.at(4, q + 1))
                    qc = bass.ds(g.at(4, q), 1)
                    TTn(fl(mlo[:, qc, :]), sga[:, q, :], fl(mhi[:, qc, :]).bitcast(F32), ALU.subtract).then_inc(s_ml, 1)

            def merge(g):
                for s in range(24):
                    lo("merge", g, s)
                    if s == 1 and not g.first:
                        merge_end(g.prev())
                    if s == 21:
                        dve.wait_ge(s_mm, g.at(24, m0 + 20))
                        dve.wait_ge(s_gate, g.at(2, 1))
                        TTn(sga[:, :, :], sga[:, :, :], ps[:, 0:4, 0:T], ALU.mult).then_inc(s_evm, 1)

            merge_end(singles(dve, 4, merge))

            def residual(name, gate, done):
                n0, ks, _ = stages[name]

                def evac(g):
                    b4 = 4 * g.parity
                    dve.wait_ge(s_mm, g.at(ks, n0 + ks))
                    for q in range(4):
                        kc = bass.ds(g.at(4, q), 1)
                        x = fl(xT[:, kc, :])
                        STT(x[:, 0:TP], ps[:, b4 + q, 0:TP], mod[:, bass.ds(g.at(4, gate + q), 1), 0], x[:, 0:TP], ALU.mult, ALU.add)
                        i = TTn(samp(rsd[:, q, :]), samp(ps[:, b4 + q, TP:T]),
                                bc(mod[:, bass.ds(g.at(4, gate + q), 1), 1:NC].rearrange("p o b -> p (o b)").unsqueeze(2), [P, NB, TS]), ALU.mult)
                    i.then_inc(s_rs, 1)
                    dve.wait_ge(s_rs, g.at(1, 1 + (4 if name == "down" else 0)))
                    k4 = bass.ds(g.at(4), 4)
                    TTn(xT[:, k4, TP:T], xT[:, k4, TP:T], rsd[:, :, :], ALU.add).then_inc(done, 1)
                plain(name, evac)

            residual("out", 32, s_ev_out)
            dve.wait_ge(s_ev_out, 4)
            dve.wait_ge(s_adaev, ADA_G)
            norm_x(1)
            own.wait()
            norm_h(1, "norm2_g", 48, 64, "up")
            own(dve.memset(ext[:, :, 0:2], 0.0))
            dve.memset(cv[:, :, EPAD - 2:], 0.0).then_inc(s_zero, 1)

            w1, w2 = pcol("conv_w1"), pcol("conv_w2")

            def up_taps(g):
                for h in range(2):
                    dve.wait_ge(s_cv, g.at(2, h + 1))
                    STT(cv[:, h, 0:EPAD - 2], ext[:, h, 1:EPAD - 1], w1[:, bass.ds(g.at(2, h), 1)], cv[:, h, 0:EPAD - 2], ALU.mult, ALU.add).then_inc(s_cv2, 1)
                for h in range(2):
                    dve.wait_ge(s_cv2, g.at(2, h + 1))
                    STT(cv[:, h, 0:EPAD - 2], ext[:, h, 2:EPAD], w2[:, bass.ds(g.at(2, h), 1)], cv[:, h, 0:EPAD - 2], ALU.mult, ALU.add).then_inc(s_cv1, 1)

            def up_f(g):
                dve.wait_ge(s_gl, g.at(1, 1))
                b4 = 4 * g.parity
                TTn(ff[:, :, :], gl[:, :, :], ps[:, b4 + 2:b4 + 4, 0:T], ALU.mult).then_inc(s_f, 1)

            def up_lo(g):
                dve.wait_ge(s_fh, g.at(1, 1))
                TTn(flo[:, bass.ds(g.at(2), 2), :], ff[:, :, :], fhi[:, bass.ds(g.at(2), 2), :].bitcast(F32), ALU.subtract).then_inc(s_fl, 1)

            def up_group(g):
                for s in range(4 if g.first else 0, 8):
                    lo("up", g, s)
                    if not g.first and s in (2, 4, 6):
                        (up_taps if s == 2 else up_f if s == 4 else up_lo)(g.prev())

            last = over(dve, 22, up_group)
            up_taps(last)
            up_f(last)
            up_lo(last)
            residual("down", 80, s_evd)
            dve.wait_ge(s_evd, 4)
            norm_x(2)
            own.wait()
            for q in range(4):
                k4 = slice(4 * q, 4 * q + 4)
                TTn(sq[:, k4, :], sq[:, k4, :], bc(pcol("normf_g")[:, k4].unsqueeze(2), [P, 4, T]), ALU.mult).then_inc(s_hn, 1)
            for b in range(11):
                dve.wait_ge(s_nct, b + 1)
                dve.tensor_copy(ncn[:, b * 512:(b + 1) * 512], pbank(b % 8)[0:2 + 2 * NB, :]).then_inc(s_ncn, 1)
            for b in range(12):
                mt, q = b // 4, b % 4
                w = M_ROWS[mt]
                dve.wait_ge(s_yt, b + 1)
                dve.tensor_copy(ynat[0:w, mt, q * 512:(q + 1) * 512], pbank((b + 11) % 8)[0:w, :]).then_inc(s_yev, 1)

        @block.tensor
        def _(pe):
            m = NB * TS

            def mm(out, lhsT, rhs, start=True, stop=True, **k):
                return pe.matmul(out, lhsT, rhs, start=start, stop=stop, **k)

            def carry_wait():
                pe.sem_inc(s_carry, 1)

            pe.wait_ge(s_cst, 48)
            pe.wait_ge(s_dve, 2)
            for bi, (kind, at_) in enumerate(banks):
                dst = pbank(bi % 8)
                if bi >= 8:
                    pe.wait_ge(s_tev, bi - 8 if bi - 8 > 1 else 1)
                    if bi == 9:
                        pe.wait_ge(s_silu, 1)
                if kind == "par":
                    pe.wait_ge(s_par, 16 * (len(PARAM_ROWS) + 1))
                    for t in range(4):
                        i = pe.transpose(dst[:, t * P:(t + 1) * P], prow[:, t, :], ident)
                elif kind == "c":
                    for k in range(KD):
                        i = pe.transpose(dst[:, k * NC:(k + 1) * NC], cnat[:, k * P:(k + 1) * P], ident[0:NC, 0:NC])
                elif kind == "sh":
                    pe.wait_ge(s_sh, 32)
                    for k in range(ZT):
                        i = pe.transpose(dst[:, k * NB:(k + 1) * NB], shnat[:, k * P:(k + 1) * P], ident[0:NB, 0:NB])
                elif kind == "x":
                    mt, q = at_
                    w = M_ROWS[mt]
                    if mt == 0 and q == 0:
                        pe.wait_ge(s_x, 48)
                    for t in range(4):
                        k = 4 * q + t
                        i = pe.transpose(dst[:, t * P:t * P + w], xnat[0:w, mt, k * P:(k + 1) * P], ident[0:w, 0:w])
                else:
                    for t in range(22):
                        k = 22 * at_ + t
                        i = pe.transpose(dst[:, t * 2 * NB:(t + 1) * 2 * NB], cvnat[:, k * P:(k + 1) * P], ident[0:2 * NB, 0:2 * NB])
                i.then_inc(s_tp, 1)

            pe.wait_ge(s_tev, len(banks) - 1)
            pe.wait_ge(s_silu, 1)

            def ada_slab(n, k, bank):
                for kt in range(2):
                    i = mm(pbank(bank)[0:NC, :], scT[:, 2 * k + kt, :], raw[:, k % 4, kt, :], k == 0 and kt == 0,
                           k == ADA_K - 1 and kt == 1)
                i.then_inc(s_ada, 1)

            def ada_turn(n, bank):
                pe.wait_ge(s_adr, n)
                if not isinstance(n, int):
                    carry_wait()
                for q in range(4):
                    i = pe.transpose(pbank(bank)[:, q * NC:(q + 1) * NC], adr[:, q * P:(q + 1) * P], ident[0:NC, 0:NC])
                i.then_inc(s_adt, 1)

            def norm(u):
                for k in range(KD):
                    if k % 4 == 0:
                        pe.wait_ge(s_sq, 4 * u + k // 4 + 1)
                    i = mm(pbank(0)[:, 0:T], c("mean"), sq[:, k, :], k == 0, k == KD - 1)
                i.then_inc(s_ssq, 1)

            norm(0)
            for g in range(ADA_1):
                if g > 1:
                    pe.wait_ge(s_adaev, g - 1)
                for k in range(ADA_K):
                    pe.wait_ge(s_raw[k % 4], 16 * (2 * g + k // 4 + 1))
                    ada_slab(g * ADA_K + k, k, 1 + g % 2)
                    if k == 1 and g:
                        ada_turn(g, 3 + (g - 1) % 2)
            ada_turn(ADA_1, 3 + (ADA_1 - 1) % 2)
            pe.wait_ge(s_adaev, ADA_1)

            def products(name, g, s0, ks, b4, hi_, lo_, nt=4, off=0):
                n0, per, _ = stages[name]
                for s in range(ks):
                    n = n0 + per * g.c + s0 + s
                    pe.wait_ge(s_lo, g.at(per, n0 + s0 + s + 1))
                    if g.first and name in ("za", "up") and s % 2 == 0:
                        pe.wait_ge(s_hlo, (4 if name == "up" else 0) + s // 2 + 1)
                    for kt in range(2):
                        k = 2 * s + kt
                        for q in range(nt):
                            w = slice(q * P, (q + 1) * P)
                            out = ps[:, b4 + q, 0:T]
                            mm(out, whi[:, n % 2, kt, w], hi_[:, k, :], k == 0, False)
                            mm(out, whi[:, n % 2, kt, w], lo_[:, k, :], False, False)
                            i = mm(out, wlo[:, n % 2, kt, w], hi_[:, k, :], False, k == 2 * ks - 1)
                    i.then_inc(s_mm, 1)

            def stage(name, hi_, lo_, done, base=0, before=None):
                _, ks, ng = stages[name]

                def group(g):
                    if not g.first:
                        if not (g.i is None and g.c < 2):
                            pe.wait_ge(done, g.at(1, base - 1))
                    products(name, g, 0, ks, 4 * g.parity, hi_, lo_, 3 if name == "za" and g.i is None and g.c == 6 else 4)
                over(pe, ng, group)
                pe.wait_ge(done, base + ng)

            stage("za", hhi, hlo, s_evz)
            pe.wait_ge(s_nsh, 1)
            for b in range(7):
                for k in range(4 * b, min(4 * b + 4, ZT)):
                    i = pe.transpose(pbank(b)[0:NC, (k % 4) * P:(k % 4 + 1) * P], nsh[:, k, :], ident)
                i.then_inc(s_nst, 1)
            pe.wait_ge(s_nse, 7)
            pe.wait_ge(s_lin2, 1)

            def ada(j, s):
                if s == 0:
                    pe.wait_ge(s_adaev, 2 * j + ADA_1)
                if s == ADA_K:
                    pe.wait_ge(s_adaev, 2 * j + (ADA_1 + 1))
                k, n = s % ADA_K, ADA_1 * ADA_K + stages["za"][1] * stages["za"][2] + s
                pe.wait_ge(s_raw[k % 4], j * (ADA_J * 4) + 16 * (n // 4 + 1))
                ada_slab(None, k, 7)

            with pe.Fori(0, KA) as j:
                pe.wait_ge(s_gr, j)
                pe.wait_ge(s_stp, j)
                pe.wait_ge(s_sto, 2 * j)
                pe.wait_ge(s_lora, j * 64 + 64)
                mm(pbank(0)[:, 0:T], lora[0:LORA_W, 0, :], lw[0:LORA_W, :])
                mm(pbank(1)[:, 0:T], lora[LORA_W:P, 0, :], lw[LORA_W:P, :])
                mm(pbank(2)[:, 0:T], lora[:, 1, :], lsg[:, 0, :], True, False)
                mm(pbank(2)[:, 0:T], lora[0:LORA_G - P, 2, :], lsg[0:LORA_G - P, 1, :], False, True).then_inc(s_lmm, 1)
                ada(j, 0)
                pe.wait_ge(s_kkq, j + 1)
                mm(pbank(3)[:, 0:T], c("head"), v_sq[:, :]).then_inc(s_kkp, 1)
                ada(j, 1)
                pe.wait_ge(s_ld, j + 1)
                pe.transpose(pbank(4)[:, 0:P], v_ld[:, 0:P], ident)
                pe.transpose(pbank(4)[:, P:2 * P], v_ld[:, P:2 * P], ident)
                pe.transpose(pbank(4)[0:m, 2 * P:3 * P], v_ld[:, TP:T], ident).then_inc(s_ldt, 1)
                ada(j, 2)
                pe.wait_ge(s_ldn, j + 1)
                for b, cum, cum4 in ((5, "cumx", "lt4"), (6, "cumi", "le4")):
                    for ck in range(2):
                        mm(pbank(b)[:, ck * P:(ck + 1) * P], ldn[:, ck, :], c(cum))
                    i = mm(pbank(b)[:, TP:T], ldn[0:m, 2, :], c(cum4, m))
                i.then_inc(s_cum, 1)
                ada(j, 3)
                pe.wait_ge(s_rkk, j + 1)
                pe.wait_ge(s_kkr, j + 1)
                mm(pbank(3)[:, 0:T], c("head"), v_sq[:, :]).then_inc(s_bon, 1)
                ada(j, 4)
                pe.wait_ge(s_dec, j + 1)
                v_ = rkv[:, 2, :]
                for ck in range(2):
                    pe.transpose(pbank(0)[:, ck * P:(ck + 1) * P], v_[:, ck * P:(ck + 1) * P], ident)
                    pe.transpose(pbank(0)[:, (2 + ck) * P:(3 + ck) * P], v_k[:, ck * P:(ck + 1) * P], ident)
                    pe.transpose(pbank(1)[:, ck * P:(ck + 1) * P], v_b[:, ck * P:(ck + 1) * P], ident)
                for q, a in enumerate((v_, v_k[:, :], v_b[:, :])):
                    i = pe.transpose(pbank(4)[0:m, q * P:(q + 1) * P], a[:, TP:T], ident)
                i.then_inc(s_tr, 1)
                pe.wait_ge(s_g, j + 1)
                pe.wait_ge(s_bonv, j + 1)
                r_ = rkv[:, 0, :]
                carry_wait()
                for e in range(2):
                    f = slice(64 * e, 64 * e + 64)
                    for b, right in ((2 + e, v_kk), (5 + e, r_)):
                        for a, left in enumerate((v_k, v_b)):
                            for ck in range(2):
                                t = slice(ck * P, (ck + 1) * P)
                                mm(pbank(b)[:, (2 * a + ck) * P:(2 * a + ck + 1) * P], left[f, t], right[f, t])
                pe.wait_ge(s_vkb, j + 1)
                carry_wait()
                for e in range(2):
                    f = slice(64 * e, 64 * e + 64)
                    dst = pbank(4 * e)[0:m, 3 * e * P:(3 * e + 1) * P]
                    for a, (left, right) in enumerate(((v_k, v_kk), (v_b, v_kk), (v_k, r_), (v_b, r_))):
                        i = mm(dst[:, 32 * a:32 * a + 32], left[f, TP:T], right[f, TP:T])
                i.then_inc(s_mat, 1)
                ada(j, 5)
                ada(j, 6)
                for lev in range(LEVELS):
                    pe.wait_ge(s_et, j * LEVELS + lev + 1)
                    if lev:
                        pe.wait_ge(s_T, j * N_T + (2 * lev - 2 if lev > 1 else 1))
                    b = lev % 2
                    for e in range(2):
                        for ck in range(2):
                            p = 2 * e + ck
                            i = mm(pbank(0)[:, p * P:(p + 1) * P], ET[:, b, e, ck, :], Tn[:, e, ck, :] if lev else ident)
                        if lev < 2:
                            i = mm(pbank(3)[0:m, 32 * e:32 * e + 32], ETs[:, lev, e, :], Tns[:, e, :] if lev else ident[0:m, 0:m])
                    i.then_inc(s_X, 1)
                    if lev == 0:
                        ada(j, 7)
                        continue
                    if lev == ADA_ROWS1 + 1:
                        ada_turn(2 * j + (ADA_1 + 1), 7)
                    if lev > ADA_ROWS1 + 1:
                        ada(j, ADA_K + 2 * (lev - ADA_ROWS1 - 2))
                    pe.wait_ge(s_Xe, j * (LEVELS - 1) + lev)
                    pe.wait_ge(s_T, j * N_T + 2 * lev - 1)
                    quarters = [(e, ck) for e in range(2) for ck in range(2)]
                    if lev < LEVELS - 1:
                        for p, (e, ck) in enumerate(quarters):
                            i = mm(pbank(1)[:, p * P:(p + 1) * P], TT[:, e, ck, :], Xs[:, e, ck, :])
                        i.then_inc(s_XT, 1)
                    for p, (e, ck) in enumerate(quarters):
                        i = mm(pbank(2)[:, p * P:(p + 1) * P], Xs[:, e, ck, :], TT[:, e, ck, :])
                    if lev == 1:
                        for e in range(2):
                            i = mm(pbank(3)[0:m, 128 + 32 * e:160 + 32 * e], Xss[:, e, :], TTs[:, e, :])
                    i.then_inc(s_XT, 1)
                    if lev > ADA_ROWS1 + 1:
                        if lev < LEVELS - 1:
                            ada(j, ADA_K + 2 * (lev - ADA_ROWS1 - 2) + 1)
                pe.wait_ge(s_s0, j * (16 * NB) + 16 * NB)
                pe.wait_ge(s_T, j * N_T + N_T)
                carry_wait()
                for b in range(NB):
                    i = pe.transpose(pbank(2)[:, b * 64:b * 64 + 64], s0n[:, b, :, :].rearrange("p h k -> p (h k)"), ident[0:64, 0:64])
                i.then_inc(s_s0t, 1)
                pe.wait_ge(s_am, 8 * j + 8)
                E = [slice(0, 64), slice(64, P)]

                def right_sides(ck):
                    t = slice(ck * P, (ck + 1) * P)
                    for e in range(2):
                        dst = pbank(5)[:, E[e]] if ck == 0 else pbank(5 + e)[:, 0:64]
                        i = mm(dst, Am[:, e, 0, ck, :], VN[:, ck, E[e]], True, ck == 0)
                        if ck:
                            i = mm(dst, v_kk[E[e], t], S1[E[e], :], False, True)
                    i.then_inc(s_m, 1)

                def solve(ck):
                    pe.wait_ge(s_me, 2 * j + ck + 1)
                    carry_wait()
                    for e in range(2):
                        i = mm(pbank(0)[:, E[e]], TT[:, e, ck, :], Ms[:, E[e]])
                    i.then_inc(s_u, 1)

                def results(ck):
                    t = slice(ck * P, (ck + 1) * P)
                    pe.wait_ge(s_ue, 2 * j + ck + 1)
                    for e in range(2):
                        st = pbank(4)[E[e], ck * 64:ck * 64 + 64]
                        mm(st, KN[:, ck, E[e]], VN[:, ck, E[e]], True, False)
                        i = mm(st, BN[:, ck, E[e]], Us[:, E[e]], False, True)
                    i.then_inc(s_y, 1)
                    for e in range(2):
                        y = pbank(3)[E[e], t]
                        mm(y, VN[:, ck, E[e]], Rm[:, e, 0, ck, :], True, False)
                        i = mm(y, Us[:, E[e]], Rm[:, e, 1, ck, :], False, ck == 0)
                        if ck:
                            i = mm(y, S1[E[e], :], r_[E[e], t], False, True)
                    return i

                right_sides(0)
                pe.wait_ge(s_s0e, j + 1)
                carry_wait()
                for e in range(2):
                    mt = pbank(1 + e)[E[e], P:P + m]
                    for b in range(NB):
                        mm(mt[:, 4 * b:4 * b + 4], s0T[E[e], b, :], v_kk[E[e], TP + 4 * b:TP + 4 * b + 4], b == 0, False,
                           skip_group_check=True)
                    i = mm(mt, VN[0:m, 2, E[e]], As[:, e, 0, :], False, True, skip_group_check=True)
                i.then_inc(s_mt, 1)
                solve(0)
                pe.wait_ge(s_mte, j + 1)
                pe.transpose(pbank(1)[0:m, 0:P], MTs[:, :], ident).then_inc(s_mst, 1)
                results(0)
                pe.wait_ge(s_mse, j + 1)
                carry_wait()
                for e in range(2):
                    i = mm(pbank(2)[0:m, 64 * e:64 * e + 64], TTs[:, e, :], Mss[:, E[e]])
                i.then_inc(s_us, 1)
                pe.wait_ge(s_s1, j + 1)
                right_sides(1)
                pe.wait_ge(s_use, j + 1)
                carry_wait()
                for e in range(2):
                    y = pbank(3)[E[e], TP:T]
                    for b in range(NB):
                        mm(y[:, 4 * b:4 * b + 4], s0T[E[e], b, :], r_[E[e], TP + 4 * b:TP + 4 * b + 4], b == 0, False,
                           skip_group_check=True)
                    mm(y, VN[0:m, 2, E[e]], As[:, e, 2, :], False, False, skip_group_check=True)
                    i = mm(y, Uss[:, E[e]], As[:, e, 3, :], False, True, skip_group_check=True)
                solve(1)
                pe.wait_ge(s_blk, j + 1)
                for e in range(2):
                    st = pbank(1)[E[e], :]
                    mm(st, KN[0:m, 2, E[e]], Vblk[:, e, :, :].rearrange("p b v -> p (b v)"), True, False)
                    i = mm(st, BN[0:m, 2, E[e]], Ublk[:, e, :, :].rearrange("p b v -> p (b v)"), False, True)
                i.then_inc(s_ss, 1)
                results(1).then_inc(s_ys, 1)
                ada(j, 13)
                pe.wait_ge(s_se, j + 1)
                carry_wait()
                pe.transpose(pbank(2)[0:64, 0:P], SE[:, :], ident).then_inc(s_set, 1)
                pe.wait_ge(s_ses, j + 1)
                carry_wait()
                for b in range(NB):
                    i = pe.transpose(pbank(5 + b // 4)[0:64, (b % 4) * P:(b % 4 + 1) * P], endS[:, b, :], ident)
                    if b % 4 == 3:
                        i.then_inc(s_sst, 1)
                pe.wait_ge(s_yc, j + 1)
                mm(pbank(0)[:, 0:T], c("head"), v_thw[:, :]).then_inc(s_gm, 1)
                ada(j, 14)
                pe.wait_ge(s_gv, j + 1)
                mm(pbank(0)[:, 0:T], c("head"), v_sq[:, :]).then_inc(s_gq, 1)
                ada(j, 15)
                ada_turn(2 * j + (ADA_1 + 2), 7)

            pe.wait_ge(s_yal, KA)
            pe.wait_ge(s_sto, 2 * KA)
            pe.wait_ge(s_stp, KA)
            stage("qkv", hhi, hlo, s_evq)

            def rotate(h):
                pe.wait_ge(s_rope, h)
                mm(pbank(0)[:, 0:T], c("rot"), qkv[:, one(h), :].rearrange("p o t -> p (o t)"))
                mm(pbank(1)[:, 0:T], c("rot"), qkv[:, one(h, off=HB), :].rearrange("p o t -> p (o t)")).then_inc(s_rot, 1)

            def head_scores(h):
                pe.wait_ge(s_rope, h + 1)
                pe.wait_ge(s_vt, h + 1)
                pe.wait_ge(s_vnh, h)
                for b, a in ((2, kr), (3, vT)):
                    pe.transpose(pbank(b)[:, 0:P], a[:, 0:P], ident)
                    pe.transpose(pbank(b)[:, P:2 * P], a[:, P:2 * P], ident)
                    i = pe.transpose(pbank(b)[0:m, 2 * P:3 * P], a[:, TP:T], ident)
                i.then_inc(s_kvt, 1)
                pe.wait_ge(s_new, h)
                mm(pbank(4)[:, 0:P], qr[:, 0:P], kr[:, 0:P])
                mm(pbank(5)[:, 0:TP], qr[:, P:TP], kr[:, 0:TP])
                mm(pbank(7)[0:m, 0:m], kr[:, TP:T], qr[:, TP:T]).then_inc(s_sc, 1)

            def head_out(h):
                pe.wait_ge(s_prn, h + 1)
                pe.wait_ge(s_evh, h)
                for q in range(3):
                    i = pe.transpose(pbank(6)[:, q * P:(q + 1) * P], prob[:, q, :], ident)
                i.then_inc(s_prt, 1)
                pe.wait_ge(s_pt2, h + 1)
                pe.wait_ge(s_vnh, h + 1)
                mm(pbank(6)[:, 0:P], vnh[:, 0, :], pT[:, 0, :])
                mm(pbank(6)[:, P:TP], vnh[:, 0, :], pT[:, 1, :], True, False)
                mm(pbank(6)[:, P:TP], vnh[:, 1, :], pT[:, 2, :], False, True).then_inc(s_o, 1)

            def head_first():
                rotate(0)
                head_scores(0)
                rotate(1)

            def head(h, last=False):
                head_scores(h)
                if not last:
                    rotate(h + 1)
                head_out(h - 1)

            def head_last():
                head(HB - 1, True)
                head_out(HB - 1)

            heads(pe, head_first, head, head_last)
            pe.wait_ge(s_evh, HB)
            def keys(b, landed_, rest):
                def turn(p):
                    if p % 2 == 0:
                        pe.wait_ge(s_page[p // 2], landed_)
                    if p == 1:
                        rest()
                    for h in range(HB):
                        i = pe.transpose(pbank(2 * (p % 2) + h // 4)[:, (h % 4) * P:(h % 4 + 1) * P], kpage[:, p, h * P:(h + 1) * P], ident)
                    i.then_inc(s_kt, 1)

                qf = qz[:, :, :].rearrange("p h x -> p (h x)")
                turn(0)
                for p in range(NPG):
                    if p < NPG - 1:
                        turn(p + 1)
                    pe.wait_ge(s_kta, b * NPG + (p + 1))
                    for h in range(HB):
                        i = mm(ps[0:m, 4 + p // 4, (p % 4) * P:(p % 4 + 1) * P], qf[:, h * 32:h * 32 + 32], kT[:, p % 2, h, :], h == 0, h == HB - 1)
                    i.then_inc(s_ksc, 1)
                pe.transpose(pbank(3)[0:m, 0:m], Snew[:, :, :].rearrange("p h t -> p (h t)"), ident[0:m, 0:m]).then_inc(s_st, 1)

            def values(b, landed_):
                pe.wait_ge(s_pn2, b + 1)
                carry_wait()
                for p in range(NPG):
                    pe.transpose(pbank(0)[:, p * 32:p * 32 + 32], srow2[:, p * P:(p + 1) * P], ident[0:m, 0:m])
                pe.transpose(pbank(0)[0:m, NPG * 32:NPG * 32 + 32], srow2[:, PAST:], ident[0:m, 0:m]).then_inc(s_pt3, 1)
                pe.wait_ge(s_p3e, b + 1)
                for p in range(NPG):
                    if p % 2 == 0:
                        pe.wait_ge(s_page[p // 2], landed_)
                    for a in range(2):
                        i = mm(ps[0:m, 6 + a, :], PT2[:, p, :], kpage[:, p, a * CH:(a + 1) * CH], p == 0, False)
                    i.then_inc(s_pvu, 1)
                for a in range(2):
                    i = mm(ps[0:m, 6 + a, :], PT2[0:m, NPG, :], vns[:, 4 * a:4 * a + 4, :].rearrange("p h f -> p (h f)"), False, True)
                i.then_inc(s_pv, 1)
                pe.wait_ge(s_oc, b * 2 + 2)
                carry_wait()
                for h in range(HB):
                    i = pe.transpose(pbank(2)[:, h * 32:h * 32 + 32], osb[:, h * P:(h + 1) * P], ident[0:m, 0:m])
                i.then_inc(s_ot, 1)

            keys(0, 32, lambda: pe.wait_ge(s_q, 1))
            with pe.Fori(0, NB - 1) as b:
                def rest():
                    pe.wait_ge(s_pve, b)
                    pe.wait_ge(s_srow, b + 1)
                    pe.wait_ge(s_q, b + 2)
                keys(b + 1, b * 64 + 64, rest)
                values(b, b * 64 + 96)
            values(NB - 1, 32 * 2 * NB)

            pe.wait_ge(s_pve, 8)
            pe.wait_ge(s_evm, 1)
            with pe.Fori(0, 4) as i:
                g = G(1, i, 0)
                pe.wait_ge(s_evm, g.at(2))
                products("merge", g, 0, 8, 0, hhi, hlo)
                pe.wait_ge(s_evm, g.at(2, 1))
                products("merge", g, 8, 8, 4, hhi, hlo)
                pe.wait_ge(s_gate, g.at(2, 1))
                products("merge", g, 16, 4, 0, yahi, yalo)
                pe.wait_ge(s_gate, g.at(2, 2))
                products("merge", g, 20, 4, 4, ohi, olo)
            pe.wait_ge(s_evm, 9)
            pe.wait_ge(s_ml, 16)
            stage("out", mhi, mlo, s_ev_out)
            norm(1)
            stage("up", hhi, hlo, s_f)
            pe.wait_ge(s_fl, 22)
            stage("down", fhi, flo, s_evd)
            norm(2)
            pe.wait_ge(s_ncv, 22)
            pe.wait_ge(s_rms, 3)
            for b in range(11):
                if b >= 8:
                    pe.wait_ge(s_ncn, b - 7)
                for q in range(4):
                    i = pe.transpose(pbank(b % 8)[0:2 + 2 * NB, q * P:(q + 1) * P], newconv[:, 4 * b + q, :], ident)
                i.then_inc(s_nct, 1)
            for b in range(12):
                mt, q = b // 4, b % 4
                w = M_ROWS[mt]
                pe.wait_ge(s_hn, 8 + q + 1)
                pe.wait_ge(s_ncn, min(b + 4, 11))
                if b + 4 > 11:
                    pe.wait_ge(s_yev, b - 7)
                for t in range(4):
                    i = pe.transpose(pbank((b + 11) % 8)[0:w, t * P:(t + 1) * P], sq[:, 4 * q + t, mt * P:mt * P + w], ident)
                i.then_inc(s_yt, 1)


_INS = ['x_prompt', 'x_sample', 'cache_k', 'cache_v', 'state_wkv', 'state_shift', 'state_conv', 'page_table',
        'c_prompt', 'c_sample', 'w_ada', 'b_ada', 'norm1_g', 'w_in', 'mu_shift', 'rwkv_w0', 'rwkv_w2', 'rwkv_a0',
        'rwkv_a2', 'rwkv_g2', 'rwkv_kk', 'rwkv_ka', 'rwkv_rk', 'lnx_g', 'lnx_b', 'w_proj_a', 'w_proj_b', 'w_out',
        'norm2_g', 'w_up', 'conv_w', 'conv_b', 'w_down', 'normf_g']
_OUTS = [("y_prompt", (1, TP, D)), ("y_sample", (NB, TS, D)), ("k_prompt", (1, TP, HB, HEAD_B)),
         ("v_prompt", (1, TP, HB, HEAD_B)), ("wkv_prompt", (1, HA, HEAD_A, HEAD_A)), ("shift_prompt", (1, ZA)),
         ("conv_prompt", (1, 2, FF)), ("k_sample", (NB, TS, HB, HEAD_B)), ("v_sample", (NB, TS, HB, HEAD_B)),
         ("wkv_sample", (NB, HA, HEAD_A, HEAD_A)), ("shift_sample", (NB, ZA)), ("conv_sample", (NB, 2, FF))]


def kernel(**inputs):
    import concourse.bacc as _bacc
    from concourse.bass_utils import run_bass_kernel_spmd as _run

    nc = _bacc.Bacc("TRN2", target_bir_lowering=False, num_devices=1)
    arrays, d = {}, {}
    for name in _INS:
        a = np.ascontiguousarray(inputs[name])
        arrays[f"in_{name}"] = a
        d[name] = nc.dram_tensor(f"in_{name}", a.shape, mybir.dt.from_np(a.dtype), kind="ExternalInput").ap()
    consts, _cols = shape_constants()
    arrays["in_consts"] = consts
    d["consts"] = nc.dram_tensor("in_consts", consts.shape, F32, kind="ExternalInput").ap()
    for name, shape in _OUTS:
        d[name] = nc.dram_tensor(f"out_{name}", shape, F32, kind="ExternalOutput").ap()
    build(nc, d)
    r = _run(nc, [arrays], core_ids=[0])
    return tuple(r.results[0][f"out_{name}"] for name, _shape in _OUTS)
```

```python
from contextlib import ExitStack

import concourse.bass as bass
import numpy as np
from concourse import mybir

ALU = mybir.AluOpType
ACT = mybir.ActivationFunctionType
AX = mybir.AxisListType
F32 = mybir.dt.float32
F32R = mybir.dt.float32r
I32 = mybir.dt.int32

P = 128
D = 2048
KD = D // P
TP, NB, TS = 256, 8, 4
T = TP + NB * TS
NC = NB + 1
DA, HA, HEAD_A = 1024, 16, 64
DB, HB, HEAD_B = 1024, 8, 128
KA = DA // P
LORA_W, LORA_A, LORA_G = 64, 64, 160
ZA = 3 * DA + LORA_W + LORA_A + LORA_G
ZT = -(-ZA // P)
ZPAD = 1 + TP + NB * (TS + 1)
FF = 5632
KF = FF // P
PAST, PAGE = 1024, 128
NPG = PAST // PAGE
NBLK, BLK = 4, 256
ROW = PAST + NB * TS
EPAD = 2 + TP + NB * (TS + 2)
RMS_EPS, LNX_EPS, NEG = 1e-6, 64e-5, -1e30
DECAY = float(np.exp(-0.5))
SCALE = HEAD_B ** -0.5
CH = 512
LEVELS = 7


def shape_constants():
    cols, parts, n = {}, [], 0

    def add(name, a):
        nonlocal n
        full = np.zeros((P, a.shape[1]), np.float32)
        full[:a.shape[0]] = a
        cols[name] = (n, a.shape[1])
        parts.append(full)
        n += a.shape[1]

    s, t = np.arange(P)[:, None], np.arange(P)[None, :]
    add("ident", (s == t) * 1.0)
    add("mean", np.full((P, P), 1.0 / D))
    add("head", (s // HEAD_A == t // HEAD_A) * 1.0)
    add("rot", np.where(s == t + 64, -1.0, 0.0) + np.where(s == t - 64, 1.0, 0.0))
    add("lt", (s < t) * 1.0)
    add("le", (s <= t) * 1.0)
    add("nle", (s <= t) * -1.0)
    add("cumx", (s < t) * 1.0 - (s < 64))
    add("cumi", (s <= t) * 1.0 - (s < 64))
    for lev in range(LEVELS):
        b = 1 << lev
        add(f"lev{lev}", ((s // (2 * b) == t // (2 * b)) & ((s // b) % 2 == 0) & ((t // b) % 2 == 1)) * 1.0)
    s4, t4 = np.arange(NB * TS)[:, None], np.arange(NB * TS)[None, :]
    same = s4 // TS == t4 // TS
    add("lt4", (same & (s4 < t4)) * 1.0)
    add("lt4b", (same & (s4 < t4)) * 1.0)
    add("le4", (same & (s4 <= t4)) * 1.0)
    add("nle4", (same & (s4 <= t4)) * -1.0)
    add("seq", (s4 // TS == np.arange(NB)[None, :]) * 1.0)
    add("causal", np.where(t <= s, 0.0, NEG))
    add("own", np.where(same & (s4 <= t4), 0.0, NEG))
    half = HEAD_B // 2
    inv = np.float32(10000.0) ** (-np.arange(half, dtype=np.float32) / np.float32(half))
    pos = np.concatenate([np.arange(TP), np.tile(PAST + np.arange(TS), NB)]).astype(np.float32)
    ang = np.concatenate([inv, inv])[:, None].astype(np.float32) * pos[None, :]
    add("cos", np.cos(ang))
    add("sin", np.sin(ang))
    add("eps_rms", np.full((P, 1), RMS_EPS))
    add("eps_lnx", np.full((P, 1), LNX_EPS))
    return np.concatenate(parts, axis=1).astype(np.float32), cols


_, CCOLS = shape_constants()
NCONST = sum(w for _, w in CCOLS.values())

PARAM_ROWS = {
    "b_ada": (0, 0, 96), "norm1_g": (0, 96, 16), "norm2_g": (0, 112, 16),
    "normf_g": (1, 0, 16), "rwkv_w0": (1, 16, 8), "rwkv_a0": (1, 24, 8), "rwkv_kk": (1, 32, 8),
    "rwkv_ka": (1, 40, 8), "rwkv_rk": (1, 48, 8), "lnx_g": (1, 56, 8), "lnx_b": (1, 64, 8),
    "mu_shift": (1, 72, ZT), "conv_b": (2, 0, KF), "conv_w0": (2, 44, KF), "conv_w1": (3, 0, KF),
    "conv_w2": (3, 44, KF),
}


def build(nc, d):
    ctx = ExitStack()
    with ctx:
        def sem(name):
            return ctx.enter_context(nc.semaphore(name))

        base = -(-nc.sbuf_base // 32) * 32

        def at(name, shape, off, dt=F32):
            return nc.alloc_sbuf_tensor_at(name, shape, dt, offset=base + off)

        def size(*shape):
            n = 4
            for x in shape:
                n *= x
            return -(-n // 32) * 32

        o = 0
        cst = at("cst", [P, NCONST], o); o_cst = o; o += size(NCONST)
        par = at("par", [P, 4, P], o); o += size(4 * P)
        mod = at("mod", [P, 96, NC], o); o += size(96 * NC)
        xT = at("xT", [P, KD, T], o); o += size(KD * T)
        sconvT = at("sconvT", [P, KF, 2 * NB], o); o += size(KF * 2 * NB)
        newconv = at("newconv", [P, KF, 2 + 2 * NB], o); o += size(KF * (2 + 2 * NB))
        o_ring = o
        raw = at("raw", [P, 4, 2, CH], o); o += size(4 * 2 * CH)
        whi = at("whi", [P, 2, 2, CH], o, F32R); o += size(2 * 2 * CH)
        wlo = at("wlo", [P, 2, 2, CH], o, F32R); o += size(2 * 2 * CH)
        kpage = at("kpage", [P, NPG, HB * P], o_ring)
        assert size(NPG * HB * P) == o - o_ring
        za_ = o
        hhi = at("hhi", [P, KD, T], za_, F32R)
        hlo = at("hlo", [P, KD, T], za_ + size(KD * T), F32R)
        o += 2 * size(KD * T)
        zb = o
        o += 2 * size(KF * T)
        assert base + o <= nc.sbuf_usable_end, (base + o, nc.sbuf_usable_end)

        def c(name, rows=P):
            n, w = CCOLS[name]
            return cst[0:rows, n:n + w]

        def pcol(name):
            t, r, n = PARAM_ROWS[name]
            return par[:, t, r:r + n]

        ident = c("ident")

        zz = zb + size(ZT * ZPAD)
        za = at("za", [P, ZT, ZPAD], zb)
        xnat = at("xnat", [P, 3, D], zz)
        prow = at("prow", [P, 4, P], zz + size(3 * D))
        cnat = at("cnat", [NC, D], zz + size(3 * D) + 2048)
        shnat = at("shnat", [NB, ZT * P], za_)
        cvnat = at("cvnat", [2 * NB, FF], za_ + size(ZT * P))
        adr = at("adr", [NC, CH], zb + 96256)
        scT = at("scT", [P, KD, NC], zb + 98304)
        o_n = zb + 57344
        sqs = [at("sq0", [P, KD, T], o_n), at("sq1", [P, KD, T], zb + 79872), at("sq2", [P, KD, T], za_)]
        gsc = at("gsc", [P, KD, NC], o_n + size(KD * T))
        rms = at("rms", [P, T], o_n + size(KD * T) + size(KD * NC))
        rstd = at("rstd", [P, T], o_n + size(KD * T) + size(KD * NC) + size(T))
        nsh = at("nsh", [P, ZT, NC], o_n + size(KD * T) + size(KD * NC) + 2 * size(T))
        nshn = at("nshn", [NC, ZT * P], o_ring + size(4 * 2 * CH))
        assert ZT * P <= 8 * CH

        yahi = at("yahi", [P, KA, T], zb, F32R)
        yalo = at("yalo", [P, KA, T], zb + 4 * KA * ZPAD, F32R)
        o_h = zb + 2 * 4 * KA * ZPAD
        o_w = zz
        o = zz
        top = zb + 96256

        def nxt(name, shape, dt=F32):
            nonlocal o
            n = 1
            for x in shape[1:]:
                n *= x
            r = at(name, shape, o, dt)
            o += size(n)
            assert o <= top, name
            return r

        lw = nxt("lw", [P, T])
        lsg = nxt("lsg", [P, 2, T])
        lora = nxt("lora", [P, 3, P])
        s0n = nxt("s0n", [HEAD_A, NB, 2, HEAD_A])
        s0T = nxt("s0T", [P, NB, HEAD_A])
        o_dif = o
        dif = nxt("dif", [P, 3, ZPAD])
        endS = at("endS", [P, NB, HEAD_A], o_dif)
        rkv = nxt("rkv", [P, 3, T])
        v_thw = nxt("v_thw", [P, T])
        v_tha = nxt("v_tha", [P, T])
        v_g = nxt("v_g", [P, T])
        v_ld = nxt("v_ld", [P, T])
        v_px = nxt("v_px", [P, T])
        v_pi = nxt("v_pi", [P, T])
        v_pv = nxt("v_pv", [P, T])
        v_kk = nxt("v_kk", [P, T])
        v_sq = nxt("v_sq", [P, T])
        v_k = nxt("v_k", [P, T])
        v_b = nxt("v_b", [P, T])
        v_bon = nxt("v_bon", [P, T])
        ldn = nxt("ldn", [P, 3, P])
        smallc = nxt("smallc", [P, 32])
        midc = nxt("midc", [P, 4])
        Am = nxt("Am", [P, 2, 2, 2, P])
        o_rm = o
        Rm = nxt("Rm", [P, 2, 2, 2, P])
        stout = at("stout", [HEAD_A, NB, 2, HEAD_A], o_rm)
        o_et = o
        ET = nxt("ET", [P, 2, 2, 2, P])
        Vblk = at("Vblk", [NB * TS, 2, NB, HEAD_A], o_et)
        TT = nxt("TT", [P, 2, 2, P])
        o_tn = o
        Tn = nxt("Tn", [P, 2, 2, P])
        Xs = nxt("Xs", [P, 2, 2, P])
        Ublk = at("Ublk", [NB * TS, 2, NB, HEAD_A], o_tn)
        VN = nxt("VN", [P, 3, P])
        KN = nxt("KN", [P, 3, P])
        BN = nxt("BN", [P, 3, P])
        As = nxt("As", [NB * TS, 2, 4, 32])
        ETs = nxt("ETs", [NB * TS, 2, 2, 32])
        Tns = nxt("Tns", [NB * TS, 2, 32])
        TTs = nxt("TTs", [NB * TS, 2, 32])
        Xss = nxt("Xss", [NB * TS, 2, 32])
        Ms = nxt("Ms", [P, P])
        Us = nxt("Us", [P, P])
        S1 = nxt("S1", [P, HEAD_A])
        SE = nxt("SE", [P, HEAD_A])
        stp = nxt("stp", [HEAD_A, 2, HEAD_A])
        MTs = nxt("MTs", [P, 32])
        Mss = nxt("Mss", [NB * TS, P])
        Uss = nxt("Uss", [NB * TS, P])

        top = zb + 2 * size(KF * T)
        ohi = at("ohi", [P, KA, T], o_h, F32R)
        olo = at("olo", [P, KA, T], o_h + size(KA * T), F32R)
        o = o_h + 2 * size(KA * T)
        vT = nxt("vT", [P, T])
        qr = nxt("qr", [P, T])
        kr = nxt("kr", [P, T])
        qs = nxt("qs", [P, HB, NB * TS])
        knh = nxt("knh", [P, 3, P])
        vnh = nxt("vnh", [P, 3, P])
        o_w = o
        qkv = nxt("qkv", [P, 3 * HB, T])
        vns = nxt("vns", [NB * TS, HB, P])
        STo = nxt("STo", [NB * TS, NB, HB, TS])
        ptab = nxt("ptab", [1, NB * NPG], I32)
        of = nxt("of", [P, HB, T])
        srow = nxt("srow", [P, 3, P])
        prob = nxt("prob", [P, 3, P])
        pT = nxt("pT", [P, 3, P])
        rtmp = nxt("rtmp", [P, 2, T])
        sm = nxt("sm", [P, 2, 4])
        o = o_w
        kT = nxt("kT", [P, 2, HB, P])
        smg = nxt("smg", [NB * TS, 32])
        srow2 = nxt("srow2", [NB * TS, ROW])
        PT2 = nxt("PT2", [P, NPG + 1, 32])
        osb = nxt("osb", [NB * TS, HB * P])
        Snew = nxt("Snew", [NB * TS, HB, TS])
        qz = nxt("qz", [P, HB, HB * TS + TS])
        assert o <= o_w + size(3 * HB * T)

        o_m = o_h + 2 * size(KA * T)
        mhi = at("mhi", [P, KD, T], o_m, F32R)
        mlo = at("mlo", [P, KD, T], o_m + size(KD * T), F32R)
        o = o_m + 2 * size(KD * T)
        sga = nxt("sga", [P, 4, T])
        sgb = nxt("sgb", [P, 4, T])

        fhi = at("fhi", [P, KF, T], zb, F32R)
        flo = at("flo", [P, KF, T], zb + size(KF * T), F32R)
        o_f = o_cst + size(2 * P)
        ext = at("ext", [P, 2, EPAD], o_f)
        cv = at("cv", [P, 2, EPAD], o_f + size(2 * EPAD))
        gl = at("gl", [P, 2, T], o_f + 2 * size(2 * EPAD))
        rsd = at("rsd", [P, 4, NB * TS], o_f + 2 * size(2 * EPAD))
        ff = at("ff", [P, 2, T], o_f + 2 * size(2 * EPAD) + size(2 * T))
        assert o_f + 2 * size(2 * EPAD) + 2 * size(2 * T) <= o_cst + 4 * CCOLS["eps_rms"][0]
        ynat = at("ynat", [P, 3, D], zb + size(FF))
        ncn = at("ncn", [2 + 2 * NB, FF], zb)

        ps = ctx.enter_context(nc.psum_tensor("ps", [P, 8, 512], F32))

        def samp(ap):
            return ap.rearrange("p (b t) -> p b t", t=TS)

        def bc(ap, shape):
            return ap.to_broadcast(shape)

        consts_in = sem("consts_in")
        params_in = sem("params_in")
        x_in = sem("x_in")
        states_in = sem("states_in")
        zeroed = sem("zeroed")
        bank_turned = sem("bank_turned")
        bank_read = sem("bank_read")
        silu_done = sem("silu_done")
        carried = sem("carried")
        dve_done = sem("dve_done")
        slab_in = [sem(f"slab_in{r}") for r in range(4)]
        slab_hi = sem("slab_hi")
        slab_lo = sem("slab_lo")
        slab_used = sem("slab_used")
        ada_used = sem("ada_used")
        ada_copied = sem("ada_copied")
        ada_turned = sem("ada_turned")
        ada_in_mod = sem("ada_in_mod")
        squares_done = sem("squares_done")
        means_done = sem("means_done")
        rms_done = sem("rms_done")
        h_normed = sem("h_normed")
        normed_hi = sem("normed_hi")
        normed_lo = sem("normed_lo")
        za_in_sbuf = sem("za_in_sbuf")
        qkv_in_sbuf = sem("qkv_in_sbuf")
        out_added = sem("out_added")
        down_added = sem("down_added")
        gated_samples = sem("gated_samples")
        last_cols = sem("last_cols")
        last_turned = sem("last_turned")
        last_rows = sem("last_rows")
        outputs_out = sem("outputs_out")
        lora_in = sem("lora_in")
        lora_used = sem("lora_used")
        state_in = sem("state_in")
        state_turned = sem("state_turned")
        state_in_sbuf = sem("state_in_sbuf")
        pstate_rows = sem("pstate_rows")
        pstate_out = sem("pstate_out")
        sstate_rows = sem("sstate_rows")
        sstate_out = sem("sstate_out")
        lora_mixed = sem("lora_mixed")
        lora_acted = sem("lora_acted")
        diffs_done = sem("diffs_done")
        mixed = sem("mixed")
        kk_squares = sem("kk_squares")
        kk_sums = sem("kk_sums")
        kk_norms = sem("kk_norms")
        kk_unit = sem("kk_unit")
        decay_tanh = sem("decay_tanh")
        a_tanh = sem("a_tanh")
        gate_copied = sem("gate_copied")
        logdecay = sem("logdecay")
        logdecay_turned = sem("logdecay_turned")
        logdecay_rows = sem("logdecay_rows")
        cums_done = sem("cums_done")
        decays_done = sem("decays_done")
        bonus_in = sem("bonus_in")
        bonus_sums = sem("bonus_sums")
        bonus_done = sem("bonus_done")
        forms_decayed = sem("forms_decayed")
        rows_turned = sem("rows_turned")
        rows_done = sem("rows_done")
        pairs_done = sem("pairs_done")
        pairs_masked = sem("pairs_masked")
        et_done = sem("et_done")
        x_done = sem("x_done")
        x_in_sbuf = sem("x_in_sbuf")
        tx_done = sem("tx_done")
        t_done = sem("t_done")
        rhs_done = sem("rhs_done")
        rhs_in_sbuf = sem("rhs_in_sbuf")
        u_done = sem("u_done")
        u_in_sbuf = sem("u_in_sbuf")
        chunk_state = sem("chunk_state")
        mid_state = sem("mid_state")
        end_state = sem("end_state")
        end_turned = sem("end_turned")
        srhs_done = sem("srhs_done")
        srhs_in_sbuf = sem("srhs_in_sbuf")
        srhs_turned = sem("srhs_turned")
        srhs_rows = sem("srhs_rows")
        su_done = sem("su_done")
        su_in_sbuf = sem("su_in_sbuf")
        su_blocks = sem("su_blocks")
        sadd_done = sem("sadd_done")
        send_state = sem("send_state")
        send_turned = sem("send_turned")
        y_done = sem("y_done")
        y_copied = sem("y_copied")
        gn_means = sem("gn_means")
        gn_squares = sem("gn_squares")
        gn_vars = sem("gn_vars")
        gn_roots = sem("gn_roots")
        ya_done = sem("ya_done")
        ya_hi = sem("ya_hi")
        ya_lo = sem("ya_lo")
        rotated = sem("rotated")
        roped = sem("roped")
        v_copied = sem("v_copied")
        kv_turned = sem("kv_turned")
        k_rows = sem("k_rows")
        v_rows = sem("v_rows")
        kv_out = sem("kv_out")
        scores_done = sem("scores_done")
        scores_max = sem("scores_max")
        new_scores = sem("new_scores")
        probs_done = sem("probs_done")
        probs_normed = sem("probs_normed")
        probs_turned = sem("probs_turned")
        probs_cols = sem("probs_cols")
        head_done = sem("head_done")
        head_copied = sem("head_copied")
        pages_in = [sem(f"pages_in{r}") for r in range(NPG // 2)]
        keys_turned = sem("keys_turned")
        keys_in_sbuf = sem("keys_in_sbuf")
        page_scored = sem("page_scored")
        query_laid = sem("query_laid")
        seq_scored = sem("seq_scored")
        seq_selected = sem("seq_selected")
        seq_exp = sem("seq_exp")
        seq_normed = sem("seq_normed")
        seq_turned = sem("seq_turned")
        seq_cols = sem("seq_cols")
        values_used = sem("values_used")
        seq_done = sem("seq_done")
        seq_rows = sem("seq_rows")
        seq_out_turned = sem("seq_out_turned")
        seq_copied = sem("seq_copied")
        ob_hi = sem("ob_hi")
        gate_done = sem("gate_done")
        merge_read = sem("merge_read")
        merged = sem("merged")
        merged_hi_done = sem("merged_hi_done")
        merged_lo_done = sem("merged_lo_done")
        conv_in = sem("conv_in")
        conv_past = sem("conv_past")
        tap0_done = sem("tap0_done")
        tap1_done = sem("tap1_done")
        tap2_done = sem("tap2_done")
        gelu_done = sem("gelu_done")
        ffn_done = sem("ffn_done")
        ffn_hi = sem("ffn_hi")
        ffn_lo = sem("ffn_lo")
        newconv_done = sem("newconv_done")
        newconv_turned = sem("newconv_turned")
        newconv_rows = sem("newconv_rows")
        y_turned = sem("y_turned")
        y_rows = sem("y_rows")

        stages = {}
        n = 0
        for name, ks, groups in (("za", 8, 7), ("qkv", 8, 6), ("merge", 24, 4), ("out", 8, 4),
                                 ("up", 8, 22), ("down", 22, 4)):
            stages[name] = (n, ks, groups)
            n += ks * groups
            assert n % 4 == 0
        ADA_K, ADA_1, ADA_G = 8, 8, 24
        ADA_J = (ADA_G - ADA_1) // KA * ADA_K
        assert ADA_J == 16
        N_XT, N_T = 2 * LEVELS - 3, 2 * LEVELS - 2
        ADA_ROWS1 = 1

        banks = [("par", None), ("c", None), ("sh", None)] + [("x", (m, q)) for m in range(3) for q in range(4)] \
            + [("cv", q) for q in range(2)]
        M_ROWS = [P, P, NB * TS]

        block = ctx.enter_context(nc.Block())

        H = P // 2

        def half_blocks(ap, lev, odd):
            return ap.rearrange("p (n two t) -> p n two t", two=2, t=1 << lev)[:, :, odd, :]

        def one(h, n=1, step=1, off=0):
            return slice(h * step + off, h * step + off + n) if isinstance(h, int) else bass.ds(h * step + off, n)

        @block.sync
        def _(sp):
            sp.dma_start(cst[:, :], d["consts"]).then_inc(consts_in, 16)
            sp.dma_start(cnat[0:1, :], d["c_prompt"]).then_inc(consts_in, 16)
            sp.dma_start(cnat[1:NC, :], d["c_sample"]).then_inc(consts_in, 16)

            def slab(n, step, i, src, wait, carry=False):
                r = n % 4
                if wait is not None:
                    s, v = wait
                    sp.wait_ge(s, v)
                    if carry:
                        sp.sem_inc(carried, 1)
                sp.dma_start(raw[:, r, :, 0:src.shape[2]], src).then_inc(slab_in[r], 16)

            def wsrc(w, k0, col, n):
                return w[k0:k0 + 2 * P, bass.ds(col, n)].rearrange("(t p) n -> p t n", p=P)

            for s in range(4):
                slab(s, 0, 0, wsrc(d["w_ada"], s * 2 * P, 0, CH), None)
            sp.wait_ge(zeroed, 1)
            for name, (t, r, n) in PARAM_ROWS.items():
                dst = prow[r:r + n, t, :]
                if name == "mu_shift":
                    sp.dma_start(prow[r:r + n - 1, t, :], d[name][0:(n - 1) * P].rearrange("(r c) -> r c", c=P)).then_inc(params_in, 16)
                    w = ZA - (n - 1) * P
                    sp.dma_start(prow[r + n - 1:r + n, t, 0:w], d[name][(n - 1) * P:ZA].rearrange("(r c) -> r c", r=1)).then_inc(params_in, 16)
                elif name == "rwkv_rk":
                    sp.dma_start(dst, d[name].rearrange("(r a) c -> r (a c)", a=2)).then_inc(params_in, 16)
                elif name.startswith("conv_w"):
                    sp.dma_start(dst, d["conv_w"][int(name[-1]), :].rearrange("(r c) -> r c", c=P)).then_inc(params_in, 16)
                else:
                    sp.dma_start(dst, d[name].rearrange("(r c) -> r c", c=P)).then_inc(params_in, 16)
            sp.dma_start(shnat[:, 0:ZA], d["state_shift"]).then_inc(states_in, 16)
            sp.dma_start(cvnat[:, :], d["state_conv"].rearrange("b r f -> (b r) f")).then_inc(states_in, 16)
            for m in range(2):
                sp.dma_start(xnat[:, m, :], d["x_prompt"][0, m * P:(m + 1) * P, :]).then_inc(x_in, 16)
            sp.dma_start(xnat[0:NB * TS, 2, :], d["x_sample"].rearrange("b t f -> (b t) f")).then_inc(x_in, 16)
            for s in range(4, ADA_K):
                slab(s, 0, 0, wsrc(d["w_ada"], s * 2 * P, 0, CH), (ada_used, s - 3))
            with sp.Fori(1, ADA_1) as g:
                for s in range(ADA_K):
                    slab(s, ADA_K, g, wsrc(d["w_ada"], s * 2 * P, g * CH, CH), (ada_used, g * ADA_K + (s - 3)))

            def split_group(name, src, loop0=0, groups=None):
                n0, ks, _ = stages[name]
                with sp.Fori(loop0, groups) as g:
                    for s in range(ks):
                        slab(n0 + s, ks, g, src(g, s), (slab_lo, g * ks + (n0 + s - 3)))

            def za_src(g, s):
                return wsrc(d["w_in"], s * 2 * P, g * CH, CH)

            for s in range(8):
                slab(s, 0, 0, za_src(0, s), (ada_used, ADA_1 * ADA_K + (s - 3)) if s < 4 else (slab_lo, s - 3))
            split_group("za", za_src, 1, 6)
            n0 = stages["za"][0] + 48
            for s in range(8):
                slab(n0 + s, 0, 0, wsrc(d["w_in"], s * 2 * P, 6 * CH, 3 * P), (slab_lo, n0 + s - 3))

            def pair_loads(j):
                cols, pair = (bass.ds(0, P), bass.ds(0, 2)) if j is None else (bass.ds(j * P + P, P), bass.ds(j * 2 + 2, 2))
                if j is not None:
                    sp.wait_ge(lora_used, j + 1)
                    sp.wait_ge(state_turned, j + 1)
                sp.dma_start(lora[0:LORA_W, 0, :], d["rwkv_w2"][:, cols]).then_inc(lora_in, 16)
                sp.dma_start(lora[LORA_W:P, 0, :], d["rwkv_a2"][:, cols]).then_inc(lora_in, 16)
                sp.dma_start(lora[:, 1, :], d["rwkv_g2"][0:P, cols]).then_inc(lora_in, 16)
                sp.dma_start(lora[0:LORA_G - P, 2, :], d["rwkv_g2"][P:LORA_G, cols]).then_inc(lora_in, 16)
                for b in range(NB):
                    sp.dma_start(s0n[:, b, :, :], d["state_wkv"][b, pair, :, :].rearrange("h v k -> v h k")).then_inc(state_in, 16)

            def ada_pair(j, s0, s1):
                for s in range(s0, s1):
                    src = wsrc(d["w_ada"], s % ADA_K * 2 * P, j * (2 * CH) + (ADA_1 + s // ADA_K) * CH, CH)
                    slab(s, 0, 0, src, (ada_used, j * ADA_J + (ADA_1 * ADA_K + s - 3)))

            pair_loads(None)
            sp.wait_ge(slab_lo, stages["za"][1] * stages["za"][2])
            sp.wait_ge(last_rows, 7)
            sp.dma_start(d["shift_prompt"], nshn[0:1, 0:ZA]).then_inc(outputs_out, 16)
            sp.dma_start(d["shift_sample"], nshn[1:NC, 0:ZA]).then_inc(outputs_out, 16)

            def pair_stores(j):
                sp.wait_ge(pstate_rows, j + 1)
                sp.dma_start(d["wkv_prompt"][0, one(j, 2, 2), :, :].rearrange("h v k -> v h k"), stp[:, :, :]).then_inc(pstate_out, 16)
                sp.wait_ge(sstate_rows, 2 * j + 2)
                for b in range(NB):
                    sp.dma_start(d["wkv_sample"][b, one(j, 2, 2), :, :].rearrange("h v k -> v h k"), stout[:, b, :, :]).then_inc(sstate_out, 16)

            with sp.Fori(0, 1) as j:
                ada_pair(j, 0, ADA_J)
                pair_loads(j)
            with sp.Fori(1, KA - 1) as j:
                ada_pair(j, 0, 6)
                pair_stores(j - 1)
                ada_pair(j, 6, ADA_J)
                pair_loads(j)
            with sp.Fori(KA - 1, KA) as j:
                ada_pair(j, 0, 6)
                pair_stores(j - 1)
                ada_pair(j, 6, ADA_J)

            n0 = stages["qkv"][0]

            def qkv_src(g, s):
                return wsrc(d["w_in"], s * 2 * P, g * CH + ZA, CH)

            for s in range(8):
                slab(n0 + s, 0, 0, qkv_src(0, s), (ada_used, ADA_G * ADA_K + (s - 3)) if s < 4 else (slab_lo, n0 + s - 3))
                if s == 3:
                    pair_stores(KA - 1)
            split_group("qkv", qkv_src, 1, 6)

            sp.dma_start(ptab[:, :], d["page_table"].rearrange("(o b) p -> o (b p)", o=1)).then_inc(states_in, 16)
            with sp.Fori(0, HB) as h:
                hh = bass.ds(h, 1)
                for nat, ready, po, so in ((knh, k_rows, "k_prompt", "k_sample"), (vnh, v_rows, "v_prompt", "v_sample")):
                    sp.wait_ge(ready, h + 1)
                    sp.dma_start(d[po][0, :, hh, :].rearrange("(c p) h f -> p c (h f)", p=P), nat[:, 0:2, :]).then_inc(kv_out, 16)
                    sp.dma_start(d[so][:, :, hh, :].rearrange("b t h f -> (b t) (h f)"), nat[0:NB * TS, 2, :]).then_inc(kv_out, 16)
            sp.wait_ge(states_in, 48)
            sp.wait_ge(slab_used, stages["merge"][0])

            def pages(cache, R, used, value):
                for p in range(NPG):
                    col = slice(R * NPG + p, R * NPG + p + 1) if isinstance(R, int) else bass.ds(R * NPG + p, 1)
                    page = sp.value_load(ptab[0:1, col], min_val=0, max_val=d[cache].shape[0] - 1)
                    if used is not None:
                        sp.wait_ge(used, value(p))
                    sp.dma_start(kpage[:, p, :], d[cache][bass.ds(page, 1), :, :, :].rearrange("o p h f -> p (o h f)")).then_inc(pages_in[p // 2], 16)

            pages("cache_k", 0, None, None)
            pages("cache_k", 1, keys_turned, lambda p: p + 1)
            pages("cache_v", 0, keys_turned, lambda p: NPG + p + 1)
            with sp.Fori(1, NB - 1) as b:
                pages("cache_k", b + 1, values_used, lambda p: b * NPG + (p - 7))
                pages("cache_v", b, keys_turned, lambda p: b * NPG + (NPG + p + 1))
            pages("cache_v", NB - 1, values_used, lambda p: (NB - 2) * NPG + p + 1)

            g0 = ZA + 3 * DB
            n0 = stages["merge"][0]
            sp.wait_ge(values_used, NB * NPG)
            with sp.Fori(0, 4) as g:
                parts = [(d["w_in"], g0, 8), (d["w_in"], g0 + D, 8), (d["w_proj_a"], 0, 4), (d["w_proj_b"], 0, 4)]
                s = 0
                for w, col, ks in parts:
                    for k in range(ks):
                        slab(n0 + s, 24, g, wsrc(w, k * 2 * P, g * CH + col, CH), (slab_lo, g * 24 + (n0 + s - 3)), s == 16)
                        s += 1
            split_group("out", lambda g, s: wsrc(d["w_out"], s * 2 * P, g * CH, CH), 0, 4)
            n0 = stages["up"][0]
            with sp.Fori(0, 22) as g:
                for s in range(8):
                    r = (n0 + s) % 4
                    sp.wait_ge(slab_lo, g * 8 + (n0 + s - 3))
                    for half in range(2):
                        sp.dma_start(raw[:, r, :, half * 256:half * 256 + 256],
                                     wsrc(d["w_up"], s * 2 * P, g * 256 + half * FF, 256)).then_inc(slab_in[r], 16)
            n0 = stages["down"][0]
            with sp.Fori(0, 2) as i:
                for gg in range(2):
                    for s in range(22):
                        q = gg * 22 + s
                        slab(n0 + q, 44, i, wsrc(d["w_down"], s * 2 * P, i * 1024 + gg * CH, CH), (slab_lo, i * 44 + (n0 + q - 3)))
            sp.wait_ge(newconv_rows, 11)
            sp.dma_start(d["conv_prompt"][0, :, :], ncn[0:2, :]).then_inc(outputs_out, 16)
            sp.dma_start(d["conv_sample"].rearrange("b r f -> (b r) f"), ncn[2:2 + 2 * NB, :]).then_inc(outputs_out, 16)
            for q in range(4):
                sp.wait_ge(y_rows, 3 * (q + 1))
                cols = slice(q * CH, (q + 1) * CH)
                for m in range(2):
                    sp.dma_start(d["y_prompt"][0, m * P:(m + 1) * P, cols], ynat[:, m, cols]).then_inc(outputs_out, 16)
                sp.dma_start(d["y_sample"][:, :, cols].rearrange("b t f -> (b t) f"), ynat[0:NB * TS, 2, cols]).then_inc(outputs_out, 16)
            sp.wait_ge(outputs_out, 16 * 16)
            sp.wait_ge(pstate_out, 16 * KA)
            sp.wait_ge(sstate_out, 16 * NB * KA)
            sp.wait_ge(kv_out, 64 * HB)


        def landed(name, g, s):
            n0, ks, _ = stages[name]
            up0 = stages["up"][0]
            n = n0 + ks * g.c + s
            before = (ADA_1 if name == "za" else ADA_G) * ADA_K
            v, per = 16 * (before // 4 + n // 4 + 1), 4
            if name == "up":
                v, per = v + 16 * ((n - up0) // 4 + 1), 8
            if name == "down":
                v += 16 * (stages["down"][0] - up0) // 4
            return v if g.i is None else g.i * (g.a * ks * per) + v

        class Chain:

            def __init__(self, eng, s):
                self.eng, self.s, self.base, self.n, self.i, self.per = eng, s, 0, 0, 0, 0

            def inc(self, ins):
                ins.then_inc(self.s, 1)
                self.n += 1

            def wait(self):
                self.eng.wait_ge(self.s, self.i * self.per + (self.base + self.n) if self.per else self.base + self.n)

            def __call__(self, ins):
                self.inc(ins)
                self.wait()

            def enter(self, i, per, i0=0):
                self.base, self.n, self.i, self.per, self.i0 = self.base + self.n - i0 * per, 0, i, per, i0

            def leave(self, trips):
                assert self.n == self.per, ("per", self.n)
                self.base, self.n, self.i, self.per = self.base + self.per * (trips + self.i0), 0, 0, 0

        def pbank(b):
            return ps[:, b, :]

        def heads(eng, first, body, last, own=None, per=0):
            first()
            with eng.Fori(1, HB - 1) as h:
                if own:
                    own.enter(h, per, 1)
                body(h)
            if own:
                own.leave(HB - 2)
            last()

        class G:

            def __init__(self, a, i, c):
                self.a, self.i, self.c = a, i, c
                self.parity = c % 2
                self.first = i is None and c == 0

            def at(self, k, plus=0):
                v = self.c * k + plus
                return v if self.i is None else self.i * (self.a * k) + v

            def prev(self):
                return G(self.a, self.i, self.c - 1)

        def over(eng, ng, body):
            body(G(0, None, 0))
            pairs = (ng - 1) // 2
            if pairs:
                with eng.Fori(0, pairs) as i:
                    body(G(2, i, 1))
                    body(G(2, i, 2))
            if (ng - 1) % 2:
                body(G(0, None, ng - 1))
            return G(0, None, ng - 1)

        def singles(eng, ng, body):
            body(G(0, None, 0))
            with eng.Fori(1, ng) as i:
                body(G(1, i, 0))
            return G(0, None, ng - 1)

        @block.gpsimd
        def _(pool):
            pool.wait_ge(za_in_sbuf, 7)
            pool.wait_ge(last_turned, 7)
            pool.wait_ge(lora_mixed, 2)
            zv = za[:, 0:3 * KA, :].rearrange("p (g j) c -> p g j c", g=3)
            with pool.Fori(0, KA) as j:
                jj = bass.ds(j, 1)
                pool.wait_ge(sadd_done, j)
                pool.wait_ge(send_turned, 2 * j)
                pool.wait_ge(mixed, j)
                pool.tensor_tensor(dif[:, :, 1:ZPAD], zv[:, :, jj, 0:ZPAD - 1].rearrange("p g j c -> p g (j c)"),
                                   zv[:, :, jj, 1:ZPAD].rearrange("p g j c -> p g (j c)"), ALU.subtract).then_inc(diffs_done, 1)
                pool.wait_ge(pairs_masked, 8 * j + 4)
                for lev in range(LEVELS):
                    b = lev % 2
                    if lev >= 2:
                        pool.wait_ge(x_done, j * LEVELS + (lev - 1))
                    if lev == 2:
                        pool.wait_ge(t_done, j * N_T + 1)
                    for e in range(2):
                        i = pool.tensor_tensor(ET[:, b, e, :, :], Am[:, e, 1, :, :],
                                               bc(c(f"lev{lev}").unsqueeze(1), [P, 2, P]), ALU.mult)
                        if lev < 2:
                            i = pool.tensor_tensor(ETs[:, lev, e, :], As[:, e, 1, :],
                                                   c(f"lev{lev}", 32)[:, 0:32], ALU.mult)
                    i.then_inc(et_done, 1)

            pool.wait_ge(bank_read, len(banks) - 1)
            with pool.Fori(0, KF // 2) as g:
                pool.wait_ge(tap2_done, 2 * g)
                e8 = ext[:, :, 2 + TP:EPAD].rearrange("p h (b t) -> p h b t", t=TS + 2)
                for h in range(2):
                    i = pool.tensor_copy(e8[:, h, :, 0:2], sconvT[:, bass.ds(g * 2 + h, 1), :].rearrange("p o (b r) -> p (o b) r", r=2))
                i.then_inc(conv_past, 1)
                pool.wait_ge(conv_in, g + 1)
                for h in range(2):
                    nv = newconv[:, bass.ds(g * 2 + h, 1), :].rearrange("p o c -> p (o c)")
                    pool.tensor_copy(nv[:, 0:2], ext[:, h, TP:TP + 2])
                    i = pool.tensor_copy(nv[:, 2:].rearrange("p (b r) -> p b r", r=2), e8[:, h, :, TS:TS + 2])
                i.then_inc(newconv_done, 1)

        @block.scalar
        def _(act):

            def copy(o, i, **k):
                return act.activation(o, i, ACT.Copy, **k)

            act.wait_ge(bank_turned, 2)
            act.activation(scT[:, :, :], pbank(1)[:, 0:KD * NC].rearrange("p (k c) -> p k c", c=NC), ACT.Silu).then_inc(silu_done, 1)

            def hi(name, g, s, width=CH):
                n0, ks, _ = stages[name]
                n = n0 + ks * g.c + s
                act.wait_ge(slab_in[n % 4], landed(name, g, s))
                if n >= 2:
                    act.wait_ge(slab_used, g.at(ks, n0 + s - 1))
                copy(whi[:, n % 2, :, 0:width], raw[:, n % 4, :, 0:width]).then_inc(slab_hi, 1)

            def squares(u, q):
                act.activation(sqs[u][:, one(q, 4, 4), :], xT[:, one(q, 4, 4), :], ACT.Square).then_inc(squares_done, 1)

            def first_slabs(name):
                for s in range(2):
                    hi(name, G(0, None, 0), s)

            def norm_sums(u):
                for q in range(0 if u == 0 else 3, 4):
                    squares(u, q)
                if u == 1:
                    first_slabs("up")
                act.wait_ge(means_done, u + 1)
                act.activation(rms[:, :], pbank(0)[:, 0:T], ACT.Sqrt, bias=c("eps_rms")).then_inc(rms_done, 1)

            def norm_hi(u, name):
                first = G(0, None, 0)
                for q in range(4):
                    act.wait_ge(h_normed, 4 * u + q + 1)
                    copy(hhi[:, 4 * q:4 * q + 4, :], sqs[u][:, 4 * q:4 * q + 4, :]).then_inc(normed_hi, 1)
                    if q in (1, 2):
                        hi(name, first, q + 1)

            def ada_rows(n, bank):
                act.wait_ge(ada_used, n * ADA_K + ADA_K)
                copy(adr[:, :], pbank(bank)[0:NC, :]).then_inc(ada_copied, 1)

            act.wait_ge(bank_read, 2 + 12)
            norm_sums(0)
            for g in range(ADA_1):
                if g:
                    act.wait_ge(ada_turned, g)
                ada_rows(g, 1 + g % 2)
            first_slabs("za")
            norm_hi(0, "za")

            def za_evac(g, n=4):
                b4 = 4 * g.parity
                act.wait_ge(slab_used, g.at(8, 8))
                zt = za[:, bass.ds(g.at(4), n), :]
                copy(zt[:, :, 1:1 + TP], ps[:, b4:b4 + n, 0:TP])
                for k in range(n):
                    i = copy(za[:, bass.ds(g.at(4, k), 1), 1 + TP:].rearrange("p o (b t) -> p (o b) t", t=TS + 1)[:, :, 1:],
                             samp(ps[:, b4 + k, TP:T]))
                i.then_inc(za_in_sbuf, 1)

            def za_group(g):
                for s in range(4 if g.first else 0, 8):
                    hi("za", g, s, 3 * P if g.i is None and g.c == 6 else CH)
                    if s == 1 and not g.first:
                        za_evac(g.prev())
            za_evac(over(act, 7, za_group), 3)
            act.wait_ge(lora_mixed, 2)
            act.activation(lw[0:LORA_W, :], rkv[0:LORA_W, 0, :], ACT.Tanh)
            copy(lw[LORA_W:P, :], rkv[LORA_W:P, 0, :])
            act.activation(lsg[:, :, :], rkv[:, 1:3, :], ACT.Sigmoid).then_inc(lora_acted, 1)
            for b in range(4, 7):
                w = min(4, ZT - 4 * b) * P
                act.wait_ge(last_turned, b + 1)
                copy(nshn[:, 4 * b * P:4 * b * P + w], pbank(b)[0:NC, 0:w]).then_inc(last_rows, 1)

            with act.Fori(0, KA) as j:
                jc = bass.ds(j, 1)
                w0h, a0h = smallc[:, bass.ds(j, 1)], smallc[:, bass.ds(j + 8, 1)]
                act.wait_ge(lora_used, j + 1)
                act.wait_ge(ya_lo, j)
                act.activation(v_thw[:, :], pbank(0)[:, 0:T], ACT.Tanh, bias=w0h, scale=0.5).then_inc(decay_tanh, 1)
                act.activation(v_tha[:, :], pbank(1)[:, 0:T], ACT.Tanh, bias=a0h, scale=0.5).then_inc(a_tanh, 1)
                copy(v_g[:, :], pbank(2)[:, 0:T]).then_inc(gate_copied, 1)
                act.wait_ge(kk_sums, j + 1)
                act.activation(v_pv[:, :], pbank(3)[:, 0:T], ACT.Sqrt).then_inc(kk_norms, 1)
                act.wait_ge(logdecay_turned, j + 1)
                copy(ldn[:, 0:2, :], pbank(4)[:, 0:2 * P].rearrange("p (c f) -> p c f", f=P))
                copy(ldn[0:NB * TS, 2, :], pbank(4)[0:NB * TS, 2 * P:3 * P]).then_inc(logdecay_rows, 1)
                act.wait_ge(cums_done, j + 1)
                act.activation(v_px[:, :], pbank(5)[:, 0:T], ACT.Exp)
                act.activation(v_pi[:, :], pbank(6)[:, 0:T], ACT.Exp)
                act.wait_ge(kk_unit, j + 1)
                act.activation(v_pv[:, :], pbank(6)[:, 0:T], ACT.Exp, scale=-1.0)
                act.activation(midc[:, 0:2], pbank(5)[:, 0:2 * P:P], ACT.Exp, scale=-1.0).then_inc(decays_done, 1)
                act.wait_ge(rows_turned, j + 1)
                m = NB * TS
                copy(VN[:, 0:2, :], pbank(0)[:, 0:2 * P].rearrange("p (c f) -> p c f", f=P))
                copy(KN[:, 0:2, :], pbank(0)[:, 2 * P:4 * P].rearrange("p (c f) -> p c f", f=P))
                copy(BN[:, 0:2, :], pbank(1)[:, 0:2 * P].rearrange("p (c f) -> p c f", f=P), scale=-1.0)
                copy(VN[0:m, 2, :], pbank(4)[0:m, 0:P])
                copy(KN[0:m, 2, :], pbank(4)[0:m, P:2 * P])
                copy(BN[0:m, 2, :], pbank(4)[0:m, 2 * P:3 * P], scale=-1.0).then_inc(rows_done, 1)
                for lev in range(1, LEVELS):
                    act.wait_ge(x_done, j * LEVELS + lev + 1)
                    i = copy(Xs[:, :, :, :], pbank(0).rearrange("p (e c t) -> p e c t", e=2, c=2))
                    if lev == 1:
                        i = copy(Xss[:, :, :], pbank(3)[0:m, 0:64].rearrange("p (e t) -> p e t", e=2))
                    i.then_inc(x_in_sbuf, 1)
                    if lev == ADA_ROWS1:
                        act.wait_ge(ada_turned, 2 * j + ADA_1)
                        act.wait_ge(ada_used, j * ADA_J + (ADA_1 + 1) * ADA_K)
                        copy(adr[:, :], pbank(7)[0:NC, :]).then_inc(ada_copied, 1)
                act.wait_ge(state_turned, j + 1)
                copy(s0T[:, :, :], pbank(2).rearrange("p (b v) -> p b v", b=NB)).then_inc(state_in_sbuf, 1)
                def right_sides(ck):
                    act.wait_ge(rhs_done, 2 * j + ck + 1)
                    if ck == 0:
                        copy(Ms[:, :], pbank(5)[:, 0:P]).then_inc(rhs_in_sbuf, 1)
                    else:
                        copy(Ms[:, 0:64], pbank(5)[:, 0:64])
                        copy(Ms[:, 64:P], pbank(6)[:, 0:64]).then_inc(rhs_in_sbuf, 1)

                def solved(ck):
                    act.wait_ge(u_done, 2 * j + ck + 1)
                    copy(Us[:, :], pbank(0)[:, 0:P]).then_inc(u_in_sbuf, 1)

                right_sides(0)
                act.wait_ge(srhs_done, j + 1)
                copy(MTs[0:64, :], pbank(1)[0:64, P:P + m])
                copy(MTs[64:P, :], pbank(2)[64:P, P:P + m]).then_inc(srhs_in_sbuf, 1)
                solved(0)
                act.wait_ge(srhs_turned, j + 1)
                copy(Mss[:, :], pbank(1)[0:m, 0:P]).then_inc(srhs_rows, 1)
                act.wait_ge(su_done, j + 1)
                copy(Uss[:, :], pbank(2)[0:m, 0:P]).then_inc(su_in_sbuf, 1)
                right_sides(1)
                solved(1)
                act.wait_ge(end_turned, j + 1)
                act.wait_ge(pstate_out, 16 * j)
                copy(stp[:, :, :], pbank(2)[0:64, 0:P].rearrange("p (h k) -> p h k", h=2)).then_inc(pstate_rows, 1)
                for h in range(2):
                    act.wait_ge(send_turned, 2 * j + h + 1)
                    act.wait_ge(y_done, j + 1)
                    act.wait_ge(sstate_out, 16 * NB * j)
                    copy(stout[:, 4 * h:4 * h + 4, :, :].rearrange("p b h k -> p (b h k)"), pbank(5 + h)[0:64, :]).then_inc(sstate_rows, 1)
                act.wait_ge(gn_vars, j + 1)
                act.activation(v_px[:, :], pbank(0)[:, 0:T], ACT.Sqrt, bias=c("eps_lnx"), scale=1.0 / HEAD_A).then_inc(gn_roots, 1)
                act.wait_ge(ada_turned, 2 * j + (ADA_1 + 1))
                act.wait_ge(ada_used, j * ADA_J + (ADA_1 + 2) * ADA_K)
                copy(adr[:, :], pbank(7)[0:NC, :]).then_inc(ada_copied, 1)
                act.wait_ge(ya_done, j + 1)
                act.activation(yahi[:, jc, :].rearrange("p o t -> p (o t)"), v_thw[:, :], ACT.Copy).then_inc(ya_hi, 1)

            def plain(name, u=None, added=None, ends={}):
                def group(g):
                    for s in range(stages[name][1]):
                        hi(name, g, s)
                        if g.first and s in ends:
                            ends[s]()
                        if s == 3 and added and not g.first:
                            act.wait_ge(added, g.at(1))
                            squares(u, g.at(1, -1))
                over(act, stages[name][2], group)

            act.wait_ge(outputs_out, 32)
            plain("qkv")

            m = NB * TS

            def v_tile(h):
                act.wait_ge(kv_turned, h)
                copy(vT[:, :], qkv[:, one(h, off=2 * HB), :].rearrange("p o t -> p (o t)")).then_inc(v_copied, 1)

            def kv_rows(h):
                act.wait_ge(kv_turned, h + 1)
                act.wait_ge(kv_out, 64 * h)
                act.wait_ge(head_done, h)
                copy(knh[:, 0:2, :], pbank(2)[:, 0:2 * P].rearrange("p (c f) -> p c f", f=P))
                copy(knh[0:m, 2, :], pbank(2)[0:m, 2 * P:3 * P]).then_inc(k_rows, 1)
                copy(vnh[:, 0:2, :], pbank(3)[:, 0:2 * P].rearrange("p (c f) -> p c f", f=P))
                copy(vnh[0:m, 2, :], pbank(3)[0:m, 2 * P:3 * P])
                copy(vns[:, one(h), :].rearrange("p o f -> p (o f)"), pbank(3)[0:m, 2 * P:3 * P]).then_inc(v_rows, 1)

            def head_exp(h):
                act.wait_ge(scores_max, h + 1)
                act.activation(prob[:, 0, :], srow[:, 0, :], ACT.Exp, bias=sm[:, 0, 0:1], accum_out=sm[:, 1, 0:1])
                act.activation(prob[:, 1:3, :], srow[:, 1:3, :], ACT.Exp, bias=sm[:, 0, 1:2], accum_out=sm[:, 1, 1:2]).then_inc(probs_done, 1)

            def head_pT(h):
                act.wait_ge(probs_turned, h + 1)
                copy(pT[:, :, :], pbank(6)[:, 0:3 * P].rearrange("p (c f) -> p c f", f=P)).then_inc(probs_cols, 1)

            def head_first():
                act.wait_ge(qkv_in_sbuf, 6)
                v_tile(0)
                kv_rows(0)
                head_exp(0)
                v_tile(1)

            def head(h, last=False):
                head_pT(h - 1)
                head_exp(h)
                if not last:
                    v_tile(h + 1)
                kv_rows(h)

            def head_last():
                head(HB - 1, True)
                head_pT(HB - 1)

            heads(act, head_first, head, head_last)

            m = NB * TS
            def keys(b):
                for p in range(NPG):
                    act.wait_ge(keys_turned, b * NPG + (p + 1))
                    act.wait_ge(page_scored, b * NPG + (p - 1 if p else 0))
                    copy(kT[:, p % 2, :, :].rearrange("p (a h) f -> p a (h f)", a=2), ps[:, 2 * (p % 2):2 * (p % 2) + 2, :]).then_inc(keys_in_sbuf, 1)

            def exps(b):
                act.wait_ge(seq_selected, b + 1)
                act.activation(srow2[:, :], srow2[:, :], ACT.Exp, bias=smg[:, 0:1], accum_out=smg[:, 1:2]).then_inc(seq_exp, 1)

            def outs(b):
                act.wait_ge(seq_done, b + 1)
                copy(osb[:, 0:CH], pbank(6)[0:m, :]).then_inc(seq_rows, 1)

            keys(0)
            with act.Fori(0, NB - 1) as b:
                exps(b)
                keys(b + 1)
                outs(b)
            exps(NB - 1)
            outs(NB - 1)
            act.wait_ge(seq_copied, 8)
            copy(ohi[:, :, :], of[:, :, :]).then_inc(ob_hi, 1)

            m0 = stages["merge"][0]

            def merged_hi(g):
                for q in range(4):
                    act.wait_ge(merged, g.at(4, q + 1))
                    copy(mhi[:, bass.ds(g.at(4, q), 1), :].rearrange("p o t -> p (o t)"), sga[:, q, :]).then_inc(merged_hi_done, 1)

            def merge(g):
                for s in range(24):
                    hi("merge", g, s)
                    if s == 2 and not g.first:
                        merged_hi(g.prev())
                    if s == 9:
                        act.wait_ge(slab_used, g.at(24, m0 + 8))
                        act.wait_ge(merged_lo_done, g.at(4))
                        act.activation(sga[:, :, :], ps[:, 0:4, 0:T], ACT.Sigmoid).then_inc(gate_done, 1)
                    if s == 17:
                        act.wait_ge(slab_used, g.at(24, m0 + 16))
                        act.activation(sgb[:, :, :], ps[:, 4:8, 0:T], ACT.Sigmoid).then_inc(gate_done, 1)

            last_merge = singles(act, 4, merge)
            plain("out", 1, out_added, {2: lambda: merged_hi(last_merge)})
            act.wait_ge(out_added, 4)
            norm_sums(1)
            norm_hi(1, "up")

            cb, w0 = pcol("conv_b"), pcol("conv_w0")

            def up_in(g):
                b4 = 4 * g.parity
                act.wait_ge(slab_used, g.at(8, stages["up"][0] + 8))
                act.wait_ge(tap2_done, g.at(2))
                act.wait_ge(newconv_done, g.at(1))
                copy(ext[:, :, 2:2 + TP], ps[:, b4:b4 + 2, 0:TP])
                for h in range(2):
                    e8 = ext[:, h, 2 + TP:EPAD].rearrange("p (b t) -> p b t", t=TS + 2)
                    i = copy(e8[:, :, 2:], samp(ps[:, b4 + h, TP:T]))
                i.then_inc(conv_in, 1)
                act.wait_ge(conv_in, g.at(1, 1))
                act.wait_ge(conv_past, g.at(1, 1))
                act.wait_ge(zeroed, 2)
                act.wait_ge(gelu_done, g.at(1))
                for h in range(2):
                    act.activation(cv[:, h, 0:EPAD - 2], ext[:, h, 0:EPAD - 2], ACT.Identity, bias=cb[:, bass.ds(g.at(2, h), 1)],
                                   scale=w0[:, bass.ds(g.at(2, h), 1)]).then_inc(tap0_done, 1)

            def up_gelu(g):
                act.wait_ge(tap2_done, g.at(2, 2))
                act.wait_ge(ffn_done, g.at(1))
                act.activation(gl[:, :, 0:TP], cv[:, :, 0:TP], ACT.Gelu_apprx_tanh)
                for h in range(2):
                    i = act.activation(samp(gl[:, h, TP:T]), cv[:, h, 2 + TP:EPAD].rearrange("p (b t) -> p b t", t=TS + 2)[:, :, 0:TS],
                                       ACT.Gelu_apprx_tanh)
                i.then_inc(gelu_done, 1)

            def up_hi(g):
                act.wait_ge(ffn_done, g.at(1, 1))
                copy(fhi[:, bass.ds(g.at(2), 2), :], ff[:, :, :]).then_inc(ffn_hi, 1)

            def up_group(g):
                for s in range(4 if g.first else 0, 8):
                    hi("up", g, s)
                    if not g.first and s in (1, 3, 5):
                        (up_in if s == 1 else up_gelu if s == 3 else up_hi)(g.prev())

            last = over(act, 22, up_group)
            plain("down", 2, down_added, {1: lambda: up_in(last), 3: lambda: up_gelu(last), 5: lambda: up_hi(last)})
            act.wait_ge(down_added, 4)
            norm_sums(2)
            for b in range(11):
                act.wait_ge(newconv_turned, b + 1)
                copy(ncn[:, b * CH:(b + 1) * CH], pbank(b % 8)[0:2 + 2 * NB, :]).then_inc(newconv_rows, 1)

        @block.vector
        def _(dve):
            own = Chain(dve, dve_done)
            TTn, STT, TS_ = dve.tensor_tensor, dve.scalar_tensor_tensor, dve.tensor_scalar
            m = NB * TS
            dve.memset(prow[:, :, :], 0.0).then_inc(zeroed, 1)
            own(dve.memset(shnat[:, ZA:], 0.0))
            own(dve.memset(za[:, :, 0:1], 0.0))
            for bi, (kind, at_) in enumerate(banks):
                src = pbank(bi % 8)
                if kind == "c":
                    continue
                dve.wait_ge(bank_turned, bi + 1)
                if kind == "par":
                    i = dve.tensor_copy(par[:, :, :], src.rearrange("p (t c) -> p t c", t=4))
                elif kind == "sh":
                    i = dve.tensor_copy(za[:, :, 1 + TP:ZPAD].rearrange("p k (b t) -> p k b t", t=TS + 1)[:, :, :, 0],
                                        src[:, 0:ZT * NB].rearrange("p (k b) -> p k b", b=NB))
                elif kind == "x":
                    mt, q = at_
                    w = M_ROWS[mt]
                    i = dve.tensor_copy(xT[:, 4 * q:4 * q + 4, mt * P:mt * P + w],
                                        src.rearrange("p (i t) -> p i t", i=4)[:, :, 0:w])
                else:
                    i = dve.tensor_copy(sconvT[:, 22 * at_:22 * at_ + 22, :],
                                        src[:, 0:22 * 2 * NB].rearrange("p (k b) -> p k b", b=2 * NB))
                i.then_inc(bank_read, 1)

            bada = pcol("b_ada")
            dve.wait_ge(bank_read, 1)

            def ada_cols(g, n, bank):
                dve.wait_ge(ada_turned, n)
                TTn(mod[:, bass.ds(g * 4, 4), :], pbank(bank)[:, 0:4 * NC].rearrange("p (q c) -> p q c", c=NC),
                    bc(bada[:, bass.ds(g * 4, 4)].unsqueeze(2), [P, 4, NC]), ALU.add).then_inc(ada_in_mod, 1)

            def lo(name, g, s, width=CH):
                n0, ks, _ = stages[name]
                n = n0 + ks * g.c + s
                dve.wait_ge(slab_hi, g.at(ks, n0 + s + 1))
                TTn(wlo[:, n % 2, :, 0:width], raw[:, n % 4, :, 0:width], whi[:, n % 2, :, 0:width].bitcast(F32),
                    ALU.subtract).then_inc(slab_lo, 1)

            def inverse_roots(u):
                dve.wait_ge(rms_done, u + 1)
                own(dve.reciprocal(rstd[:, :], rms[:, :]))

            def over_root(u, q):
                k4 = slice(4 * q, 4 * q + 4)
                return TTn(sqs[u][:, k4, :], xT[:, k4, :], bc(rstd[:, :].unsqueeze(1), [P, 4, T]), ALU.mult)

            def norm_h(u, gname, shift, scale, name):
                first = G(0, None, 0)
                for s in range(2):
                    lo(name, first, s)
                own(STT(gsc[:, :, :], mod[:, scale:scale + KD, :], 1.0,
                        bc(pcol(gname).unsqueeze(2), [P, KD, NC]), ALU.add, ALU.mult))
                if u:
                    inverse_roots(u)
                    own(over_root(u, 0))
                for q in range(4):
                    if u and q:
                        own.wait()
                    for k in range(4 * q, 4 * q + 4):
                        own.inc(TS_(sqs[u][:, k, 0:TP], sqs[u][:, k, 0:TP], gsc[:, k, 0:1], mod[:, shift + k, 0:1], ALU.mult, ALU.add))
                        own.inc(TTn(samp(sqs[u][:, k, TP:T]), samp(sqs[u][:, k, TP:T]), bc(gsc[:, k, 1:NC].unsqueeze(2), [P, NB, TS]), ALU.mult))
                    own.wait()
                    for k in range(4 * q, 4 * q + 4):
                        i = TTn(samp(sqs[u][:, k, TP:T]), samp(sqs[u][:, k, TP:T]), bc(mod[:, shift + k, 1:NC].unsqueeze(2), [P, NB, TS]), ALU.add)
                    i.then_inc(h_normed, 1)
                    if u and q < 3:
                        own.inc(over_root(u, q + 1))
                    if q:
                        norm_lo(u, q - 1)
                    if q > 1:
                        lo(name, first, q)
                norm_lo(u, 3)

            def norm_lo(u, q):
                k4 = slice(4 * q, 4 * q + 4)
                dve.wait_ge(normed_hi, 4 * u + q + 1)
                TTn(hlo[:, k4, :], sqs[u][:, k4, :], hhi[:, k4, :].bitcast(F32), ALU.subtract).then_inc(normed_lo, 1)

            inverse_roots(0)
            for q in range(4):
                own.inc(over_root(0, q))
            for g in range(ADA_1):
                ada_cols(g, g + 1, 3 + g % 2)
            dve.wait_ge(ada_in_mod, ADA_1)
            norm_h(0, "norm1_g", 0, KD, "za")

            def plain(name, evac, ends={}):
                ks = stages[name][1]

                def group(g):
                    for s in range(4 if g.first and name == "za" else 0, ks):
                        lo(name, g, s, 3 * P if name == "za" and g.i is None and g.c == 6 else CH)
                        if s == 1 and evac and not g.first:
                            evac(g.prev())
                        if g.first and s in ends:
                            ends[s]()
                last = over(dve, stages[name][2], group)
                if evac:
                    evac(last)

            plain("za", None)
            dve.wait_ge(za_in_sbuf, 7)
            own(dve.tensor_copy(nsh[:, :, 0:1], za[:, :, TP:TP + 1]))
            dve.tensor_copy(nsh[:, :, 1:NC], za[:, :, 1 + TP:].rearrange("p k (b t) -> p k b t", t=TS + 1)[:, :, :, TS]).then_inc(last_cols, 1)
            own.inc(TS_(smallc[:, 0:8], pcol("rwkv_w0"), 0.5, None, ALU.mult))
            own.inc(TS_(smallc[:, 8:16], pcol("rwkv_a0"), 0.5, None, ALU.mult))
            own.inc(TS_(smallc[:, 16:24], pcol("rwkv_ka"), 0.5, None, ALU.mult))
            own.inc(TS_(smallc[:, 24:32], pcol("rwkv_ka"), -0.5, 1.0, ALU.mult, ALU.add))
            own.wait()
            mu = pcol("mu_shift")

            def mix(dst, df, z, muc):
                STT(dst[:, 0:TP], df[:, 1:1 + TP], muc, z[:, 1:1 + TP], ALU.mult, ALU.add)
                dv, zv = (a[:, 1 + TP:ZPAD].rearrange("p (b t) -> p b t", t=TS + 1)[:, :, 1:] for a in (df, z))
                return STT(samp(dst[:, TP:T]), dv, muc, zv, ALU.mult, ALU.add)

            for q in range(3):
                z = za[:, 3 * KA + q, :]
                own(TTn(dif[:, q, 1:ZPAD], z[:, 0:ZPAD - 1], z[:, 1:ZPAD], ALU.subtract))
                i = mix(rkv[:, q, :], dif[:, q, :], z, mu[:, 3 * KA + q:3 * KA + q + 1])
                if q:
                    i.then_inc(lora_mixed, 1)
            for b in range(4):
                w = min(4, ZT - 4 * b) * P
                dve.wait_ge(last_turned, b + 1)
                dve.tensor_copy(nshn[:, 4 * b * P:4 * b * P + w], pbank(b)[0:NC, 0:w]).then_inc(last_rows, 1)
            dve.wait_ge(lora_acted, 1)

            def pc(name, j):
                return pcol(name)[:, bass.ds(j, 1)]

            with dve.Fori(0, KA) as j:
                own.enter(j, 19)
                r_, k_, v_ = rkv[:, 0, :], rkv[:, 1, :], rkv[:, 2, :]
                dve.wait_ge(diffs_done, j + 1)
                for q in range(3):
                    z = za[:, bass.ds(j + q * KA, 1), :].rearrange("p o t -> p (o t)")
                    i = mix(rkv[:, q, :], dif[:, q, :], z, mu[:, bass.ds(j + q * KA, 1)])
                i.then_inc(mixed, 1)
                dve.wait_ge(mixed, j + 1)
                own(TS_(v_kk[:, :], k_, pc("rwkv_kk", j), None, ALU.mult))
                TTn(v_sq[:, :], v_kk[:, :], v_kk[:, :], ALU.mult).then_inc(kk_squares, 1)
                dve.wait_ge(decay_tanh, j + 1)
                TS_(v_ld[:, :], v_thw[:, :], -0.5 * DECAY, -0.5 * DECAY, ALU.mult, ALU.add).then_inc(logdecay, 1)
                dve.wait_ge(a_tanh, j + 1)
                own(TS_(v_k[:, :], v_tha[:, :], smallc[:, bass.ds(j + 16, 1)], smallc[:, bass.ds(j + 24, 1)], ALU.mult, ALU.add))
                own(TTn(v_k[:, :], v_k[:, :], k_, ALU.mult))
                own(TS_(v_tha[:, :], v_tha[:, :], 0.5, 0.5, ALU.mult, ALU.add))
                dve.wait_ge(kk_sums, j + 1)
                STT(v_sq[:, :], r_, pc("rwkv_rk", j), v_k[:, :], ALU.mult, ALU.mult).then_inc(bonus_in, 1)
                dve.wait_ge(kk_norms, j + 1)
                own(TS_(v_pv[:, :], v_pv[:, :], 1e-12, None, ALU.max))
                own(dve.reciprocal(v_pv[:, :], v_pv[:, :]))
                TTn(v_kk[:, :], v_kk[:, :], v_pv[:, :], ALU.mult).then_inc(kk_unit, 1)
                dve.wait_ge(kk_unit, j + 1)
                own(TTn(v_b[:, :], v_kk[:, :], v_tha[:, :], ALU.mult))
                dve.wait_ge(bonus_sums, j + 1)
                TTn(v_bon[:, :], pbank(3)[:, 0:T], v_, ALU.mult).then_inc(bonus_done, 1)
                dve.wait_ge(decays_done, j + 1)
                own.inc(TTn(v_k[:, :], v_k[:, :], v_pv[:, :], ALU.mult))
                own.inc(TTn(v_b[:, :], v_b[:, :], v_pv[:, :], ALU.mult))
                own.inc(TTn(v_kk[:, :], v_kk[:, :], v_px[:, :], ALU.mult))
                own(TTn(r_, r_, v_pi[:, :], ALU.mult))
                TTn(midc[:, 2:3], midc[:, 1:2], v_pi[:, P - 1:P], ALU.mult).then_inc(forms_decayed, 1)
                dve.wait_ge(pairs_done, j + 1)
                for e in range(2):
                    TTn(Am[:, e, :, :, :].rearrange("p a c t -> p (a c) t"), pbank(2 + e).rearrange("p (a t) -> p a t", t=P),
                        bc(c("lt").unsqueeze(1), [P, 4, P]), ALU.mult).then_inc(pairs_masked, 1)
                n4 = CCOLS["lt4"][0]
                for e in range(2):
                    src = pbank(4 * e)[0:m, 3 * e * P:(3 * e + 1) * P]
                    TTn(As[:, e, :, :].rearrange("p a t -> p (a t)"), src, cst[0:m, n4:n4 + P], ALU.mult).then_inc(pairs_masked, 1)
                dve.wait_ge(sstate_out, 16 * NB * j)
                nle = CCOLS["le"][0]
                for e in range(2):
                    for a in range(2):
                        TTn(Rm[:, e, a, :, :], pbank(5 + e)[:, 2 * a * P:2 * a * P + 2 * P].rearrange("p (c t) -> p c t", t=P),
                            bc(cst[:, nle + a * P:nle + (a + 1) * P].unsqueeze(1), [P, 2, P]), ALU.mult).then_inc(pairs_masked, 1)
                for lev in range(LEVELS):
                    if lev == 0:
                        dve.wait_ge(x_done, j * LEVELS + 1)
                        idb = bc(ident.unsqueeze(1), [P, 4, P])
                        v4 = lambda a: a.rearrange("p e c t -> p (e c) t")
                        TTn(v4(Tn[:, :, :, :]), idb, pbank(0).rearrange("p (a t) -> p a t", t=P), ALU.subtract)
                        TTn(v4(TT[:, :, :, :]), idb, v4(ET[:, 0, :, :, :]), ALU.subtract)
                        ids = bc(ident[0:m, 0:m].unsqueeze(1), [m, 2, m])
                        TTn(Tns[:, :, :], ids, pbank(3)[0:m, 0:64].rearrange("p (e t) -> p e t", e=2), ALU.subtract)
                        TTn(TTs[:, :, :], ids, ETs[:, 0, :, :], ALU.subtract).then_inc(t_done, 1)
                    else:
                        n = j * N_XT + 2 * lev
                        f = lambda a: a.rearrange("p e c t -> p (e c t)")
                        if lev < LEVELS - 1:
                            dve.wait_ge(tx_done, n - 1)
                            even = half_blocks(f(Tn[:, :, :, :]), lev, 0)
                            TTn(even, even, pbank(1)[:, 0:4 * H].rearrange("p (n t) -> p n t", t=1 << lev), ALU.subtract).then_inc(t_done, 1)
                        dve.wait_ge(tx_done, n if lev < LEVELS - 1 else n - 1)
                        if lev == 1:
                            TTn(TTs[:, :, :], TTs[:, :, :], pbank(3)[0:m, 128:192].rearrange("p (e t) -> p e t", e=2), ALU.subtract)
                        odd = half_blocks(f(TT[:, :, :, :]), lev, 1)
                        TTn(odd, odd, pbank(2)[:, 0:4 * H].rearrange("p (n t) -> p n t", t=1 << lev), ALU.subtract).then_inc(t_done, 1)
                    if lev == ADA_ROWS1 + 1:
                        ada_cols(2 * j + ADA_1, 2 * j + (ADA_1 + 1), 7)
                def blocks(dst, src):
                    seq = bc(c("seq", m).unsqueeze(2), [m, NB, HEAD_A])
                    for e in range(2):
                        i = TTn(dst[:, e, :, :], bc(src[:, e * HEAD_A:(e + 1) * HEAD_A].unsqueeze(1), [m, NB, HEAD_A]), seq, ALU.mult)
                    return i
                own(blocks(Vblk, VN[0:m, 2, :]))
                dve.wait_ge(chunk_state, 2 * j + 1)
                TS_(S1[:, :], pbank(4)[:, 0:HEAD_A], midc[:, 2:3], None, ALU.mult).then_inc(mid_state, 1)
                dve.wait_ge(su_in_sbuf, j + 1)
                blocks(Ublk, Uss[:, :]).then_inc(su_blocks, 1)
                dve.wait_ge(sadd_done, j + 1)
                own(TTn(endS[:, :, :], pbank(1).rearrange("p (b v) -> p b v", b=NB), s0T[:, :, :], ALU.add))
                TTn(endS[:, :, :], endS[:, :, :], bc(samp(v_pi[:, TP:T])[:, :, TS - 1:TS], [P, NB, HEAD_A]), ALU.mult).then_inc(send_state, 1)
                dve.wait_ge(chunk_state, 2 * j + 2)
                own(TTn(SE[:, :], pbank(4)[:, HEAD_A:2 * HEAD_A], S1[:, :], ALU.add))
                TS_(SE[:, :], SE[:, :], v_pi[:, TP - 1:TP], None, ALU.mult).then_inc(end_state, 1)
                dve.wait_ge(y_done, j + 1)
                dve.tensor_copy(v_thw[:, :], pbank(3)[:, 0:T]).then_inc(y_copied, 1)
                dve.wait_ge(gn_means, j + 1)
                own(STT(v_ld[:, :], pbank(0)[:, 0:T], -1.0 / HEAD_A, v_thw[:, :], ALU.mult, ALU.add))
                TTn(v_sq[:, :], v_ld[:, :], v_ld[:, :], ALU.mult).then_inc(gn_squares, 1)
                dve.wait_ge(gn_roots, j + 1)
                own(dve.reciprocal(v_px[:, :], v_px[:, :]))
                own(TTn(v_ld[:, :], v_ld[:, :], v_px[:, :], ALU.mult))
                own(TS_(v_ld[:, :], v_ld[:, :], pc("lnx_g", j), pc("lnx_b", j), ALU.mult, ALU.add))
                own(TTn(v_ld[:, :], v_ld[:, :], v_bon[:, :], ALU.add))
                TTn(v_thw[:, :], v_ld[:, :], v_g[:, :], ALU.mult).then_inc(ya_done, 1)
                dve.wait_ge(ya_hi, j + 1)
                jc = bass.ds(j, 1)
                TTn(yalo[:, jc, :].rearrange("p o t -> p (o t)"), v_thw[:, :],
                    yahi[:, jc, :].rearrange("p o t -> p (o t)").bitcast(F32), ALU.subtract).then_inc(ya_lo, 1)
                ada_cols(2 * j + (ADA_1 + 1), 2 * j + (ADA_1 + 2), 7)
            own.leave(KA)

            def qkv_evac(g):
                b4 = 4 * g.parity
                dve.wait_ge(slab_used, g.at(8, stages["qkv"][0] + 8))
                dve.tensor_copy(qkv[:, bass.ds(g.at(4), 4), :], ps[:, b4:b4 + 4, 0:T]).then_inc(qkv_in_sbuf, 1)

            dve.wait_ge(pstate_out, 16 * KA)
            dve.wait_ge(sstate_out, 16 * NB * KA)
            dve.wait_ge(outputs_out, 32)
            plain("qkv", qkv_evac)
            dve.wait_ge(qkv_in_sbuf, 6)

            def fl(ap):
                return ap.rearrange("p o t -> p (o t)")

            def rope(h):
                q_, k_ = fl(qkv[:, one(h), :]), fl(qkv[:, one(h, off=HB), :])
                own.inc(TTn(qr[:, :], q_, c("cos"), ALU.mult))
                own.inc(TTn(kr[:, :], k_, c("cos"), ALU.mult))
                dve.wait_ge(rotated, h + 1)
                own.inc(TTn(rtmp[:, 0, :], pbank(0)[:, 0:T], c("sin"), ALU.mult))
                own(TTn(rtmp[:, 1, :], pbank(1)[:, 0:T], c("sin"), ALU.mult))
                own.inc(TTn(qr[:, :], qr[:, :], rtmp[:, 0, :], ALU.add))
                own(TTn(kr[:, :], kr[:, :], rtmp[:, 1, :], ALU.add))
                dve.tensor_copy(fl(qs[:, one(h), :]), qr[:, TP:T]).then_inc(roped, 1)

            def head_scores(h):
                dve.wait_ge(scores_done, h + 1)
                own.inc(STT(srow[:, 0, :], pbank(4)[:, 0:P], SCALE, c("causal"), ALU.mult, ALU.add))
                own.inc(TS_(srow[:, 1, :], pbank(5)[:, 0:P], SCALE, None, ALU.mult))
                own(STT(srow[:, 2, :], pbank(5)[:, P:2 * P], SCALE, c("causal"), ALU.mult, ALU.add))
                own.inc(dve.tensor_reduce(sm[:, 0, 0:1], srow[:, 0, :], AX.X, ALU.max, negate=True))
                dve.tensor_reduce(sm[:, 0, 1:2], srow[:, 1:3, :], AX.XY, ALU.max, negate=True).then_inc(scores_max, 1)
                STT(STo[:, :, one(h), :].rearrange("p b o t -> p b (o t)"), samp(pbank(7)[0:m, 0:m]), SCALE,
                    samp(c("own", m)), ALU.mult, ALU.add).then_inc(new_scores, 1)

            def head_norm(h):
                dve.wait_ge(probs_done, h + 1)
                own(dve.reciprocal(sm[:, 1, 2:4], sm[:, 1, 0:2]))
                TS_(prob[:, 0, :], prob[:, 0, :], sm[:, 1, 2:3], None, ALU.mult)
                TS_(prob[:, 1:3, :], prob[:, 1:3, :], sm[:, 1, 3:4], None, ALU.mult).then_inc(probs_normed, 1)

            def head_out(h):
                dve.wait_ge(head_done, h + 1)
                dve.tensor_copy(of[:, one(h), 0:TP].rearrange("p o t -> p (o t)"), pbank(6)[:, 0:TP]).then_inc(head_copied, 1)

            def head_first():
                rope(0)
                head_scores(0)
                rope(1)
                head_norm(0)

            def head(h, last=False):
                head_scores(h)
                if not last:
                    rope(h + 1)
                head_out(h - 1)
                head_norm(h)

            def head_last():
                head(HB - 1, True)
                head_out(HB - 1)

            heads(dve, head_first, head, head_last, own, 11)
            dve.wait_ge(new_scores, HB)

            dve.wait_ge(head_copied, HB)
            def queries(b):
                col = slice(TS * b, TS * b + TS) if isinstance(b, int) else bass.ds(b * TS, TS)
                one = slice(b, b + 1) if isinstance(b, int) else bass.ds(b, 1)
                dve.tensor_copy(Snew[:, :, :], STo[:, one, :, :].rearrange("p o h t -> p (o h) t"))
                diag = qz[:, :, :].rearrange("p h x -> p (h x)")[:, 0:HB * (HB * TS + TS)]
                dve.tensor_copy(diag.rearrange("p (h x) -> p h x", x=HB * TS + TS)[:, :, 0:TS], qs[:, :, col]).then_inc(query_laid, 1)

            def select(b):
                row, sg = srow2, smg
                dve.wait_ge(seq_scored, b + 1)
                own.inc(dve.tensor_copy(row[:, PAST:], pbank(3)[0:m, 0:m]))
                own(TS_(row[:, 0:PAST], ps[0:m, 4:6, :].rearrange("p a t -> p (a t)"), SCALE, None, ALU.mult))
                blk = row[:, 0:PAST].rearrange("p (n k) -> p n k", n=NBLK)
                own(dve.tensor_reduce(sg[:, 4:8], blk, AX.X, ALU.add))
                own(dve.tensor_reduce(sg[:, 8:9], sg[:, 4:8], AX.X, ALU.min))
                own(TS_(sg[:, 12:16], sg[:, 4:8], sg[:, 8:9], None, ALU.is_equal))
                own(TS_(sg[:, 20:24], sg[:, 12:16], -1.0, 1.0, ALU.mult, ALU.add))
                own(dve.memset(sg[:, 19:20], 1.0))
                for n in (2, 1, 0):
                    own(TTn(sg[:, 16 + n:17 + n], sg[:, 17 + n:18 + n], sg[:, 21 + n:22 + n], ALU.mult))
                own(STT(sg[:, 24:28], sg[:, 12:16], NEG, sg[:, 16:20], ALU.mult, ALU.mult))
                own(TTn(blk, blk, bc(sg[:, 24:28].unsqueeze(2), [m, NBLK, BLK]), ALU.add))
                dve.tensor_reduce(sg[:, 0:1], row[:, :], AX.X, ALU.max, negate=True).then_inc(seq_selected, 1)

            def normalise(b):
                dve.wait_ge(seq_exp, b + 1)
                own(dve.reciprocal(smg[:, 2:3], smg[:, 1:2]))
                TS_(srow2[:, :], srow2[:, :], smg[:, 2:3], None, ALU.mult).then_inc(seq_normed, 1)
                dve.wait_ge(seq_turned, b + 1)
                own.inc(dve.tensor_copy(PT2[:, 0:NPG, :], pbank(0)[:, 0:NPG * 32].rearrange("p (b t) -> p b t", t=32)))
                dve.tensor_copy(PT2[0:m, NPG, :], pbank(0)[0:m, NPG * 32:NPG * 32 + 32]).then_inc(seq_cols, 1)

            def outs(b):
                dve.wait_ge(seq_done, b + 1)
                dve.tensor_copy(osb[:, CH:], pbank(7)[0:m, :]).then_inc(seq_rows, 1)
                dve.wait_ge(seq_out_turned, b + 1)
                col = slice(TP + TS * b, TP + TS * b + TS) if isinstance(b, int) else bass.ds(b * TS + TP, TS)
                dve.tensor_copy(of[:, :, col], pbank(2)[:, 0:HB * 36].rearrange("p (h x) -> p h x", x=36)[:, :, 0:TS]).then_inc(seq_copied, 1)

            own(dve.memset(qz[:, :, :], 0.0))
            queries(0)
            select(0)
            with dve.Fori(0, NB - 1) as b:
                own.enter(b, 14)
                queries(b + 1)
                normalise(b)
                select(b + 1)
                outs(b)
            own.leave(NB - 1)
            normalise(NB - 1)
            outs(NB - 1)
            dve.wait_ge(ob_hi, 1)
            TTn(olo[:, :, :], of[:, :, :], ohi[:, :, :].bitcast(F32), ALU.subtract).then_inc(merge_read, 1)

            m0 = stages["merge"][0]

            def merge_end(g):
                dve.wait_ge(slab_used, g.at(24, m0 + 24))
                dve.wait_ge(gate_done, g.at(2, 2))
                TTn(sgb[:, :, :], sgb[:, :, :], ps[:, 4:8, 0:T], ALU.mult).then_inc(merge_read, 1)
                dve.wait_ge(merge_read, g.at(2, 3))
                for q in range(4):
                    TTn(sga[:, q, :], sga[:, q, :], sgb[:, q, :], ALU.add).then_inc(merged, 1)
                for q in range(4):
                    dve.wait_ge(merged_hi_done, g.at(4, q + 1))
                    qc = bass.ds(g.at(4, q), 1)
                    TTn(fl(mlo[:, qc, :]), sga[:, q, :], fl(mhi[:, qc, :]).bitcast(F32), ALU.subtract).then_inc(merged_lo_done, 1)

            def merge(g):
                for s in range(24):
                    lo("merge", g, s)
                    if s == 1 and not g.first:
                        merge_end(g.prev())
                    if s == 21:
                        dve.wait_ge(slab_used, g.at(24, m0 + 20))
                        dve.wait_ge(gate_done, g.at(2, 1))
                        TTn(sga[:, :, :], sga[:, :, :], ps[:, 0:4, 0:T], ALU.mult).then_inc(merge_read, 1)

            last_merge = singles(dve, 4, merge)

            def residual(name, gate, done, ends):
                n0, ks, _ = stages[name]

                def evac(g):
                    b4 = 4 * g.parity
                    dve.wait_ge(slab_used, g.at(ks, n0 + ks))
                    for q in range(4):
                        kc = bass.ds(g.at(4, q), 1)
                        x = fl(xT[:, kc, :])
                        STT(x[:, 0:TP], ps[:, b4 + q, 0:TP], mod[:, bass.ds(g.at(4, gate + q), 1), 0], x[:, 0:TP], ALU.mult, ALU.add)
                        i = TTn(samp(rsd[:, q, :]), samp(ps[:, b4 + q, TP:T]),
                                bc(mod[:, bass.ds(g.at(4, gate + q), 1), 1:NC].rearrange("p o b -> p (o b)").unsqueeze(2), [P, NB, TS]), ALU.mult)
                    i.then_inc(gated_samples, 1)
                    dve.wait_ge(gated_samples, g.at(1, 1 + (4 if name == "down" else 0)))
                    k4 = bass.ds(g.at(4), 4)
                    TTn(xT[:, k4, TP:T], xT[:, k4, TP:T], rsd[:, :, :], ALU.add).then_inc(done, 1)
                plain(name, evac, ends)

            residual("out", 32, out_added, {1: lambda: merge_end(last_merge)})
            dve.wait_ge(out_added, 4)
            dve.wait_ge(ada_in_mod, ADA_G)
            norm_h(1, "norm2_g", 48, 64, "up")
            own(dve.memset(ext[:, :, 0:2], 0.0))
            dve.memset(cv[:, :, EPAD - 2:], 0.0).then_inc(zeroed, 1)

            w1, w2 = pcol("conv_w1"), pcol("conv_w2")

            def up_taps(g):
                for h in range(2):
                    dve.wait_ge(tap0_done, g.at(2, h + 1))
                    STT(cv[:, h, 0:EPAD - 2], ext[:, h, 1:EPAD - 1], w1[:, bass.ds(g.at(2, h), 1)], cv[:, h, 0:EPAD - 2], ALU.mult, ALU.add).then_inc(tap1_done, 1)
                for h in range(2):
                    dve.wait_ge(tap1_done, g.at(2, h + 1))
                    STT(cv[:, h, 0:EPAD - 2], ext[:, h, 2:EPAD], w2[:, bass.ds(g.at(2, h), 1)], cv[:, h, 0:EPAD - 2], ALU.mult, ALU.add).then_inc(tap2_done, 1)

            def up_f(g):
                dve.wait_ge(gelu_done, g.at(1, 1))
                b4 = 4 * g.parity
                TTn(ff[:, :, :], gl[:, :, :], ps[:, b4 + 2:b4 + 4, 0:T], ALU.mult).then_inc(ffn_done, 1)

            def up_lo(g):
                dve.wait_ge(ffn_hi, g.at(1, 1))
                TTn(flo[:, bass.ds(g.at(2), 2), :], ff[:, :, :], fhi[:, bass.ds(g.at(2), 2), :].bitcast(F32), ALU.subtract).then_inc(ffn_lo, 1)

            def up_group(g):
                for s in range(4 if g.first else 0, 8):
                    lo("up", g, s)
                    if not g.first and s in (2, 4, 6):
                        (up_taps if s == 2 else up_f if s == 4 else up_lo)(g.prev())

            last = over(dve, 22, up_group)
            residual("down", 80, down_added, {2: lambda: up_taps(last), 4: lambda: up_f(last), 6: lambda: up_lo(last)})
            dve.wait_ge(down_added, 4)
            inverse_roots(2)
            for q in range(4):
                own(over_root(2, q))
                k4 = slice(4 * q, 4 * q + 4)
                TTn(sqs[2][:, k4, :], sqs[2][:, k4, :], bc(pcol("normf_g")[:, k4].unsqueeze(2), [P, 4, T]), ALU.mult).then_inc(h_normed, 1)
            for b in range(12):
                q, mt = b // 3, b % 3
                w = M_ROWS[mt]
                dve.wait_ge(y_turned, b + 1)
                dve.tensor_copy(ynat[0:w, mt, q * CH:(q + 1) * CH], pbank((b + 11) % 8)[0:w, :]).then_inc(y_rows, 1)

        @block.tensor
        def _(pe):
            m = NB * TS

            def mm(out, lhsT, rhs, start=True, stop=True, **k):
                return pe.matmul(out, lhsT, rhs, start=start, stop=stop, **k)

            def carry_wait():
                pe.sem_inc(carried, 1)

            pe.wait_ge(consts_in, 48)
            pe.wait_ge(dve_done, 2)
            for bi, (kind, at_) in enumerate(banks):
                dst = pbank(bi % 8)
                if bi >= 8:
                    pe.wait_ge(bank_read, bi - 8 if bi - 8 > 1 else 1)
                    if bi == 9:
                        pe.wait_ge(silu_done, 1)
                if kind == "par":
                    pe.wait_ge(params_in, 16 * (len(PARAM_ROWS) + 1))
                    for t in range(4):
                        i = pe.transpose(dst[:, t * P:(t + 1) * P], prow[:, t, :], ident)
                elif kind == "c":
                    for k in range(KD):
                        i = pe.transpose(dst[:, k * NC:(k + 1) * NC], cnat[:, k * P:(k + 1) * P], ident[0:NC, 0:NC])
                elif kind == "sh":
                    pe.wait_ge(states_in, 32)
                    for k in range(ZT):
                        i = pe.transpose(dst[:, k * NB:(k + 1) * NB], shnat[:, k * P:(k + 1) * P], ident[0:NB, 0:NB])
                elif kind == "x":
                    mt, q = at_
                    w = M_ROWS[mt]
                    if mt == 0 and q == 0:
                        pe.wait_ge(x_in, 48)
                    for t in range(4):
                        k = 4 * q + t
                        i = pe.transpose(dst[:, t * P:t * P + w], xnat[0:w, mt, k * P:(k + 1) * P], ident[0:w, 0:w])
                else:
                    for t in range(22):
                        k = 22 * at_ + t
                        i = pe.transpose(dst[:, t * 2 * NB:(t + 1) * 2 * NB], cvnat[:, k * P:(k + 1) * P], ident[0:2 * NB, 0:2 * NB])
                i.then_inc(bank_turned, 1)

            pe.wait_ge(bank_read, len(banks) - 1)
            pe.wait_ge(silu_done, 1)

            def ada_half(k, kt, bank):
                i = mm(pbank(bank)[0:NC, :], scT[:, 2 * k + kt, :], raw[:, k % 4, kt, :], k == 0 and kt == 0,
                       k == ADA_K - 1 and kt == 1)
                if kt:
                    i.then_inc(ada_used, 1)

            def ada_turn(n, bank):
                pe.wait_ge(ada_copied, n)
                if not isinstance(n, int):
                    carry_wait()
                for q in range(4):
                    i = pe.transpose(pbank(bank)[:, q * NC:(q + 1) * NC], adr[:, q * P:(q + 1) * P], ident[0:NC, 0:NC])
                i.then_inc(ada_turned, 1)

            def means(u, q):
                pe.wait_ge(squares_done, 4 * u + q + 1)
                for k in range(4 * q, 4 * q + 4):
                    i = mm(pbank(0)[:, 0:T], c("mean"), sqs[u][:, k, :], k == 0, k == KD - 1)
                if q == 3:
                    i.then_inc(means_done, 1)

            for q in range(4):
                means(0, q)
            for g in range(ADA_1):
                if g > 1:
                    pe.wait_ge(ada_in_mod, g - 1)
                for k in range(ADA_K):
                    pe.wait_ge(slab_in[k % 4], 16 * (2 * g + k // 4 + 1))
                    ada_half(k, 0, 1 + g % 2)
                    ada_half(k, 1, 1 + g % 2)
                    if k == 1 and g:
                        ada_turn(g, 3 + (g - 1) % 2)
            ada_turn(ADA_1, 3 + (ADA_1 - 1) % 2)
            pe.wait_ge(ada_in_mod, ADA_1)

            def products(name, g, s0, ks, b4, hi_, lo_, nt=4, between=None, needs={}):
                n0, per, _ = stages[name]
                for s in range(ks):
                    n = n0 + per * g.c + s0 + s
                    pe.wait_ge(slab_lo, g.at(per, n0 + s0 + s + 1))
                    if g.first and s in needs:
                        pe.wait_ge(*needs[s])
                    if g.first and name in ("za", "up") and s % 2 == 0:
                        pe.wait_ge(normed_lo, (4 if name == "up" else 0) + s // 2 + 1)
                    for kt in range(2):
                        k = 2 * s + kt
                        for q in range(nt):
                            w = slice(q * P, (q + 1) * P)
                            out = ps[:, b4 + q, 0:T]
                            mm(out, whi[:, n % 2, kt, w], hi_[:, k, :], k == 0, False)
                            mm(out, whi[:, n % 2, kt, w], lo_[:, k, :], False, False)
                            i = mm(out, wlo[:, n % 2, kt, w], hi_[:, k, :], False, k == 2 * ks - 1)
                    i.then_inc(slab_used, 1)
                    if between:
                        between(s)

            def stage(name, hi_, lo_, done, u=None, needs={}, left=0):
                _, ks, ng = stages[name]

                def group(g):
                    if g.i is not None or g.c > 1:
                        pe.wait_ge(done, g.at(1, -1))
                    last = g.i is None and g.c == ng - 1

                    def between(s):
                        if s in (4, 5, 6):
                            if s == 4:
                                pe.wait_ge(done, ng - 1)
                            means(u, s - 4)

                    products(name, g, 0, ks, 4 * g.parity, hi_, lo_, 3 if name == "za" and last else 4,
                             between if u and last else None, needs)
                over(pe, ng, group)
                pe.wait_ge(done, ng - left)

            stage("za", hhi, hlo, za_in_sbuf)
            pe.wait_ge(last_cols, 1)
            for b in range(7):
                for k in range(4 * b, min(4 * b + 4, ZT)):
                    i = pe.transpose(pbank(b)[0:NC, (k % 4) * P:(k % 4 + 1) * P], nsh[:, k, :], ident)
                i.then_inc(last_turned, 1)
            pe.wait_ge(last_rows, 7)
            pe.wait_ge(lora_acted, 1)

            def ada(j, s, halves=(0, 1)):
                k, n = s % ADA_K, ADA_1 * ADA_K + stages["za"][1] * stages["za"][2] + s
                for kt in halves:
                    if kt == 0:
                        if k == 0:
                            pe.wait_ge(ada_in_mod, 2 * j + (ADA_1 + s // ADA_K))
                        pe.wait_ge(slab_in[k % 4], j * (ADA_J * 4) + 16 * (n // 4 + 1))
                    ada_half(k, kt, 7)

            with pe.Fori(0, KA) as j:
                pe.wait_ge(gn_roots, j)
                pe.wait_ge(pstate_rows, j)
                pe.wait_ge(sstate_rows, 2 * j)
                pe.wait_ge(lora_in, j * 64 + 64)
                mm(pbank(0)[:, 0:T], lora[0:LORA_W, 0, :], lw[0:LORA_W, :])
                mm(pbank(1)[:, 0:T], lora[LORA_W:P, 0, :], lw[LORA_W:P, :])
                mm(pbank(2)[:, 0:T], lora[:, 1, :], lsg[:, 0, :], True, False)
                mm(pbank(2)[:, 0:T], lora[0:LORA_G - P, 2, :], lsg[0:LORA_G - P, 1, :], False, True).then_inc(lora_used, 1)
                ada(j, 0)
                pe.wait_ge(kk_squares, j + 1)
                mm(pbank(3)[:, 0:T], c("head"), v_sq[:, :]).then_inc(kk_sums, 1)
                ada(j, 1)
                pe.wait_ge(logdecay, j + 1)
                pe.transpose(pbank(4)[:, 0:P], v_ld[:, 0:P], ident)
                pe.transpose(pbank(4)[:, P:2 * P], v_ld[:, P:2 * P], ident)
                pe.transpose(pbank(4)[0:m, 2 * P:3 * P], v_ld[:, TP:T], ident).then_inc(logdecay_turned, 1)
                ada(j, 2)
                pe.wait_ge(logdecay_rows, j + 1)
                for b, cum, cum4 in ((5, "cumx", "lt4"), (6, "cumi", "le4")):
                    for ck in range(2):
                        mm(pbank(b)[:, ck * P:(ck + 1) * P], ldn[:, ck, :], c(cum))
                    i = mm(pbank(b)[:, TP:T], ldn[0:m, 2, :], c(cum4, m))
                i.then_inc(cums_done, 1)
                ada(j, 3)
                pe.wait_ge(bonus_in, j + 1)
                pe.wait_ge(kk_norms, j + 1)
                mm(pbank(3)[:, 0:T], c("head"), v_sq[:, :]).then_inc(bonus_sums, 1)
                ada(j, 4)
                pe.wait_ge(forms_decayed, j + 1)
                v_ = rkv[:, 2, :]
                for ck in range(2):
                    pe.transpose(pbank(0)[:, ck * P:(ck + 1) * P], v_[:, ck * P:(ck + 1) * P], ident)
                    pe.transpose(pbank(0)[:, (2 + ck) * P:(3 + ck) * P], v_k[:, ck * P:(ck + 1) * P], ident)
                    pe.transpose(pbank(1)[:, ck * P:(ck + 1) * P], v_b[:, ck * P:(ck + 1) * P], ident)
                for q, a in enumerate((v_, v_k[:, :], v_b[:, :])):
                    i = pe.transpose(pbank(4)[0:m, q * P:(q + 1) * P], a[:, TP:T], ident)
                i.then_inc(rows_turned, 1)
                pe.wait_ge(gate_copied, j + 1)
                pe.wait_ge(bonus_done, j + 1)
                r_ = rkv[:, 0, :]
                carry_wait()
                for e in range(2):
                    f = slice(64 * e, 64 * e + 64)
                    for b, right in ((2 + e, v_kk), (5 + e, r_)):
                        for a, left in enumerate((v_k, v_b)):
                            for ck in range(2):
                                t = slice(ck * P, (ck + 1) * P)
                                mm(pbank(b)[:, (2 * a + ck) * P:(2 * a + ck + 1) * P], left[f, t], right[f, t])
                pe.wait_ge(rows_done, j + 1)
                carry_wait()
                for e in range(2):
                    f = slice(64 * e, 64 * e + 64)
                    dst = pbank(4 * e)[0:m, 3 * e * P:(3 * e + 1) * P]
                    for a, (left, right) in enumerate(((v_k, v_kk), (v_b, v_kk), (v_k, r_), (v_b, r_))):
                        i = mm(dst[:, 32 * a:32 * a + 32], left[f, TP:T], right[f, TP:T])
                i.then_inc(pairs_done, 1)
                ada(j, 5)
                ada(j, 6)
                for lev in range(LEVELS):
                    pe.wait_ge(et_done, j * LEVELS + lev + 1)
                    if lev:
                        pe.wait_ge(t_done, j * N_T + (2 * lev - 2 if lev > 1 else 1))
                    b = lev % 2
                    for e in range(2):
                        for ck in range(2):
                            p = 2 * e + ck
                            i = mm(pbank(0)[:, p * P:(p + 1) * P], ET[:, b, e, ck, :], Tn[:, e, ck, :] if lev else ident)
                        if lev < 2:
                            i = mm(pbank(3)[0:m, 32 * e:32 * e + 32], ETs[:, lev, e, :], Tns[:, e, :] if lev else ident[0:m, 0:m])
                    i.then_inc(x_done, 1)
                    if lev == 0:
                        ada(j, 7)
                        continue
                    if lev == ADA_ROWS1 + 1:
                        ada_turn(2 * j + (ADA_1 + 1), 7)
                    if lev > ADA_ROWS1 + 1:
                        ada(j, ADA_K + lev - ADA_ROWS1 - 2, (0,))
                    pe.wait_ge(x_in_sbuf, j * (LEVELS - 1) + lev)
                    pe.wait_ge(t_done, j * N_T + 2 * lev - 1)
                    quarters = [(e, ck) for e in range(2) for ck in range(2)]
                    if lev < LEVELS - 1:
                        for p, (e, ck) in enumerate(quarters):
                            i = mm(pbank(1)[:, p * H:(p + 1) * H].rearrange("p (n t) -> p n t", t=1 << lev),
                                   TT[:, e, ck, :], half_blocks(Xs[:, e, ck, :], lev, 0))
                        i.then_inc(tx_done, 1)
                    for p, (e, ck) in enumerate(quarters):
                        i = mm(pbank(2)[:, p * H:(p + 1) * H].rearrange("p (n t) -> p n t", t=1 << lev),
                               Xs[:, e, ck, :], half_blocks(TT[:, e, ck, :], lev, 1))
                    if lev == 1:
                        for e in range(2):
                            i = mm(pbank(3)[0:m, 128 + 32 * e:160 + 32 * e], Xss[:, e, :], TTs[:, e, :])
                    i.then_inc(tx_done, 1)
                    if lev > ADA_ROWS1 + 1:
                        ada(j, ADA_K + lev - ADA_ROWS1 - 2, (1,))
                pe.wait_ge(state_in, j * (16 * NB) + 16 * NB)
                pe.wait_ge(t_done, j * N_T + N_T)
                carry_wait()
                for b in range(NB):
                    i = pe.transpose(pbank(2)[:, b * 64:b * 64 + 64], s0n[:, b, :, :].rearrange("p h k -> p (h k)"), ident[0:64, 0:64])
                i.then_inc(state_turned, 1)
                pe.wait_ge(pairs_masked, 8 * j + 8)
                E = [slice(0, 64), slice(64, P)]

                def right_sides(ck):
                    t = slice(ck * P, (ck + 1) * P)
                    for e in range(2):
                        dst = pbank(5)[:, E[e]] if ck == 0 else pbank(5 + e)[:, 0:64]
                        i = mm(dst, Am[:, e, 0, ck, :], VN[:, ck, E[e]], True, ck == 0)
                        if ck:
                            i = mm(dst, v_kk[E[e], t], S1[E[e], :], False, True)
                    i.then_inc(rhs_done, 1)

                def solve(ck):
                    pe.wait_ge(rhs_in_sbuf, 2 * j + ck + 1)
                    carry_wait()
                    for e in range(2):
                        i = mm(pbank(0)[:, E[e]], TT[:, e, ck, :], Ms[:, E[e]])
                    i.then_inc(u_done, 1)

                def results(ck):
                    t = slice(ck * P, (ck + 1) * P)
                    pe.wait_ge(u_in_sbuf, 2 * j + ck + 1)
                    for e in range(2):
                        st = pbank(4)[E[e], ck * 64:ck * 64 + 64]
                        mm(st, KN[:, ck, E[e]], VN[:, ck, E[e]], True, False)
                        i = mm(st, BN[:, ck, E[e]], Us[:, E[e]], False, True)
                    i.then_inc(chunk_state, 1)
                    for e in range(2):
                        y = pbank(3)[E[e], t]
                        mm(y, VN[:, ck, E[e]], Rm[:, e, 0, ck, :], True, False)
                        i = mm(y, Us[:, E[e]], Rm[:, e, 1, ck, :], False, ck == 0)
                        if ck:
                            i = mm(y, S1[E[e], :], r_[E[e], t], False, True)
                    return i

                right_sides(0)
                pe.wait_ge(state_in_sbuf, j + 1)
                carry_wait()
                for e in range(2):
                    mt = pbank(1 + e)[E[e], P:P + m]
                    for b in range(NB):
                        mm(mt[:, 4 * b:4 * b + 4], s0T[E[e], b, :], v_kk[E[e], TP + 4 * b:TP + 4 * b + 4], b == 0, False,
                           skip_group_check=True)
                    i = mm(mt, VN[0:m, 2, E[e]], As[:, e, 0, :], False, True, skip_group_check=True)
                i.then_inc(srhs_done, 1)
                solve(0)
                ada(j, 12, (0,))
                pe.wait_ge(srhs_in_sbuf, j + 1)
                pe.transpose(pbank(1)[0:m, 0:P], MTs[:, :], ident).then_inc(srhs_turned, 1)
                results(0)
                pe.wait_ge(srhs_rows, j + 1)
                carry_wait()
                for e in range(2):
                    i = mm(pbank(2)[0:m, 64 * e:64 * e + 64], TTs[:, e, :], Mss[:, E[e]])
                i.then_inc(su_done, 1)
                pe.wait_ge(mid_state, j + 1)
                right_sides(1)
                pe.wait_ge(su_in_sbuf, j + 1)
                carry_wait()
                for e in range(2):
                    y = pbank(3)[E[e], TP:T]
                    for b in range(NB):
                        mm(y[:, 4 * b:4 * b + 4], s0T[E[e], b, :], r_[E[e], TP + 4 * b:TP + 4 * b + 4], b == 0, False,
                           skip_group_check=True)
                    mm(y, VN[0:m, 2, E[e]], As[:, e, 2, :], False, False, skip_group_check=True)
                    i = mm(y, Uss[:, E[e]], As[:, e, 3, :], False, True, skip_group_check=True)
                solve(1)
                ada(j, 12, (1,))
                pe.wait_ge(su_blocks, j + 1)
                for e in range(2):
                    st = pbank(1)[E[e], :]
                    mm(st, KN[0:m, 2, E[e]], Vblk[:, e, :, :].rearrange("p b v -> p (b v)"), True, False)
                    i = mm(st, BN[0:m, 2, E[e]], Ublk[:, e, :, :].rearrange("p b v -> p (b v)"), False, True)
                i.then_inc(sadd_done, 1)
                results(1).then_inc(y_done, 1)
                ada(j, 13)
                pe.wait_ge(end_state, j + 1)
                carry_wait()
                pe.transpose(pbank(2)[0:64, 0:P], SE[:, :], ident).then_inc(end_turned, 1)
                pe.wait_ge(send_state, j + 1)
                carry_wait()
                for b in range(NB):
                    i = pe.transpose(pbank(5 + b // 4)[0:64, (b % 4) * P:(b % 4 + 1) * P], endS[:, b, :], ident)
                    if b % 4 == 3:
                        i.then_inc(send_turned, 1)
                pe.wait_ge(y_copied, j + 1)
                mm(pbank(0)[:, 0:T], c("head"), v_thw[:, :]).then_inc(gn_means, 1)
                ada(j, 14)
                pe.wait_ge(gn_squares, j + 1)
                mm(pbank(0)[:, 0:T], c("head"), v_sq[:, :]).then_inc(gn_vars, 1)
                ada(j, 15)
                ada_turn(2 * j + (ADA_1 + 2), 7)

            pe.wait_ge(ya_lo, KA)
            pe.wait_ge(sstate_rows, 2 * KA)
            pe.wait_ge(pstate_rows, KA)
            stage("qkv", hhi, hlo, qkv_in_sbuf)

            def rotate(h):
                pe.wait_ge(roped, h)
                mm(pbank(0)[:, 0:T], c("rot"), qkv[:, one(h), :].rearrange("p o t -> p (o t)"))
                mm(pbank(1)[:, 0:T], c("rot"), qkv[:, one(h, off=HB), :].rearrange("p o t -> p (o t)")).then_inc(rotated, 1)

            def head_scores(h):
                pe.wait_ge(roped, h + 1)
                pe.wait_ge(v_copied, h + 1)
                pe.wait_ge(v_rows, h)
                for b, a in ((2, kr), (3, vT)):
                    pe.transpose(pbank(b)[:, 0:P], a[:, 0:P], ident)
                    pe.transpose(pbank(b)[:, P:2 * P], a[:, P:2 * P], ident)
                    i = pe.transpose(pbank(b)[0:m, 2 * P:3 * P], a[:, TP:T], ident)
                i.then_inc(kv_turned, 1)
                pe.wait_ge(new_scores, h)
                mm(pbank(4)[:, 0:P], qr[:, 0:P], kr[:, 0:P])
                mm(pbank(5)[:, 0:TP], qr[:, P:TP], kr[:, 0:TP])
                mm(pbank(7)[0:m, 0:m], kr[:, TP:T], qr[:, TP:T]).then_inc(scores_done, 1)

            def head_out(h):
                pe.wait_ge(probs_normed, h + 1)
                pe.wait_ge(head_copied, h)
                for q in range(3):
                    i = pe.transpose(pbank(6)[:, q * P:(q + 1) * P], prob[:, q, :], ident)
                i.then_inc(probs_turned, 1)
                pe.wait_ge(probs_cols, h + 1)
                pe.wait_ge(v_rows, h + 1)
                mm(pbank(6)[:, 0:P], vnh[:, 0, :], pT[:, 0, :])
                mm(pbank(6)[:, P:TP], vnh[:, 0, :], pT[:, 1, :], True, False)
                mm(pbank(6)[:, P:TP], vnh[:, 1, :], pT[:, 2, :], False, True).then_inc(head_done, 1)

            def head_first():
                rotate(0)
                head_scores(0)
                rotate(1)

            def head(h, last=False):
                head_scores(h)
                if not last:
                    rotate(h + 1)
                head_out(h - 1)

            def head_last():
                head(HB - 1, True)
                head_out(HB - 1)

            heads(pe, head_first, head, head_last)
            pe.wait_ge(head_copied, HB)
            def keys(b, landed_, rest):
                def turn(p):
                    if p % 2 == 0:
                        pe.wait_ge(pages_in[p // 2], landed_)
                    if p == 1:
                        rest()
                    for h in range(HB):
                        i = pe.transpose(pbank(2 * (p % 2) + h // 4)[:, (h % 4) * P:(h % 4 + 1) * P], kpage[:, p, h * P:(h + 1) * P], ident)
                    i.then_inc(keys_turned, 1)

                qf = qz[:, :, :].rearrange("p h x -> p (h x)")
                turn(0)
                for p in range(NPG):
                    if p < NPG - 1:
                        turn(p + 1)
                    pe.wait_ge(keys_in_sbuf, b * NPG + (p + 1))
                    for h in range(HB):
                        i = mm(ps[0:m, 4 + p // 4, (p % 4) * P:(p % 4 + 1) * P], qf[:, h * 32:h * 32 + 32], kT[:, p % 2, h, :], h == 0, h == HB - 1)
                    i.then_inc(page_scored, 1)
                pe.transpose(pbank(3)[0:m, 0:m], Snew[:, :, :].rearrange("p h t -> p (h t)"), ident[0:m, 0:m]).then_inc(seq_scored, 1)

            def values(b, landed_):
                pe.wait_ge(seq_normed, b + 1)
                carry_wait()
                for p in range(NPG):
                    pe.transpose(pbank(0)[:, p * 32:p * 32 + 32], srow2[:, p * P:(p + 1) * P], ident[0:m, 0:m])
                pe.transpose(pbank(0)[0:m, NPG * 32:NPG * 32 + 32], srow2[:, PAST:], ident[0:m, 0:m]).then_inc(seq_turned, 1)
                pe.wait_ge(seq_cols, b + 1)
                for p in range(NPG):
                    if p % 2 == 0:
                        pe.wait_ge(pages_in[p // 2], landed_)
                    for a in range(2):
                        i = mm(ps[0:m, 6 + a, :], PT2[:, p, :], kpage[:, p, a * CH:(a + 1) * CH], p == 0, False)
                    i.then_inc(values_used, 1)
                for a in range(2):
                    i = mm(ps[0:m, 6 + a, :], PT2[0:m, NPG, :], vns[:, 4 * a:4 * a + 4, :].rearrange("p h f -> p (h f)"), False, True)
                i.then_inc(seq_done, 1)
                pe.wait_ge(seq_rows, b * 2 + 2)
                carry_wait()
                for h in range(HB):
                    i = pe.transpose(pbank(2)[:, h * 32:h * 32 + 32], osb[:, h * P:(h + 1) * P], ident[0:m, 0:m])
                i.then_inc(seq_out_turned, 1)

            keys(0, 32, lambda: pe.wait_ge(query_laid, 1))
            with pe.Fori(0, NB - 1) as b:
                def rest():
                    pe.wait_ge(seq_copied, b)
                    pe.wait_ge(seq_selected, b + 1)
                    pe.wait_ge(query_laid, b + 2)
                keys(b + 1, b * 64 + 64, rest)
                values(b, b * 64 + 96)
            values(NB - 1, 32 * 2 * NB)

            pe.wait_ge(seq_copied, 8)
            pe.wait_ge(merge_read, 1)
            with pe.Fori(0, 4) as i:
                g = G(1, i, 0)
                pe.wait_ge(merge_read, g.at(2))
                products("merge", g, 0, 8, 0, hhi, hlo)
                pe.wait_ge(merge_read, g.at(2, 1))
                products("merge", g, 8, 8, 4, hhi, hlo)
                pe.wait_ge(gate_done, g.at(2, 1))
                products("merge", g, 16, 4, 0, yahi, yalo)
                pe.wait_ge(gate_done, g.at(2, 2))
                products("merge", g, 20, 4, 4, ohi, olo)
            pe.wait_ge(merge_read, 8)
            pe.wait_ge(merged_lo_done, 12)
            stage("out", mhi, mlo, out_added, 1, {6: (merged_lo_done, 16)})
            means(1, 3)
            stage("up", hhi, hlo, ffn_done, left=1)
            pe.wait_ge(ffn_lo, 21)
            stage("down", fhi, flo, down_added, 2, {21: (ffn_lo, 22)})
            means(2, 3)
            pe.wait_ge(newconv_done, 22)
            pe.wait_ge(rms_done, 3)
            for b in range(11):
                if b >= 8:
                    pe.wait_ge(newconv_rows, b - 7)
                for q in range(4):
                    i = pe.transpose(pbank(b % 8)[0:2 + 2 * NB, q * P:(q + 1) * P], newconv[:, 4 * b + q, :], ident)
                i.then_inc(newconv_turned, 1)
            for b in range(12):
                q, mt = b // 3, b % 3
                w = M_ROWS[mt]
                pe.wait_ge(h_normed, 8 + q + 1)
                pe.wait_ge(newconv_rows, min(b + 4, 11))
                if b + 4 > 11:
                    pe.wait_ge(y_rows, b - 7)
                for t in range(4):
                    i = pe.transpose(pbank((b + 11) % 8)[0:w, t * P:(t + 1) * P], sqs[2][:, 4 * q + t, mt * P:mt * P + w], ident)
                i.then_inc(y_turned, 1)


_INS = ['x_prompt', 'x_sample', 'cache_k', 'cache_v', 'state_wkv', 'state_shift', 'state_conv', 'page_table',
        'c_prompt', 'c_sample', 'w_ada', 'b_ada', 'norm1_g', 'w_in', 'mu_shift', 'rwkv_w0', 'rwkv_w2', 'rwkv_a0',
        'rwkv_a2', 'rwkv_g2', 'rwkv_kk', 'rwkv_ka', 'rwkv_rk', 'lnx_g', 'lnx_b', 'w_proj_a', 'w_proj_b', 'w_out',
        'norm2_g', 'w_up', 'conv_w', 'conv_b', 'w_down', 'normf_g']
_OUTS = [("y_prompt", (1, TP, D)), ("y_sample", (NB, TS, D)), ("k_prompt", (1, TP, HB, HEAD_B)),
         ("v_prompt", (1, TP, HB, HEAD_B)), ("wkv_prompt", (1, HA, HEAD_A, HEAD_A)), ("shift_prompt", (1, ZA)),
         ("conv_prompt", (1, 2, FF)), ("k_sample", (NB, TS, HB, HEAD_B)), ("v_sample", (NB, TS, HB, HEAD_B)),
         ("wkv_sample", (NB, HA, HEAD_A, HEAD_A)), ("shift_sample", (NB, ZA)), ("conv_sample", (NB, 2, FF))]


def kernel(**inputs):
    import concourse.bacc as _bacc
    from concourse.bass_utils import run_bass_kernel_spmd as _run

    nc = _bacc.Bacc("TRN2", target_bir_lowering=False, num_devices=1)
    arrays, d = {}, {}
    for name in _INS:
        a = np.ascontiguousarray(inputs[name])
        arrays[f"in_{name}"] = a
        d[name] = nc.dram_tensor(f"in_{name}", a.shape, mybir.dt.from_np(a.dtype), kind="ExternalInput").ap()
    consts, _cols = shape_constants()
    arrays["in_consts"] = consts
    d["consts"] = nc.dram_tensor("in_consts", consts.shape, F32, kind="ExternalInput").ap()
    for name, shape in _OUTS:
        d[name] = nc.dram_tensor(f"out_{name}", shape, F32, kind="ExternalOutput").ap()
    build(nc, d)
    r = _run(nc, [arrays], core_ids=[0])
    return tuple(r.results[0][f"out_{name}"] for name, _shape in _OUTS)
```
